# Optimizing a Trainium2 kernel written in Bass

```python
import jax, jax.numpy as jnp
from jax import lax
import numpy as np

D_MODEL = 1024
BATCH = 1
SEQ = 512
DEPTH = 1

HEAD_DIM = 64
RET_HEADS = 8
DSA_HEADS = 8
RET_WIDTH = RET_HEADS * HEAD_DIM
DSA_WIDTH = DSA_HEADS * HEAD_DIM
MIX_WIDTH = RET_WIDTH + DSA_WIDTH
IDX_HEADS = 8
IDX_DIM = 64
TOPK_MAX = 256
RET_CHUNK = 128
Q_BLOCK = 128
D_FF = 2816
CONV_WIDTH = 3
ROPE_THETA = 10000.0
EPS = 1e-6
IN_SIZES = (RET_WIDTH, RET_WIDTH, RET_WIDTH, RET_WIDTH,
            DSA_WIDTH, HEAD_DIM, HEAD_DIM,
            IDX_HEADS * IDX_DIM, IDX_DIM, IDX_HEADS)
IN_WIDTH = 4 * RET_WIDTH + DSA_WIDTH + 2 * HEAD_DIM + IDX_HEADS * IDX_DIM + IDX_DIM + IDX_HEADS


def rms_norm(x, g):
    xf = x.astype(jnp.float32)
    y = xf * lax.rsqrt(jnp.mean(xf * xf, axis=-1, keepdims=True) + EPS)
    return (y * g.astype(jnp.float32)).astype(x.dtype)

def rope_tables(seq_len, dim):
    inv = ROPE_THETA ** (-jnp.arange(0, dim, 2, dtype=jnp.float32) / dim)
    ang = jnp.arange(seq_len, dtype=jnp.float32)[:, None] * inv[None, :]
    return jnp.cos(ang), jnp.sin(ang)

def apply_rope(x, cos, sin):
    shape = (cos.shape[0],) + (1,) * (x.ndim - 3) + (cos.shape[1],)
    c = cos.reshape(shape)
    s = sin.reshape(shape)
    xf = x.astype(jnp.float32)
    x1, x2 = jnp.split(xf, 2, axis=-1)
    return jnp.concatenate([x1 * c - x2 * s, x2 * c + x1 * s], axis=-1).astype(x.dtype)

def split_columns(p):
    pts, acc = [], 0
    for n in IN_SIZES[:-1]:
        acc += n
        pts.append(acc)
    return jnp.split(p, pts, axis=-1)

def retention(q, k, v, gate):
    B, S, H, d = q.shape
    C = RET_CHUNK
    N = S // C
    f32 = jnp.float32
    log_g = jnp.log(1.0 - 2.0 ** (-5.0 - jnp.arange(H, dtype=f32)))
    qf = q.astype(f32).reshape(B, N, C, H, d)
    kf = (k.astype(f32) * d ** -0.5).reshape(B, N, C, H, d)
    vf = v.astype(f32).reshape(B, N, C, H, d)
    pos = jnp.arange(C, dtype=f32)
    diff = pos[:, None] - pos[None, :]
    decay_in = jnp.where(diff >= 0, jnp.exp(log_g[:, None, None] * jnp.maximum(diff, 0.0)), 0.0)
    scores = jnp.einsum('bnchd,bnmhd->bnhcm', qf, kf) * decay_in[None, None]
    inner = jnp.einsum('bnhcm,bnmhd->bnchd', scores, vf)
    zeta = jnp.exp(log_g[:, None] * (C - 1.0 - pos)[None, :])
    chunk_state = jnp.einsum('bnmhk,hm,bnmhv->bnhkv', kf, zeta, vf)
    chunk_decay = jnp.exp(log_g * C)[None, :, None, None]

    def step(R, s):
        return chunk_decay * R + s, R

    _, prev = lax.scan(step, jnp.zeros((B, H, d, d), f32), jnp.moveaxis(chunk_state, 1, 0))
    prev = jnp.moveaxis(prev, 0, 1)
    xi = jnp.exp(log_g[:, None] * (pos + 1.0)[None, :])
    cross = jnp.einsum('bnchk,bnhkv,hc->bnchv', qf, prev, xi)
    o = (inner + cross).reshape(B, S, H, d)
    o = o * lax.rsqrt(jnp.mean(o * o, axis=-1, keepdims=True) + EPS)
    o = o * jax.nn.silu(gate.astype(f32).reshape(B, S, H, d))
    return o.reshape(B, S, H * d).astype(q.dtype)

def dsa_attention(q, k, v, qi, ki, wi):
    B, S, H, d = q.shape
    k_sel = min(TOPK_MAX, S // 4)
    NB = S // Q_BLOCK
    wi = wi * (IDX_HEADS ** -0.5 * IDX_DIM ** -0.5)

    def to_blocks(a):
        return jnp.moveaxis(a.reshape((B, NB, Q_BLOCK) + a.shape[2:]), 1, 0)

    key_pos = jnp.arange(S, dtype=jnp.int32)

    def block_fn(args):
        qb, qib, wib, blk = args
        t = blk * Q_BLOCK + jnp.arange(Q_BLOCK, dtype=jnp.int32)
        rel = jax.nn.relu(jnp.einsum('bthe,bse->bths', qib, ki))
        iscore = jnp.einsum('bths,bth->bts', rel, wib).astype(jnp.float32)
        causal = key_pos[None, :] <= t[:, None]
        iscore = jnp.where(causal[None], iscore, -jnp.inf)
        _, sel = lax.top_k(iscore, k_sel)
        valid = sel <= t[None, :, None]
        k_g = jax.vmap(lambda kb, ib: kb[ib])(k, sel)
        v_g = jax.vmap(lambda vb, ib: vb[ib])(v, sel)
        logits = jnp.einsum('bthd,btkd->bhtk', qb, k_g).astype(jnp.float32) * d ** -0.5
        logits = jnp.where(valid[:, None], logits, -1e30)
        p = jax.nn.softmax(logits, axis=-1).astype(v.dtype)
        return jnp.einsum('bhtk,btkd->bthd', p, v_g)

    out = lax.map(block_fn, (to_blocks(q), to_blocks(qi), to_blocks(wi),
                             jnp.arange(NB, dtype=jnp.int32)))
    return jnp.moveaxis(out, 0, 1).reshape(B, S, H * d)

def causal_dwconv(h, w, b):
    S = h.shape[1]
    hp = jnp.pad(h, ((0, 0), (CONV_WIDTH - 1, 0), (0, 0)))
    y = b
    for j in range(CONV_WIDTH):
        y = y + hp[:, j:j + S] * w[j]
    return y

def first_inputs(seed: int = 0) -> dict:
    key = jax.random.key(seed)
    ks = jax.random.split(key, 11)
    f32 = jnp.float32
    nrm = lambda k, shape, scale: jax.random.normal(k, shape, f32) * scale
    gain = lambda k: 1.0 + 0.02 * jax.random.normal(k, (DEPTH, D_MODEL), f32)
    return {
        "x": jax.random.normal(ks[0], (BATCH, SEQ, D_MODEL), f32),
        "mix_norm_pre": gain(ks[1]),
        "mix_norm_post": gain(ks[2]),
        "w_in": nrm(ks[3], (DEPTH, D_MODEL, IN_WIDTH), D_MODEL ** -0.5),
        "w_out": nrm(ks[4], (DEPTH, MIX_WIDTH, D_MODEL), MIX_WIDTH ** -0.5),
        "ffn_norm_pre": gain(ks[5]),
        "ffn_norm_post": gain(ks[6]),
        "w_up": nrm(ks[7], (DEPTH, D_MODEL, 2 * D_FF), D_MODEL ** -0.5),
        "conv_w": nrm(ks[8], (DEPTH, CONV_WIDTH, 2 * D_FF), CONV_WIDTH ** -0.5),
        "conv_b": nrm(ks[9], (DEPTH, 2 * D_FF), 0.01),
        "w_down": nrm(ks[10], (DEPTH, D_FF, D_MODEL), D_FF ** -0.5),
    }

def first_block(x, mix_norm_pre, mix_norm_post, w_in, w_out, ffn_norm_pre, ffn_norm_post,
              w_up, conv_w, conv_b, w_down):
    B, S, _ = x.shape
    cos_h, sin_h = rope_tables(S, HEAD_DIM)
    cos_i, sin_i = rope_tables(S, IDX_DIM)
    h = x
    for l in range(DEPTH):
        hn = rms_norm(h, mix_norm_pre[l])
        proj = hn @ w_in[l]
        rq, rk, rv, rg, aq, ak, av, iq, ik, iw = split_columns(proj)
        rq = apply_rope(rq.reshape(B, S, RET_HEADS, HEAD_DIM), cos_h, sin_h)
        rk = apply_rope(rk.reshape(B, S, RET_HEADS, HEAD_DIM), cos_h, sin_h)
        rv = rv.reshape(B, S, RET_HEADS, HEAD_DIM)
        ret_out = retention(rq, rk, rv, rg)
        aq = apply_rope(aq.reshape(B, S, DSA_HEADS, HEAD_DIM), cos_h, sin_h)
        ak = apply_rope(ak, cos_h, sin_h)
        iq = apply_rope(iq.reshape(B, S, IDX_HEADS, IDX_DIM), cos_i, sin_i)
        ik = apply_rope(ik, cos_i, sin_i)
        att_out = dsa_attention(aq, ak, av, iq, ik, iw)
        mixed = jnp.concatenate([ret_out, att_out], axis=-1) @ w_out[l]
        h = h + rms_norm(mixed, mix_norm_post[l])
        hn = rms_norm(h, ffn_norm_pre[l])
        up = causal_dwconv(hn @ w_up[l], conv_w[l], conv_b[l])
        g, u = jnp.split(up, 2, axis=-1)
        ffn = (jax.nn.silu(g) * u) @ w_down[l]
        h = h + rms_norm(ffn, ffn_norm_post[l])
    return h


DEPTH_2 = 2

N_A_LAYERS = DEPTH_2 // 2
N_B_LAYERS = DEPTH_2 - N_A_LAYERS
HGRN_EXPAND = 128
HGRN_HEADS = D_MODEL // HGRN_EXPAND
HGRN_DK = HGRN_EXPAND
HGRN_DV = D_MODEL // HGRN_HEADS
HGRN_D_KEY = HGRN_HEADS * HGRN_DK
HGRN_D_VAL = HGRN_HEADS * HGRN_DV
HGRN_CHUNK = 64
NSA_HEADS = 16
NSA_KV_HEADS = 4
NSA_GROUP = NSA_HEADS // NSA_KV_HEADS
NSA_HEAD_DIM = D_MODEL // NSA_HEADS
NSA_Q_WIDTH = NSA_HEADS * NSA_HEAD_DIM
N_BRANCH = 3
CMP_BLOCK = 32
CMP_STRIDE = 16
CMP_HIDDEN = 256
SEL_BLOCK = 64
N_SELECT = 16
WINDOW = 512
FFN_HIDDEN = -(-8 * D_MODEL // (3 * 256)) * 256
NEG_INF = -1e30
FORCE_SCORE = 1e9


def rms_norm_2(x, gain):
    x32 = x.astype(jnp.float32)
    y = x32 * lax.rsqrt(jnp.mean(x32 * x32, axis=-1, keepdims=True) + EPS)
    return (y * gain.astype(jnp.float32)).astype(x.dtype)

def modulate(x, gain, shift, scale):
    return rms_norm_2(x, gain) * (1 + scale[:, None, :]) + shift[:, None, :]

def rope_tables_2(seq, dim):
    inv_freq = 1.0 / (ROPE_THETA ** (jnp.arange(0, dim, 2, dtype=jnp.float32) / dim))
    ang = jnp.arange(seq, dtype=jnp.float32)[:, None] * inv_freq[None, :]
    return jnp.cos(ang), jnp.sin(ang)

def apply_rope_2(x, cos, sin):
    x1, x2 = jnp.split(x, 2, axis=-1)
    cs = cos[None, :, None, :].astype(x.dtype)
    sn = sin[None, :, None, :].astype(x.dtype)
    return jnp.concatenate([x1 * cs - x2 * sn, x2 * cs + x1 * sn], axis=-1)

def masked_softmax(s, mask):
    p = jax.nn.softmax(jnp.where(mask, s.astype(jnp.float32), NEG_INF), axis=-1)
    return jnp.where(mask, p, 0.0)

def swiglu(h, w_in, w_out):
    a, b = jnp.split(h @ w_in, 2, axis=-1)
    return (jax.nn.silu(a) * b) @ w_out

def hgrn2_mixer(h, w_in, lower_bound, out_norm, w_out, first_layer):
    B, S, _ = h.shape
    q, f, i, g = jnp.split(h @ w_in, [HGRN_D_KEY, 2 * HGRN_D_KEY, 2 * HGRN_D_KEY + HGRN_D_VAL], axis=-1)
    q = jax.nn.silu(q)
    f32 = f.astype(jnp.float32)
    if first_layer:
        log_f = jax.nn.log_sigmoid(f32)
    else:
        lb = lower_bound.astype(jnp.float32)
        log_f = jnp.log(lb + (1.0 - lb) * jax.nn.sigmoid(f32))
    k = -jnp.expm1(log_f)
    nc = S // HGRN_CHUNK

    def to_chunks(t, d):
        return t.astype(jnp.float32).reshape(B, nc, HGRN_CHUNK, HGRN_HEADS, d).transpose(1, 0, 3, 2, 4)

    qc, kc, gc = to_chunks(q, HGRN_DK), to_chunks(k, HGRN_DK), to_chunks(log_f, HGRN_DK)
    vc = to_chunks(i, HGRN_DV)
    causal = jnp.tril(jnp.ones((HGRN_CHUNK, HGRN_CHUNK), dtype=bool))[:, :, None]

    def step(state, inp):
        q_, k_, v_, g_ = inp
        G = jnp.cumsum(g_, axis=2)
        o_inter = jnp.einsum('bhtk,bhkv->bhtv', q_ * jnp.exp(G), state)
        diff = G[:, :, :, None, :] - G[:, :, None, :, :]
        decay = jnp.where(causal, jnp.exp(jnp.where(causal, diff, 0.0)), 0.0)
        attn = jnp.einsum('bhtk,bhsk,bhtsk->bhts', q_, k_, decay)
        o_intra = jnp.einsum('bhts,bhsv->bhtv', attn, v_)
        G_last = G[:, :, -1:, :]
        new_state = jnp.exp(G_last[:, :, 0, :])[..., None] * state + jnp.einsum(
            'bhsk,bhsv->bhkv', k_ * jnp.exp(G_last - G), v_)
        return new_state, o_inter + o_intra

    s0 = jnp.zeros((B, HGRN_HEADS, HGRN_DK, HGRN_DV), jnp.float32)
    _, o = lax.scan(step, s0, (qc, kc, vc, gc))
    o = o.transpose(1, 0, 3, 2, 4).reshape(B, S, HGRN_HEADS, HGRN_DV)
    o = rms_norm_2(o, out_norm) * jax.nn.silu(g.reshape(B, S, HGRN_HEADS, HGRN_DV).astype(jnp.float32))
    return o.reshape(B, S, HGRN_D_VAL).astype(h.dtype) @ w_out

def nsa_shared_kv(h, w_kv, k_norm, cmp_pos, cmp_w1, cmp_w2, cos, sin):
    B, S, _ = h.shape
    kv = (h @ w_kv).reshape(B, S, 2 * N_BRANCH, NSA_KV_HEADS, NSA_HEAD_DIM)
    k_cmp, v_cmp, k_sel, v_sel, k_win, v_win = [kv[:, :, j] for j in range(2 * N_BRANCH)]
    n_sub = CMP_BLOCK // CMP_STRIDE
    n_cmp = S // CMP_STRIDE - n_sub + 1

    def compress(t, pos, w1, w2):
        r = t.reshape(B, S // CMP_STRIDE, CMP_STRIDE, NSA_KV_HEADS, NSA_HEAD_DIM)
        blocks = jnp.concatenate([r[:, j:j + n_cmp] for j in range(n_sub)], axis=2)
        blocks = blocks + pos[None, None, :, None, :]
        flat = blocks.transpose(0, 1, 3, 2, 4).reshape(B, n_cmp, NSA_KV_HEADS, CMP_BLOCK * NSA_HEAD_DIM)
        return jax.nn.silu(flat @ w1) @ w2

    kc = rms_norm_2(compress(k_cmp, cmp_pos[0], cmp_w1[0], cmp_w2[0]), k_norm[0])
    vc = compress(v_cmp, cmp_pos[1], cmp_w1[1], cmp_w2[1])
    n_sel = S // SEL_BLOCK
    ks = apply_rope_2(rms_norm_2(k_sel, k_norm[1]), cos, sin)
    ks_blocks = ks.reshape(B, n_sel, SEL_BLOCK, NSA_KV_HEADS, NSA_HEAD_DIM).transpose(0, 3, 1, 2, 4)
    vs_blocks = v_sel.reshape(B, n_sel, SEL_BLOCK, NSA_KV_HEADS, NSA_HEAD_DIM).transpose(0, 3, 1, 2, 4)
    kw = apply_rope_2(rms_norm_2(k_win, k_norm[2]), cos, sin)
    pad = ((0, 0), (WINDOW, 0), (0, 0), (0, 0))
    return (kc, vc, ks_blocks, vs_blocks, jnp.pad(kw, pad), jnp.pad(v_win, pad))

def nsa_mixer(h, w_q, q_norm, w_out, shared, cos, sin):
    B, S, _ = h.shape
    kc, vc, ks_blocks, vs_blocks, kw_pad, vw_pad = shared
    proj = h @ w_q
    q = rms_norm_2(proj[..., :NSA_Q_WIDTH].reshape(B, S, NSA_HEADS, NSA_HEAD_DIM), q_norm)
    gates = jax.nn.sigmoid(proj[..., NSA_Q_WIDTH:].astype(jnp.float32)).reshape(B, S, N_BRANCH, NSA_HEADS)
    q_rope = apply_rope_2(q, cos, sin)
    n_cmp = kc.shape[1]
    n_sel = ks_blocks.shape[2]
    n_top = min(N_SELECT, n_sel)
    cmp_end = jnp.arange(n_cmp) * CMP_STRIDE + CMP_BLOCK - 1
    sel_start = jnp.arange(n_sel) * SEL_BLOCK
    cs = np.arange(n_cmp) * CMP_STRIDE
    ss = np.arange(n_sel) * SEL_BLOCK
    overlap = jnp.asarray(((cs[:, None] < ss[None, :] + SEL_BLOCK) &
                           (cs[:, None] + CMP_BLOCK > ss[None, :])).astype(np.float32))
    scale = NSA_HEAD_DIM ** -0.5
    nb = S // Q_BLOCK
    bi = jnp.arange(B)[:, None, None, None]
    hi = jnp.arange(NSA_KV_HEADS)[None, :, None, None]
    blk_pos = jnp.arange(SEL_BLOCK)

    def blockify(t):
        return t.reshape(B, nb, Q_BLOCK, *t.shape[2:]).swapaxes(0, 1)

    def attend(args):
        blk, qp, qr, g = args
        t = blk * Q_BLOCK + jnp.arange(Q_BLOCK)
        qp = qp.reshape(B, Q_BLOCK, NSA_KV_HEADS, NSA_GROUP, NSA_HEAD_DIM)
        qr = qr.reshape(B, Q_BLOCK, NSA_KV_HEADS, NSA_GROUP, NSA_HEAD_DIM)
        s_c = jnp.einsum('bqhgd,bchd->bhgqc', qp, kc) * scale
        p_c = masked_softmax(s_c, cmp_end[None, :] <= t[:, None])
        o_c = jnp.einsum('bhgqc,bchd->bqhgd', p_c.astype(vc.dtype), vc)
        imp = jnp.einsum('bhgqc,cj->bhqj', p_c, overlap)
        cur = t // SEL_BLOCK
        j = jnp.arange(n_sel)[None, :]
        forced = (j == 0) | (j == cur[:, None]) | (j == cur[:, None] - 1)
        valid_blk = sel_start[None, :] <= t[:, None]
        imp = jnp.where(forced & valid_blk, FORCE_SCORE, jnp.where(valid_blk, imp, -1.0))
        top_val, top_idx = lax.top_k(imp, n_top)
        ks_g = ks_blocks[bi, hi, top_idx].reshape(B, NSA_KV_HEADS, Q_BLOCK, n_top * SEL_BLOCK, NSA_HEAD_DIM)
        vs_g = vs_blocks[bi, hi, top_idx].reshape(B, NSA_KV_HEADS, Q_BLOCK, n_top * SEL_BLOCK, NSA_HEAD_DIM)
        kpos = (top_idx[..., None] * SEL_BLOCK + blk_pos).reshape(B, NSA_KV_HEADS, Q_BLOCK, n_top * SEL_BLOCK)
        m_s = jnp.repeat(top_val >= 0, SEL_BLOCK, axis=-1) & (kpos <= t[None, None, :, None])
        s_s = jnp.einsum('bqhgd,bhqkd->bhgqk', qr, ks_g) * scale
        p_s = masked_softmax(s_s, m_s[:, :, None])
        o_s = jnp.einsum('bhgqk,bhqkd->bqhgd', p_s.astype(vs_g.dtype), vs_g)
        kw = lax.dynamic_slice_in_dim(kw_pad, blk * Q_BLOCK, Q_BLOCK + WINDOW, axis=1)
        vw = lax.dynamic_slice_in_dim(vw_pad, blk * Q_BLOCK, Q_BLOCK + WINDOW, axis=1)
        kpos_w = blk * Q_BLOCK - WINDOW + jnp.arange(Q_BLOCK + WINDOW)
        m_w = ((kpos_w[None, :] <= t[:, None]) & (kpos_w[None, :] > t[:, None] - WINDOW)
               & (kpos_w[None, :] >= 0))
        s_w = jnp.einsum('bqhgd,bkhd->bhgqk', qr, kw) * scale
        p_w = masked_softmax(s_w, m_w)
        o_w = jnp.einsum('bhgqk,bkhd->bqhgd', p_w.astype(vw.dtype), vw)
        g = g.reshape(B, Q_BLOCK, N_BRANCH, NSA_KV_HEADS, NSA_GROUP)[..., None]
        o = g[:, :, 0] * o_c + g[:, :, 1] * o_s + g[:, :, 2] * o_w
        return o.reshape(B, Q_BLOCK, NSA_Q_WIDTH).astype(h.dtype)

    out = lax.map(attend, (jnp.arange(nb), blockify(q), blockify(q_rope), blockify(gates)))
    return out.swapaxes(0, 1).reshape(B, S, NSA_Q_WIDTH) @ w_out

def second_inputs(seed: int = 0) -> dict:
    key = jax.random.key(seed)
    ks = jax.random.split(key, 24)
    D = D_MODEL

    def nrm(k, shape, scale):
        return jax.random.normal(k, shape, jnp.float32) * scale

    def gain(k, shape):
        return 1.0 + nrm(k, shape, 0.02)

    return {
        'x': nrm(ks[0], (BATCH, SEQ, D), 1.0),
        'c': nrm(ks[1], (BATCH, D), 1.0),
        'ada_w': nrm(ks[2], (2 * DEPTH_2, D, 3 * D), 0.5 * D ** -0.5),
        'ada_b': nrm(ks[3], (2 * DEPTH_2, 3 * D), 0.02),
        'norm_mix': gain(ks[4], (DEPTH_2, D)),
        'norm_ffn': gain(ks[5], (DEPTH_2, D)),
        'hgrn_w_in': nrm(ks[6], (N_A_LAYERS, D, 2 * HGRN_D_KEY + 2 * HGRN_D_VAL), D ** -0.5),
        'hgrn_lower_bounds': nrm(ks[7], (N_A_LAYERS, HGRN_D_KEY), 0.5),
        'hgrn_out_norm': gain(ks[8], (N_A_LAYERS, HGRN_DV)),
        'hgrn_w_out': nrm(ks[9], (N_A_LAYERS, HGRN_D_VAL, D), HGRN_D_VAL ** -0.5),
        'kv_ada_w': nrm(ks[10], (D, 2 * D), 0.5 * D ** -0.5),
        'kv_ada_b': nrm(ks[11], (2 * D,), 0.02),
        'kv_norm': gain(ks[12], (D,)),
        'nsa_w_kv': nrm(ks[13], (D, 2 * N_BRANCH * NSA_KV_HEADS * NSA_HEAD_DIM), D ** -0.5),
        'nsa_k_norm': gain(ks[14], (N_BRANCH, NSA_HEAD_DIM)),
        'cmp_pos': nrm(ks[15], (2, CMP_BLOCK, NSA_HEAD_DIM), 0.1),
        'cmp_w1': nrm(ks[16], (2, CMP_BLOCK * NSA_HEAD_DIM, CMP_HIDDEN), (CMP_BLOCK * NSA_HEAD_DIM) ** -0.5),
        'cmp_w2': nrm(ks[17], (2, CMP_HIDDEN, NSA_HEAD_DIM), CMP_HIDDEN ** -0.5),
        'nsa_w_q': nrm(ks[18], (N_B_LAYERS, D, NSA_Q_WIDTH + N_BRANCH * NSA_HEADS), D ** -0.5),
        'nsa_q_norm': gain(ks[19], (N_B_LAYERS, NSA_HEAD_DIM)),
        'nsa_w_out': nrm(ks[20], (N_B_LAYERS, NSA_Q_WIDTH, D), NSA_Q_WIDTH ** -0.5),
        'ffn_w_in': nrm(ks[21], (DEPTH_2, D, 2 * FFN_HIDDEN), D ** -0.5),
        'ffn_w_out': nrm(ks[22], (DEPTH_2, FFN_HIDDEN, D), FFN_HIDDEN ** -0.5),
    }

def second_block(x, c, ada_w, ada_b, norm_mix, norm_ffn, hgrn_w_in, hgrn_lower_bounds, hgrn_out_norm,
              hgrn_w_out, kv_ada_w, kv_ada_b, kv_norm, nsa_w_kv, nsa_k_norm, cmp_pos, cmp_w1, cmp_w2,
              nsa_w_q, nsa_q_norm, nsa_w_out, ffn_w_in, ffn_w_out):
    B, S, _ = x.shape
    cos, sin = rope_tables_2(S, NSA_HEAD_DIM)
    c_act = jax.nn.silu(c)
    mods = jnp.einsum('bd,lde->lbe', c_act, ada_w) + ada_b[:, None, :]
    lb = jax.nn.softmax(hgrn_lower_bounds.astype(jnp.float32), axis=0)
    lb = jnp.cumsum(lb, axis=0) - lb[0]
    shared = None
    for layer in range(DEPTH_2):
        shift, scale, gate = jnp.split(mods[2 * layer], 3, axis=-1)
        h = modulate(x, norm_mix[layer], shift, scale)
        if layer < N_A_LAYERS:
            y = hgrn2_mixer(h, hgrn_w_in[layer], lb[layer], hgrn_out_norm[layer], hgrn_w_out[layer], layer == 0)
        else:
            if layer == N_A_LAYERS:
                kv_shift, kv_scale = jnp.split(c_act @ kv_ada_w + kv_ada_b, 2, axis=-1)
                shared = nsa_shared_kv(modulate(x, kv_norm, kv_shift, kv_scale), nsa_w_kv, nsa_k_norm,
                                       cmp_pos, cmp_w1, cmp_w2, cos, sin)
            bl = layer - N_A_LAYERS
            y = nsa_mixer(h, nsa_w_q[bl], nsa_q_norm[bl], nsa_w_out[bl], shared, cos, sin)
        x = x + gate[:, None, :] * y
        shift, scale, gate = jnp.split(mods[2 * layer + 1], 3, axis=-1)
        h = modulate(x, norm_ffn[layer], shift, scale)
        x = x + gate[:, None, :] * swiglu(h, ffn_w_in[layer], ffn_w_out[layer])
    return x


def setup_inputs(seed=0):
    out = dict(first_inputs(seed))
    for name, value in second_inputs(seed + 1).items():
        if name != "x":
            out[name + "_2"] = value
    return out


def reference(
    x, mix_norm_pre, mix_norm_post, w_in, w_out, ffn_norm_pre, ffn_norm_post, w_up, conv_w,
    conv_b, w_down, c_2, ada_w_2, ada_b_2, norm_mix_2, norm_ffn_2, hgrn_w_in_2,
    hgrn_lower_bounds_2, hgrn_out_norm_2, hgrn_w_out_2, kv_ada_w_2, kv_ada_b_2, kv_norm_2,
    nsa_w_kv_2, nsa_k_norm_2, cmp_pos_2, cmp_w1_2, cmp_w2_2, nsa_w_q_2, nsa_q_norm_2,
    nsa_w_out_2, ffn_w_in_2, ffn_w_out_2,
):
    x = first_block(
        x, mix_norm_pre, mix_norm_post, w_in, w_out, ffn_norm_pre, ffn_norm_post, w_up, conv_w,
        conv_b, w_down,
    )
    return second_block(
        x, c_2, ada_w_2, ada_b_2, norm_mix_2, norm_ffn_2, hgrn_w_in_2, hgrn_lower_bounds_2,
        hgrn_out_norm_2, hgrn_w_out_2, kv_ada_w_2, kv_ada_b_2, kv_norm_2, nsa_w_kv_2,
        nsa_k_norm_2, cmp_pos_2, cmp_w1_2, cmp_w2_2, nsa_w_q_2, nsa_q_norm_2, nsa_w_out_2,
        ffn_w_in_2, ffn_w_out_2,
    )


_drawn_inputs = setup_inputs


def setup_inputs(seed=0):
    import zlib

    import numpy as np

    out = dict(_drawn_inputs(seed))
    spreads = {}
    factors = {'mix_norm_post': 3.308,
     'ffn_norm_pre': 3.174,
     'ffn_norm_post': 4.669,
     'conv_b': 6.691,
     'ada_b_2': 3.399,
     'norm_mix_2': 8.0,
     'norm_ffn_2': 8.0,
     'hgrn_out_norm_2': 8.0,
     'kv_ada_b_2': 8.0,
     'kv_norm_2': 27.059,
     'nsa_k_norm_2': 25.988,
     'cmp_pos_2': 30.129,
     'nsa_q_norm_2': 27.963}
    for name, (base, spread) in spreads.items():
        noise = np.random.default_rng([zlib.crc32(name.encode()), seed]).standard_normal(out[name].shape)
        drawn = base * np.exp(spread * noise) if base else spread * noise
        out[name] = __import__('jax').numpy.asarray(drawn.astype(out[name].dtype))
    for name, factor in factors.items():
        out[name] = (out[name] * factor).astype(out[name].dtype)
    return out
```

```python
from contextlib import ExitStack

import numpy as np

import concourse.bass as bass
from concourse import mybir

F32 = mybir.dt.float32
I8 = mybir.dt.int8
ALU = mybir.AluOpType
ACT = mybir.ActivationFunctionType
AX = mybir.AxisListType.X

P = 128
S = 512
NT = S // P
D = 1024
KT = D // P
HD = 64
RH = 8
TOPK = 128
DFF = 2816
FT = DFF // P
EPS = 1e-6
NEG = -1e30
REPLACED = -3e38
SCALE = HD ** -0.5
HH = 8
LEVELS = 7
NSA_H, NSA_KV, GROUP = 16, 4, 4
NCMP = 31
RING = 2
SLOT = 4096
FFN_UNITS = FT // 2
HALF = 512

ROWS_IN = 14 * 16
VEC_ROWS = [("mix_norm_pre", 8), ("ffn_norm_pre", 8), ("norm_mix_2", 16), ("norm_ffn_2", 16), ("kv_norm_2", 8), ("c_2", 8)]


def shape_constants():
    f = np.float32
    inv = (f(10000.0) ** (-np.arange(0, HD, 2, dtype=f) / f(HD))).astype(f)
    ang = np.arange(S, dtype=f)[:, None] * inv[None, :]
    tok = lambda a: np.ascontiguousarray(a.reshape(NT, P, -1).transpose(1, 0, 2))
    rope = np.stack([tok(np.cos(ang)), tok(np.sin(ang)), tok(-np.sin(ang))], axis=1).astype(f)
    p = np.arange(P)
    j = np.arange(S)
    log_g = np.log(1.0 - 2.0 ** (-5.0 - np.arange(RH)))
    diff = j[None, :] - p[:, None]
    decay = np.where(diff[:, None, :] >= 0, np.exp(log_g[None, :, None] * np.maximum(diff, 0)[:, None, :]), 0.0) * SCALE
    strip = np.where(j[None, :] - 3 * P > p[:, None], NEG, 0.0)
    a, b = p[:, None], p[None, :]
    masks = [a == b]
    for level in range(LEVELS):
        c = 1 << level
        masks.append((a // (2 * c) == b // (2 * c)) & (a % (2 * c) < c) & (b % (2 * c) >= c))
    t = (np.arange(NT)[None, :] * P + p[:, None])
    end = np.arange(NCMP) * 16 + 31
    cmp_bias = np.where(end[None, None, :] <= t[:, :, None], 0.0, NEG)
    keep = np.ones((P, S))
    keep[:, ::P] = 0.0
    small = np.concatenate([np.eye(P), rope.reshape(P, -1), strip, cmp_bias.reshape(P, -1), (t >= 31) * 1.0, keep], axis=1)
    return {"c_small": small.astype(f), "c_decay": decay.astype(f).reshape(P, RH * S),
            "c_masks": np.stack(masks, 1).astype(f)}


def build(nc, io, out):
    ctx = ExitStack()
    with ctx:
        def sb(name, shape, dt=F32):
            return ctx.enter_context(nc.sbuf_tensor(name, shape, dt))

        def sem(name):
            return ctx.enter_context(nc.semaphore(name))

        ps = ctx.enter_context(nc.psum_tensor("ps", [P, 8, HALF], F32))
        x_tok = sb("x_tok", [P, NT, D])
        h_t = sb("h_t", [P, KT, S])
        ring = sb("ring", [P, RING, SLOT])
        row = sb("row", [P, 2, D])
        c_rep = sb("c_rep", [P, KT, P])
        small = sb("small", [P, 128 + 3 * 128 + 512 + 124 + 4 + 512])
        masks = sb("masks", [P, LEVELS + 1, P], I8)
        vec = sb("vec", [P, 304])
        mod = sb("mod", [P, 5, 2, KT])
        ones = sb("ones", [1, P])
        out_norm = sb("out_norm", [P, P])
        qk_norm = sb("qk_norm", [P, 3, HD])
        cmp_norm = sb("cmp_norm", [P, HD])
        stat = sb("stat", [P, 256])
        fac = sb("fac", [P, 96])
        arena = sb("arena", [P, 28160])
        small2 = sb("small2", [P, 1040])
        junk = sb("junk", [P, D])
        junk2 = junk[:, HALF:D]
        eps = sb("eps", [P, 1])
        c_act = sb("c_act", [P, KT])
        best = sb("best", [P, 8])
        w2_sb = sb("w2_sb", [P, 2, 2, HD])

        ident = small[:, 0:128]
        rope_t = small[:, 128:512].rearrange("p (k t d) -> p k t d", k=3, t=NT)
        strip = small[:, 512:1024]
        cmp_bias = small[:, 1024:1148].rearrange("p (t c) -> p t c", t=NT)
        row_valid = small[:, 1148:1152]
        keep = small[:, 1152:1664]

        def carve(sizes):
            at, got = 0, []
            for n in sizes:
                got.append(arena[:, at:at + n])
                at += n
            assert at <= 28160, at
            return got

        bank_full = [sem(f"bank_full{b}") for b in range(8)]
        bank_free = [sem(f"bank_free{b}") for b in range(8)]
        landed = [sem(f"landed{r}") for r in range(RING)]
        names = """consts_in x_in rows_in out_norm_in cmp_pos_in row_in out_done vec_done c_act_done c_rep_done ones_done
            norm_rms xn_ready x_ready down_step ada_step mod_ready gate_ready rope_done iw_done decayed ret_pv
            rel_used picked ret_square ret_rms ret_normed mixed_ready p_ready pv_done o_done y_ready y_square y_rms
            y_scaled act_step dve_step pool_step hid_gate hid_up hid_done v_done sg_done f_abs logf_done k_log k_done
            g_done d_sub d_exp qk_done q1_done attn_diag attn_zero o_raw ho_square ho_rms ho_ready cmp_sq cmp_rms
            cmp_tok cmp_l cmp_p cmp_o raw_done raw_sq raw_rms raw_norm rope2_done gates_exp gates_done branch_out
            nsa_added u_done h1_done e_done conv_pre tabs_done ho_scaled eq_done vpart kvraw w2_in gained""".split()
        s = {n: sem(n) for n in names}

        bank_use, bank_fills, bank_frees, turn = {}, [0] * 8, [0] * 8, [0]

        def plan_bank(key, bank=None, counted=True):
            if bank is None:
                bank = turn[0]
                turn[0] = (bank + 1) % 8
            assert key not in bank_use, key
            bank_use[key] = (bank, bank_fills[bank], bank_frees[bank])
            bank_fills[bank] += counted
            bank_frees[bank] += 1
        FULL, FREE = bank_full, bank_free

        def open_bank(key):
            b, _, free = bank_use[key]
            if free > 0:
                nc.tensor.wait_ge(FREE[b], free)
            return ps[:, b]

        def filled(eng, key):
            b, fill, _ = bank_use[key]
            eng.wait_ge(FULL[b], fill + 1)
            return ps[:, b]

        def full(key):
            return FULL[bank_use[key][0]]

        def free(key):
            return FREE[bank_use[key][0]]

        def evacuated(eng, key):
            b, _, f = bank_use[key]
            eng.wait_ge(FREE[b], f + 1)

        def own_order(eng, own):
            count = [0]

            def step(ins):
                ins.then_inc(own, 1)
                count[0] += 1

            def after():
                if count[0]:
                    eng.wait_ge(own, count[0])

            return step, after

        units, unit_at, slot_dmas = [], {}, [0] * RING

        def unit(key, pieces, release):
            n = len(units)
            slot_dmas[n % RING] += len(pieces)
            unit_at[key] = (n % RING, 16 * slot_dmas[n % RING])
            units.append((n, pieces, release))

        def arrived(eng, key):
            slot, count = unit_at[key]
            eng.wait_ge(landed[slot], count)
            return ring[:, slot]

        def columns(w, c0, n, at=0, width=None):
            width = width or n
            return (lambda sl: sl[:, 0:KT * width].rearrange("p (k n) -> p k n", k=KT)[:, :, at:at + n],
                    w[:, c0:c0 + n].rearrange("(k p) n -> p k n", p=P))

        down_groups = [(0, 4), (4, 4), (8, 4), (12, 4), (16, 4), (20, 2)]
        down_count = [0]
        ada_count = [0]

        w_in, w_out = io["w_in"][0], io["w_out"][0]
        P1 = {"iq": [(2688, 512)], "kk": [(2560, 128), (3200, 72)], "aq": [(2048, 512)], "rk": [(512, 512)],
              "rq": [(0, 512)], "rv": [(1024, 512)], "rg": [(1536, 512)]}
        P1_ORDER = ["iq", "kk", "aq", "rk", "rq", "rv", "rg"]
        ROPED = ["iq", "kk", "aq", "rk", "rq"]

        plan_bank("vec")

        def plan_norm(i):
            for kt in range(KT):
                plan_bank(("xT", i, kt))

        def plan_tok_gemm(name, pieces_of, n_units):
            for u in range(n_units):
                for t in range(NT):
                    plan_bank((name, u, t))
                unit((name, u), pieces_of(u), ("bank", (name, u, NT - 1)))

        def plan_ffn(i, w_up, w_down):
            for u in range(FFN_UNITS):
                for j in range(4):
                    plan_bank(("up", i, u, j))
                unit(("up", i, u), [columns(w_up, u * 256, 256, 0, 512), columns(w_up, DFF + u * 256, 256, 256, 512)],
                     ("bank", ("up", i, u, 3)))
            for j in range(8):
                plan_bank(("down", i, j))
            for g, (k0, n) in enumerate(down_groups):
                down_count[0] += g < len(down_groups) - 1
                unit(("down", i, g), [(lambda sl, n=n: sl[:, 0:n * D].rearrange("p (k n) -> p k n", k=n),
                                       w_down[k0 * P:(k0 + n) * P, :].rearrange("(k p) n -> p k n", p=P))],
                     ("bank", ("down", i, 7)) if g == len(down_groups) - 1 else ("sem", "down_step", down_count[0]))

        ADA_W = [io["ada_w_2"][m] for m in range(4)] + [io["kv_ada_w_2"]]
        ADA_B = [io["ada_b_2"][m:m + 1] for m in range(4)] + [io["kv_ada_b_2"].rearrange("(a n) -> a n", a=1)]

        def ada_cols(m):
            return 6 if m < 4 else 4

        def plan_ada(m):
            n = ada_cols(m)
            for j in range(n):
                plan_bank(("ada", m, j))
            for k in range(KT):
                pieces = [(lambda sl, n=n: sl[:, 0:n * HALF], ADA_W[m][k * P:(k + 1) * P, :])]
                if 2 * k < n:
                    pieces.append((lambda sl: sl[0:1, 3072:4096], ADA_B[m][:, k * 1024:(k + 1) * 1024]))
                ada_count[0] += k < KT - 1
                unit(("ada", m, k), pieces,
                     ("bank", ("ada", m, n - 1)) if k == KT - 1 else ("sem", "ada_step", ada_count[0]))

        def plan_out(name, w, n_in=KT):
            for kt in range(n_in):
                plan_bank((name, "T", kt))
            plan_tok_gemm(name, lambda u: [columns(w, u * 512, 512)], 2)

        def plan_attention(name, n_units, okeys):
            for i in range(n_units + 2):
                if i < n_units:
                    plan_bank((name, "S", i), i % 3)
                if 1 <= i <= n_units:
                    plan_bank((name, "T", i - 1), 3 + (i - 1) % 3)
                if i >= 2 and (i - 2) % 8 == 0:
                    plan_bank((name, "O", (i - 2) // 8), 6 + ((i - 2) // 8) % 2, counted=False)

        plan_norm(0)
        lagged = []
        for name in P1_ORDER:
            pieces, at = [], 0
            total = sum(n for _, n in P1[name])
            for c0, n in P1[name]:
                pieces.append(columns(w_in, c0, n, at, total))
                at += n
            unit(name, pieces, ("bank", (name, NT - 1)))
            for t in range(NT):
                plan_bank((name, t))
                if lagged:
                    plan_bank(lagged.pop(0))
                if name in ROPED:
                    lagged.append((name, "T", t))
        for t in range(1, NT):
            for h in range(RH):
                plan_bank(("index", t, h))
        unit("decay", [(lambda sl: sl[:, :], io["c_decay"])], ("sem", "decayed", RH))
        for h in range(RH + 1):
            if h < RH:
                for m in range(NT):
                    plan_bank(("ret_s", h, m), m)
            if h == 1:
                for t in range(NT):
                    plan_bank(("ret_o", t), 4 + t)
        DSA_UNITS = [(t, h) for t in range(NT) for h in range(RH)]
        plan_attention("dsa", len(DSA_UNITS), None)
        plan_out("mix1", w_out)
        plan_norm(1)
        plan_ffn(0, io["w_up"][0], io["w_down"][0])
        plan_ada(0)
        plan_norm(2)
        hw = io["hgrn_w_in_2"][0]
        for u in range(2):
            for j in range(4):
                plan_bank(("hq", u, j))
            unit(("hq", u), [columns(hw, u * 512, 512)], ("bank", ("hq", u, 3)))
        plan_tok_gemm("hg", lambda u: [columns(hw, 3072 + u * 512, 512)], 2)
        for u in range(2):
            for j in range(4):
                plan_bank(("hf", u, j))
            unit(("hf", u), [columns(hw, 1024 + u * 512, 512)], ("bank", ("hf", u, 3)))
        plan_tok_gemm("hi", lambda u: [columns(hw, 2048 + u * 512, 512)], 2)
        for h in range(HH + 1):
            if h < HH:
                for lv in range(LEVELS + 1):
                    plan_bank(("diag", h, lv), lv % 4)
                for b in range(2):
                    plan_bank(("far", h, b), 4 + b)
            if h >= 1:
                plan_bank(("ho", h - 1), 6 + h % 2)
        plan_out("mix2", io["hgrn_w_out_2"][0])
        plan_ada(1)
        plan_norm(3)
        plan_ffn(1, io["ffn_w_in_2"][0], io["ffn_w_out_2"][0])
        plan_ada(2)
        plan_ada(4)
        plan_norm(4)
        wkv, wq = io["nsa_w_kv_2"], io["nsa_w_q_2"][0]
        for j in range(4):
            plan_bank(("kvc", j))
        unit("kvc", [columns(wkv, 0, 512)], ("bank", ("kvc", 3)))
        plan_tok_gemm("kvs", lambda u: [columns(wkv, 512 + u * 512, 512)], 2)
        plan_tok_gemm("nq", lambda u: [columns(wq, u * 512, 512 if u < 2 else 48)], 3)
        w1 = io["cmp_w1_2"]
        for kv in range(2):
            for j in range(4):
                plan_bank(("cmp1", kv, j))
            for rh in range(2):
                src = w1[kv, rh * 1024:(rh + 1) * 1024, :].rearrange("(r d) n -> d r n", d=HD)
                unit(("cmp1", kv, rh), [(lambda sl, q=q: sl[64 * q:64 * q + 64, :].rearrange("p (r n) -> p r n", r=16), src)
                                        for q in range(2)],
                     ("bank", ("cmp1", kv, 3)) if rh else ("sem", "vpart", kv + 1))
        plan_bank("cmp2")
        plan_bank("cmpT")
        for t in range(NT):
            for j in range(5):
                plan_bank(("nT", t, j))
        GROUPS = [(t, kp) for t in range(NT) for kp in range(2)]
        for i in range(len(GROUPS) + 2):
            if i < len(GROUPS):
                for q in range(2):
                    plan_bank(("cS", i, q), q + 2 * (i % 2))
            if 1 <= i <= len(GROUPS):
                for q in range(2):
                    plan_bank(("cT", i - 1, q), 4 + q)
            if i >= 2:
                plan_bank(("cO", i - 2), 6 + i % 2)
        NSA_GROUPS = [(t, kp, br) for t in range(NT) for kp in range(2) for br in range(2)]
        plan_attention("nsa", 8 * len(NSA_GROUPS), None)
        plan_out("mix3", io["nsa_w_out_2"][0])
        plan_ada(3)
        plan_norm(5)
        plan_ffn(2, io["ffn_w_in_2"][1], io["ffn_w_out_2"][1])

        (a_xn, a_rq, a_rk, a_aq, a_iq, a_kk, a_rv, a_rg, a_av, a_tmp, a_sT, a_isc, a_sel, a_rel) = carve(
            [4096, 2048, 2048, 2048, 2048, 1024, 2048, 2048, 256, 3328, 2560, 1536, 1536, 1024])
        tiles4 = lambda a: a.rearrange("p (k n) -> p k n", k=4)
        xn = tiles4(a_xn)
        T1 = {"rq": tiles4(a_rq), "rk": tiles4(a_rk), "aq": tiles4(a_aq), "iq": tiles4(a_iq),
              "kk": a_kk.rearrange("p (k n) -> p k n", k=2)}
        rv_tok, rg_tok, av_tok = tiles4(a_rv), tiles4(a_rg), tiles4(a_av)
        iw = fac[:, 64:96].rearrange("p (t h) -> p t h", t=NT)
        rope_a, rope_b, rope_o = [a_tmp[:, i * 1024:(i + 1) * 1024].rearrange("p (j n) -> p j n", j=2) for i in range(3)]
        sT = a_sT.rearrange("p (j n) -> p j n", j=2)
        isc = a_isc.rearrange("p (j n) -> p j n", j=3)
        sel_bias = a_sel.rearrange("p (j n) -> p j n", j=3)
        rel = a_rel.rearrange("p (j n) -> p j n", j=2)
        mixed = tiles4(a_xn)
        att_l, att_p, att_pt = rope_a, rope_b, rope_o
        y1 = arena[:, 4096:8192].rearrange("p (k n) -> p k n", k=4)

        f_xn, f_hid, f_tmp = carve([4096, FT * S, 8 * S])
        hid = f_hid.rearrange("p (k n) -> p k n", k=FT)
        ftmp = f_tmp.rearrange("p (j q n) -> p j q n", j=2, q=4)
        yf = tiles4(f_xn)

        (h_v, h_sg, h_q, h_k, h_g, h_d0, h_at) = carve([4096, 4096, 4096, 4096, 4096, 3584, 4096])
        v_tok, sg_tok = tiles4(h_v), tiles4(h_sg)
        xn_h = tiles4(h_v)
        HQ, HK, HG = [a.rearrange("p (h n) -> p h n", h=HH) for a in (h_q, h_k, h_g)]
        lvl = [h_d0.rearrange("p (l n) -> p l n", l=LEVELS),
               h_t[:, 0:LEVELS, :]]
        attn = h_at.rearrange("p (j s n) -> p j s n", j=2, s=NT)
        f_work = [arena[:, 20480:22528], arena[:, 22528:24576], arena[:, 24576:26624]]
        k1 = small2[:, 0:512].rearrange("p (s n) -> p s n", s=4)
        q1 = small2[:, 512:1024].rearrange("p (s n) -> p s n", s=4)
        tot = small2[:, 1024:1032]
        y2 = tiles4(h_q)

        (n_xn, n_raw, n_qn, n_qr, n_k, n_v, n_hkv) = carve([4096, 6144, 4096, 4096, 2048, 2048, 4096])
        raw = n_raw.rearrange("p (t h d) -> p t h d", t=NT, h=24)
        qn_t = n_qn.rearrange("p (k n) -> p k n", k=8)
        qr_t = n_qr.rearrange("p (k n) -> p k n", k=8)
        k_t = tiles4(n_k)
        v_nsa = n_v.rearrange("p (t b n) -> p t b n", t=NT, b=2)
        hkv_t = n_hkv.rearrange("p (k n) -> p k n", k=8)
        win = n_qn[:, 0:3968].rearrange("p (j i r) -> p j i r", j=4, i=NCMP)
        h1 = small2[:, 0:496].rearrange("p (kv n q c i) -> p kv n q c i", kv=2, n=2, q=2, c=2)
        kc_raw = small2[0:NCMP, 496:752]
        kc_tok = small2[0:NCMP, 752:1008].rearrange("p (h d) -> p h d", h=4)
        vc_tok = n_hkv[:, 3456:3712].rearrange("p (h d) -> p h d", h=4)
        kc_t = n_hkv[:, 3712:3776].rearrange("p (c i) -> p c i", c=2)
        nsa_tok = tiles4(n_xn)
        n_a, n_b, n_o = [n_hkv[:, i * 1024:(i + 1) * 1024].rearrange("p (j n) -> p j n", j=2) for i in range(3)]
        cl = n_raw[:, 0:496].rearrange("p (j h c) -> p j h c", j=2, h=8)
        cp = n_raw[:, 512:1008].rearrange("p (j h c) -> p j h c", j=2, h=8)
        cpt = n_raw[0:NCMP, 1024:3072].rearrange("p (j h n) -> p j h n", j=2, h=8)
        n_tmp = n_raw[:, 3072:4096].rearrange("p (j n) -> p j n", j=2)
        gates = n_hkv[:, 3072:3264].rearrange("p (t g) -> p t g", t=NT)
        gates_e = n_hkv[:, 3264:3456].rearrange("p (t g) -> p t g", t=NT)
        y3 = tiles4(n_qn)

        XN = {0: xn, 1: tiles4(f_xn), 2: xn_h, 3: tiles4(f_xn), 4: tiles4(n_xn), 5: tiles4(f_xn)}

        vec_at, at = {}, 0
        for n, r in VEC_ROWS:
            vec_at[n] = at
            at += r
        CONV = 64
        POS = CONV + 176

        def vcol(name, i=0):
            return vec[:, vec_at[name] + 8 * i:vec_at[name] + 8 * i + 8]

        NORM_OUT = {
            0: [(h_t, vcol("mix_norm_pre"), None)], 1: [(h_t, vcol("ffn_norm_pre"), None)],
            2: [(h_t, mod[:, 0, 0], mod[:, 0, 1])], 3: [(h_t, mod[:, 1, 0], mod[:, 1, 1])],
            4: [(h_t, mod[:, 2, 0], mod[:, 2, 1]), (hkv_t, mod[:, 4, 0], mod[:, 4, 1])],
            5: [(h_t, mod[:, 3, 0], mod[:, 3, 1])]}
        MOD_GAIN = {0: vcol("norm_mix_2", 0), 1: vcol("norm_ffn_2", 0), 2: vcol("norm_mix_2", 1),
                    3: vcol("norm_ffn_2", 1), 4: vcol("kv_norm_2")}
        MOD_ORDER = [0, 1, 2, 4, 3]
        MOD_READY = {m: i + 1 for i, m in enumerate(MOD_ORDER)}
        NORM_MOD = {2: 0, 3: 1, 4: 4, 5: 3}

        vec_rows = arena[0:64, 8192:8320]
        conv_rows = [arena[0:88, 8320:8448], arena[0:88, 8448:8576]]
        mask_rows = arena[:, 9216:9216 + (LEVELS + 1) * P].rearrange("p (l n) -> p l n", l=LEVELS + 1)
        pos_rows = arena[0:32, 8576:8832]

        def dsa_unit(i):
            t, h = DSA_UNITS[i]
            q = slice(64 * (h % 2), 64 * (h % 2) + 64)
            n = (t + 1) * P
            return dict(q=T1["aq"][q, h // 2, t * P:(t + 1) * P], k=T1["kk"][q, 0, 0:n], n=n,
                        bias=strip[:, 3 * P:] if t == 0 else sel_bias[:, t - 1, 0:n],
                        v=lambda b: av_tok[:, b, :], slot=h)

        def nsa_unit(i):
            t, kp, br = NSA_GROUPS[i // 8]
            g, ko = (i % 8) // 2, i % 2
            q = slice(64 * ko, 64 * ko + 64)
            n = (t + 1) * P
            c = (kp * 2 + ko) * HD
            return dict(q=qr_t[q, kp * 4 + g, t * P:(t + 1) * P], k=k_t[q, 2 * br + kp, 0:n], n=n,
                        bias=strip[:, 3 * P - t * P:],
                        v=lambda b: v_nsa[:, b, br, c:c + HD], slot=ko * 4 + g)

        ATT = {"dsa": (dsa_unit, len(DSA_UNITS), (att_l, att_p, att_pt), 0),
               "nsa": (nsa_unit, 8 * len(NSA_GROUPS), (n_a, n_b, n_o), len(DSA_UNITS))}
        neg_max = stat[:, 160:164]
        den = fac[:, 0:16].rearrange("p (j h) -> p j h", j=2)
        rden = fac[:, 16:32].rearrange("p (j h) -> p j h", j=2)

        def tok_keys(name):
            return [(u, t, (name, u, t)) for u in range(2) for t in range(NT)]

        def down_keys(i):
            return [(u, t, ("down", i, 2 * t + u)) for u in range(2) for t in range(NT)]

        block = ctx.enter_context(nc.Block())

        @block.sync
        def _(sp):
            for n, pieces, _ in units:
                if n >= RING:
                    kind = units[n - RING][2]
                    if kind[0] == "bank":
                        filled(sp, kind[1])
                    else:
                        sp.wait_ge(s[kind[1]], kind[2])
                for dst, src in pieces:
                    sp.dma_start(dst(ring[:, n % RING]), src).then_inc(landed[n % RING], 16)

        @block.gpsimd
        def _(pool):
            g = nc.gpsimd
            g.memset(ones[:, :], 1.0).then_inc(s["ones_done"], 1)

            def load_row(src, i, n):
                pool.dma_start(row[:, i, :], src.partition_broadcast(P)).then_inc(s["row_in"], 16)

            load_row(io["mix_norm_post"][0], 0, 0)
            load_row(io["ffn_norm_post"][0], 1, 0)

            def add_to_x(stage, y, keys=None):
                for t in range(NT):
                    if keys is None:
                        pool.wait_ge(s["y_scaled"], NT * stage + t + 1)
                    else:
                        for _, tt, key in keys:
                            if tt == t:
                                evacuated(pool, key)
                    g.tensor_tensor(x_tok[:, t], x_tok[:, t], y[:, t], ALU.add).then_inc(s["x_ready"], 1)

            dec = arrived(pool, "decay")
            for h in range(RH):
                for m in range(NT):
                    n = S - m * P
                    evacuated(pool, ("ret_s", h, m))
                    o = [0, 512, 896, 1152][m]
                    ins = g.tensor_tensor(sT[:, h % 2, o:o + n], sT[:, h % 2, o:o + n], dec[:, h * S:h * S + n], ALU.mult)
                    if m == NT - 1:
                        ins.then_inc(s["decayed"], 1)
            for t in range(NT):
                evacuated(pool, ("ret_o", t))
                g.tensor_tensor(mixed[:, t, 0:512], mixed[:, t, 0:512], rg_tok[:, t], ALU.mult).then_inc(s["mixed_ready"], 1)
            add_to_x(0, y1)
            add_to_x(1, yf)
            pool.wait_ge(s["out_norm_in"], 16)
            for u in range(2):
                for t in range(NT):
                    evacuated(pool, ("hg", u, t))
                    w = sg_tok[:, t, u * 512:(u + 1) * 512].rearrange("p (h d) -> p h d", h=4)
                    g.tensor_tensor(w, w, out_norm[:, :].unsqueeze(1).broadcast_to([P, 4, P]), ALU.mult).then_inc(s["sg_done"], 1)
            pool.wait_ge(s["k_done"], 2)
            g.memset(attn[:, :, :, :], 0.0).then_inc(s["attn_zero"], 1)
            for h in range(HH):
                pool.wait_ge(s["g_done"], h + 1)
                if h == 0:
                    pool.wait_ge(s["k_done"], 2)
                if h >= 2:
                    filled(pool, ("diag", h - 2, LEVELS))
                if h == 1:
                    filled(pool, ("hi", 1, NT - 1))
                for lv in range(LEVELS):
                    c = 1 << lv
                    src = HG[:, h].rearrange("p (b q c) -> p b q c", q=2, c=c)
                    dst = lvl[h % 2][:, lv].rearrange("p (b q c) -> p b q c", q=2, c=c)
                    mid = src[:, :, 0, c - 1:c].broadcast_to([P, S // (2 * c), c])
                    g.tensor_tensor(dst[:, :, 0], mid, src[:, :, 0], ALU.subtract).then_inc(s["d_sub"], 1)
                    g.tensor_tensor(dst[:, :, 1], src[:, :, 1], mid, ALU.subtract).then_inc(s["d_sub"], 1)
            for t in range(NT):
                pool.wait_ge(s["ho_scaled"], t + 1)
                g.tensor_tensor(v_tok[:, t], v_tok[:, t], sg_tok[:, t], ALU.mult).then_inc(s["ho_ready"], 1)
            add_to_x(2, y2, tok_keys("mix2"))
            add_to_x(3, yf, down_keys(1))
            for t in range(NT):
                for j in range(3):
                    i = 3 * t + j
                    pool.wait_ge(s["raw_norm"], i + 1)
                    if j < 2:
                        w = n_a[:, i % 2].rearrange("p (h d) -> p h d", h=8)
                        g.tensor_tensor(w, w, qk_norm[:, 0:1, :].broadcast_to([P, 8, HD]), ALU.mult).then_inc(s["gained"], 1)
                    else:
                        w = n_a[:, i % 2].rearrange("p (k h d) -> p k h d", k=2, h=4)
                        g.tensor_tensor(w, w, qk_norm[:, 1:3, :].unsqueeze(2).broadcast_to([P, 2, 4, HD]), ALU.mult).then_inc(s["gained"], 1)
            for i in range(len(NSA_GROUPS)):
                t, kp, br = NSA_GROUPS[i]
                evacuated(pool, ("nsa", "O", i))
                if i >= 1:
                    pool.wait_ge(s["nsa_added"], i)
                w = nsa_tok[:, t, kp * 512:(kp + 1) * 512]
                g.tensor_tensor(w, w, n_tmp[:, i % 2], ALU.add).then_inc(s["nsa_added"], 1)
            add_to_x(4, y3, tok_keys("mix3"))
            add_to_x(5, yf, down_keys(2))
            pool.wait_ge(s["x_ready"], 6 * NT)

        @block.scalar
        def _(act):
            a = nc.scalar
            step, after = own_order(act, s["act_step"])
            act.dma_start(small[:, :], io["c_small"]).then_inc(s["consts_in"], 16)
            act.dma_start(x_tok[:, :, :], io["x"][0].rearrange("(t p) n -> p t n", p=P)).then_inc(s["x_in"], 16)
            act.dma_start(mask_rows, io["c_masks"]).then_inc(s["consts_in"], 16)
            n_rows = 0
            for name, r in VEC_ROWS:
                src = io[name]
                src = src.rearrange("a (k p) -> (a k) p", p=P) if len(src.shape) == 2 else src.rearrange("(k p) -> k p", p=P)
                act.dma_start(vec_rows[vec_at[name]:vec_at[name] + r, :], src).then_inc(s["rows_in"], 16)
                n_rows += 16
            for j in range(3):
                act.dma_start(conv_rows[j // 2][44 * (j % 2):44 * (j % 2) + 44, :],
                              io["conv_w"][0, j].rearrange("(k p) -> k p", p=P)).then_inc(s["rows_in"], 16)
            act.dma_start(conv_rows[1][44:88, :], io["conv_b"][0].rearrange("(k p) -> k p", p=P)).then_inc(s["rows_in"], 16)
            for kv in range(2):
                for q in range(2):
                    act.dma_start(pos_rows[:, kv * 128 + q * 64:kv * 128 + q * 64 + 64], io["cmp_pos_2"][kv]).then_inc(s["rows_in"], 16)
            assert n_rows + 16 * 8 == ROWS_IN
            act.dma_start(out_norm[:, :], io["hgrn_out_norm_2"][0].partition_broadcast(P)).then_inc(s["out_norm_in"], 16)
            act.dma_start(qk_norm[:, 0, :], io["nsa_q_norm_2"][0].partition_broadcast(P)).then_inc(s["cmp_pos_in"], 16)
            act.dma_start(qk_norm[:, 1, :], io["nsa_k_norm_2"][1].partition_broadcast(P)).then_inc(s["cmp_pos_in"], 16)
            act.dma_start(qk_norm[:, 2, :], io["nsa_k_norm_2"][2].partition_broadcast(P)).then_inc(s["cmp_pos_in"], 16)
            for kv in range(2):
                act.dma_start(w2_sb[:, kv], io["cmp_w2_2"][kv].rearrange("(n p) d -> p n d", p=P)).then_inc(s["w2_in"], 16)
            act.dma_start(cmp_norm[:, :], io["nsa_k_norm_2"][0].partition_broadcast(P)).then_inc(s["cmp_pos_in"], 16)

            def norm(i):
                if i == 0:
                    act.wait_ge(s["x_in"], 16)
                for t in range(NT):
                    if i:
                        act.wait_ge(s["x_ready"], NT * (i - 1) + t + 1)
                    step(a.activation(XN[i][:, t], x_tok[:, t], ACT.Square, accum_out=stat[:, t:t + 1]))
                after()
                a.activation(stat[:, 4:8], stat[:, 0:4], ACT.Sqrt, scale=1.0 / D, bias=eps[:, :]).then_inc(s["norm_rms"], 1)
                norm_out(i)

            def norm_out(i):
                if i >= 2:
                    act.wait_ge(s["mod_ready"], MOD_READY[NORM_MOD[i]])
                for kt in range(0, KT, 2):
                    p = filled(act, ("xT", i, kt))
                    outs = NORM_OUT[i]
                    for j, (dst, gain, shift) in enumerate(outs):
                        ins = a.activation(dst[:, kt], p, ACT.Identity, scale=gain[:, kt:kt + 1],
                                           bias=0.0 if shift is None else shift[:, kt:kt + 1])
                        if j == len(outs) - 1:
                            ins.then_inc(free(("xT", i, kt)), 1)

            def post_rms(i, y, keys):
                for t in range(NT):
                    for _, tt, key in keys:
                        if tt == t:
                            evacuated(act, key)
                    step(a.activation(junk[:, 0:1024], y[:, t], ACT.Square, accum_out=stat[:, 16 + t:17 + t]))
                    after()
                a.activation(stat[:, 20:24], stat[:, 16:20], ACT.Sqrt, scale=1.0 / D, bias=eps[:, :]).then_inc(s["y_rms"], 1)

            def in_t(name):
                for kt in range(0, KT, 2):
                    p = filled(act, (name, "T", kt))
                    a.activation(h_t[:, kt], p, ACT.Copy).then_inc(free((name, "T", kt)), 1)

            def ada(m):
                if m < 4:
                    for j in range(2):
                        p = filled(act, ("ada", m, 4 + j))
                        a.activation(row[:, m % 2, j * HALF:(j + 1) * HALF], p, ACT.Copy).then_inc(free(("ada", m, 4 + j)), 1)

            def ffn(i):
                for u in range(FFN_UNITS):
                    for q in range(4):
                        buf = ftmp[:, u % 2, q]
                        if i == 0:
                            n = 22 * (q // 2) + 2 * u + q % 2
                            if u >= 2:
                                act.wait_ge(s["hid_done"], 2 * (u - 1))
                            p = filled(act, ("up", i, u, q))
                            a.activation(buf, p, ACT.Identity, scale=vec[:, CONV + 88 + n:CONV + 89 + n],
                                         bias=vec[:, CONV + 132 + n:CONV + 133 + n]).then_inc(s["conv_pre"], 1)
                        elif q < 2:
                            if u >= 2:
                                evacuated(act, ("up", i, u - 2, 2 + q))
                            p = filled(act, ("up", i, u, q))
                            a.activation(buf, p, ACT.Silu).then_inc(free(("up", i, u, q)), 1)
                    if i == 0:
                        for q in range(2):
                            evacuated(act, ("up", i, u, q))
                            a.activation(ftmp[:, u % 2, q], ftmp[:, u % 2, q], ACT.Silu).then_inc(s["hid_gate"], 1)

            def attention(name, after_t):
                unit_of, n_units, (L, PB, PT), base = ATT[name]
                for i in range(n_units + 1):
                    if i < n_units:
                        u = unit_of(i)
                        evacuated(act, (name, "S", i))
                        if i >= 2:
                            filled(act, (name, "T", i - 2))
                        if i % 8 == 0 and i >= 16:
                            evacuated(act, (name, "O", i // 8 - 2))
                        a.activation(PB[:, i % 2, 0:u["n"]], L[:, i % 2, 0:u["n"]], ACT.Exp, scale=-1.0,
                                     bias=neg_max[:, i % 4:i % 4 + 1],
                                     accum_out=den[:, (i // 8) % 2, u["slot"]:u["slot"] + 1]).then_inc(s["p_ready"], 1)
                    if i >= 1 and (i - 1) % 2 == 0:
                        pt_out(act, a, name, i - 1)

            def pt_out(eng, e, name, i):
                unit_of, _, (_, _, PT), base = ATT[name]
                n = unit_of(i)["n"]
                if i >= 2:
                    eng.wait_ge(s["pv_done"], base + i - 1)
                p = filled(eng, (name, "T", i))
                a.activation(PT[:, i % 2, 0:n], p[:, 0:n], ACT.Copy).then_inc(free((name, "T", i)), 1)

            evacuated(act, "vec")
            act.wait_ge(s["e_done"], 1)
            a.activation(c_act[:, :], vcol("c_2"), ACT.Silu).then_inc(s["c_act_done"], 1)
            norm(0)
            for n, name in enumerate(P1_ORDER):
                for t in range(NT):
                    if name == "rv":
                        p = filled(act, (name, t))
                        a.activation(rv_tok[:, t], p, ACT.Copy).then_inc(free((name, t)), 1)
                    if name == "rg":
                        p = filled(act, (name, t))
                        a.activation(rg_tok[:, t], p, ACT.Silu).then_inc(free((name, t)), 1)
                if name in ROPED:
                    for t in range(NT):
                        nb = 2 if name == "kk" else 4
                        p = filled(act, (name, "T", t))
                        a.activation(T1[name][:, :, t * P:(t + 1) * P], p[:, 0:nb * P].rearrange("p (k n) -> p k n", k=nb),
                                     ACT.Copy).then_inc(free((name, "T", t)), 1)
            i = 0
            for t in range(1, NT):
                n = (t + 1) * P
                for h in range(RH):
                    p = filled(act, ("index", t, h))
                    if i >= 2:
                        act.wait_ge(s["rel_used"], i - 1)
                    a.activation(rel[:, i % 2, 0:n], p[:, 0:n], ACT.Relu).then_inc(free(("index", t, h)), 1)
                    i += 1
            for h in range(RH):
                for m in range(NT):
                    n = S - m * P
                    o = [0, 512, 896, 1152][m]
                    if h >= 2 and m == 0:
                        act.wait_ge(s["ret_pv"], h - 1)
                    p = filled(act, ("ret_s", h, m))
                    a.activation(sT[:, h % 2, o:o + n], p[:, 0:n], ACT.Copy).then_inc(free(("ret_s", h, m)), 1)
            for t in range(NT):
                p = filled(act, ("ret_o", t))
                if t >= 1:
                    act.wait_ge(s["ret_rms"], t)
                a.activation(junk[:, 0:512], p, ACT.Square).then_inc(s["ret_square"], 1)
            act.wait_ge(s["ret_rms"], NT)
            a.activation(stat[:, 64:96], stat[:, 32:64], ACT.Sqrt, scale=1.0 / HD, bias=eps[:, :]).then_inc(s["ret_square"], 1)
            attention("dsa", None)
            in_t("mix1")
            post_rms(0, y1, tok_keys("mix1"))
            norm(1)
            ffn(0)
            post_rms(1, yf, down_keys(0))
            ada(0)
            norm(2)
            for u in range(2):
                for j in range(4):
                    p = filled(act, ("hq", u, j))
                    a.activation(HQ[:, 4 * u + j], p, ACT.Silu).then_inc(free(("hq", u, j)), 1)
            for u in range(2):
                for t in range(NT):
                    p = filled(act, ("hg", u, t))
                    a.activation(sg_tok[:, t, u * 512:(u + 1) * 512], p, ACT.Silu).then_inc(free(("hg", u, t)), 1)
            for u in range(2):
                fa, fe, fl = f_work
                if u:
                    act.wait_ge(s["logf_done"], 4)
                for j in range(4):
                    p = filled(act, ("hf", u, j))
                    step(a.activation(fa[:, j * S:(j + 1) * S], p, ACT.Abs))
                after()
                step(a.activation(fe, fa, ACT.Exp, scale=-1.0))
                after()
                a.activation(fl, fe, ACT.Ln, bias=1.0).then_inc(s["f_abs"], 1)
                for j in range(4):
                    evacuated(act, ("hf", u, j))
                a.activation(HK[:, 4 * u:4 * u + 4], HK[:, 4 * u:4 * u + 4], ACT.Exp).then_inc(s["k_done"], 1)
            for u in range(2):
                for t in range(NT):
                    p = filled(act, ("hi", u, t))
                    a.activation(v_tok[:, t, u * 512:(u + 1) * 512], p, ACT.Copy).then_inc(free(("hi", u, t)), 1)
            for h in range(HH + 1):
                if h < HH:
                    G = HG[:, h].rearrange("p (t n) -> p t n", t=NT)
                    act.wait_ge(s["d_sub"], 2 * LEVELS * (h + 1))
                    a.activation(lvl[h % 2], lvl[h % 2], ACT.Exp).then_inc(s["d_exp"], 1)
                    if h >= 1:
                        filled(act, ("far", h - 1, 1))
                        act.wait_ge(s["q1_done"], 4 * h)
                    a.activation(q1[:, 0:2], G[:, 1:3], ACT.Exp).then_inc(s["eq_done"], 1)
                    a.activation(q1[:, 3], G[:, 3], ACT.Exp).then_inc(s["eq_done"], 1)
                    act.wait_ge(s["tabs_done"], h + 1)
                    a.activation(q1[:, 2], G[:, 3], ACT.Exp, bias=G[:, 2, P - 1:P]).then_inc(s["eq_done"], 1)
                    for t in range(3):
                        a.activation(k1[:, t], G[:, t], ACT.Exp, scale=-1.0, bias=G[:, t, P - 1:P]).then_inc(s["eq_done"], 1)
                    a.activation(k1[:, 3], G[:, 0], ACT.Exp, scale=-1.0, bias=tot[:, 0:1]).then_inc(s["eq_done"], 1)
                if h >= 1:
                    if h >= 3:
                        filled(act, ("ho", h - 3))
                    p0 = filled(act, ("far", h - 1, 0))
                    a.activation(attn[:, (h - 1) % 2, 0, P:S], p0[:, 0:3 * P], ACT.Copy).then_inc(free(("far", h - 1, 0)), 1)
                    p1 = filled(act, ("far", h - 1, 1))
                    a.activation(attn[:, (h - 1) % 2, 1, 2 * P:S], p1[:, 0:2 * P], ACT.Copy)
                    a.activation(attn[:, (h - 1) % 2, 2, 3 * P:S], p1[:, 2 * P:3 * P], ACT.Copy).then_inc(free(("far", h - 1, 1)), 1)
            for h in range(HH):
                for t in range(NT):
                    evacuated(act, ("ho", h))
                    step(a.activation(junk[:, 0:P], v_tok[:, t, h * P:(h + 1) * P], ACT.Square,
                                            accum_out=stat[:, 96 + 8 * t + h:97 + 8 * t + h]))
                    after()
            a.activation(stat[:, 128:160], stat[:, 96:128], ACT.Sqrt, scale=1.0 / P, bias=eps[:, :]).then_inc(s["ho_rms"], 1)
            in_t("mix2")
            ada(1)
            norm(3)
            ffn(1)
            ada(2)
            norm(4)
            for u in range(2):
                for t in range(NT):
                    p = filled(act, ("kvs", u, t))
                    a.activation(v_nsa[:, t, u], p[:, 256:512], ACT.Copy).then_inc(s["kvraw"], 1)
                    a.activation(raw[:, t, 16 + 4 * u:20 + 4 * u], p[:, 0:256].rearrange("p (h d) -> p h d", h=4), ACT.Copy)\
                        .then_inc(free(("kvs", u, t)), 1)
            for u in range(2):
                for t in range(NT):
                    p = filled(act, ("nq", u, t))
                    a.activation(raw[:, t, 8 * u:8 * u + 8], p.rearrange("p (h d) -> p h d", h=8), ACT.Copy)\
                        .then_inc(free(("nq", u, t)), 1)
            for t in range(NT):
                p = filled(act, ("nq", 2, t))
                a.activation(gates_e[:, t], p[:, 0:48], ACT.Exp, scale=-1.0).then_inc(free(("nq", 2, t)), 1)
            act.wait_ge(s["raw_done"], 3 * NT)
            a.activation(stat[:, 128:224], stat[:, 32:128], ACT.Sqrt, scale=1.0 / HD, bias=eps[:, :]).then_inc(s["raw_rms"], 1)
            for kv in range(2):
                for n in range(2):
                    for q in range(2):
                        p = filled(act, ("cmp1", kv, 2 * n + q))
                        a.activation(h1[:, kv, n, q], p[:, 0:62].rearrange("p (c i) -> p c i", c=2), ACT.Silu)\
                            .then_inc(free(("cmp1", kv, 2 * n + q)), 1)
            act.wait_ge(s["cmp_sq"], 1)
            a.activation(stat[0:NCMP, 248:252], stat[0:NCMP, 244:248], ACT.Sqrt, scale=1.0 / HD, bias=eps[0:NCMP, :]).then_inc(s["cmp_rms"], 1)
            for t in range(NT):
                for j in range(0, 5, 2):
                    p = filled(act, ("nT", t, j))
                    dst = [qn_t[:, 0:4], qn_t[:, 4:8], qr_t[:, 0:4], qr_t[:, 4:8], k_t][j]
                    a.activation(dst[:, :, t * P:(t + 1) * P], p.rearrange("p (k n) -> p k n", k=4), ACT.Copy)\
                        .then_inc(free(("nT", t, j)), 1)
            for i in range(len(GROUPS) + 1):
                if i < len(GROUPS):
                    act.wait_ge(s["cmp_l"], i + 1)
                    if i >= 2:
                        filled(act, ("cT", i - 2, 1))
                    a.activation(cp[:, i % 2], cl[:, i % 2], ACT.Exp, scale=SCALE).then_inc(s["cmp_p"], 1)
                if i >= 1:
                    if i >= 3:
                        filled(act, ("cO", i - 3))
                    for q in range(2):
                        p = filled(act, ("cT", i - 1, q))
                        a.activation(cpt[:, (i - 1) % 2, 4 * q:4 * q + 4], p[0:NCMP, :].rearrange("p (g n) -> p g n", g=4),
                                     ACT.Copy).then_inc(free(("cT", i - 1, q)), 1)
            attention("nsa", None)
            in_t("mix3")
            ada(3)
            norm(5)
            ffn(2)
            for t in range(NT):
                act.wait_ge(s["x_ready"], 5 * NT + t + 1)
                act.dma_start(out[0, t * P:(t + 1) * P, :], x_tok[:, t]).then_inc(s["out_done"], 16)
            act.wait_ge(s["out_done"], 16 * NT)

        @block.vector
        def _(dve):
            v = nc.vector
            step, after = own_order(dve, s["dve_step"])

            def bcast(ap, shape):
                return ap.broadcast_to(shape)

            def norm(i):
                dve.wait_ge(s["norm_rms"], i + 1)
                step(v.reciprocal(stat[:, 8:12], stat[:, 4:8]))
                after()
                for t in range(NT):
                    v.tensor_scalar(XN[i][:, t], x_tok[:, t], stat[:, 8 + t:9 + t], None, ALU.mult).then_inc(s["xn_ready"], 1)
                for kt in range(1, KT, 2):
                    p = filled(dve, ("xT", i, kt))
                    outs = NORM_OUT[i]
                    if i >= 2:
                        dve.wait_ge(s["mod_ready"], MOD_READY[NORM_MOD[i]])
                    for j, (dst, gain, shift) in enumerate(outs):
                        if shift is None:
                            ins = v.tensor_scalar(dst[:, kt], p, gain[:, kt:kt + 1], None, ALU.mult)
                        else:
                            ins = v.tensor_scalar(dst[:, kt], p, gain[:, kt:kt + 1], shift[:, kt:kt + 1], ALU.mult, ALU.add)
                        if j == len(outs) - 1:
                            ins.then_inc(free(("xT", i, kt)), 1)

            def post_norm(stage, i, y, keys):
                for half, t, key in keys:
                    p = filled(dve, key)
                    v.tensor_copy(y[:, t, half * HALF:(half + 1) * HALF], p).then_inc(free(key), 1)
                dve.wait_ge(s["y_rms"], i + 1)
                step(v.reciprocal(stat[:, 24:28], stat[:, 20:24]))
                after()
                dve.wait_ge(s["row_in"], 32)
                for t in range(NT):
                    v.scalar_tensor_tensor(y[:, t], y[:, t], stat[:, 24 + t:25 + t], row[:, i], ALU.mult, ALU.mult)\
                        .then_inc(s["y_scaled"], 1)

            def post_gate(stage, m, y, keys):
                for half, t, key in keys:
                    p = filled(dve, key)
                    evacuated(dve, ("ada", m, 4 + half))
                    v.tensor_tensor(y[:, t, half * HALF:(half + 1) * HALF], p, row[:, m % 2, half * HALF:(half + 1) * HALF],
                                    ALU.mult).then_inc(free(key), 1)

            def in_t(name):
                for kt in range(1, KT, 2):
                    p = filled(dve, (name, "T", kt))
                    v.tensor_copy(h_t[:, kt], p).then_inc(free((name, "T", kt)), 1)

            def ada(m):
                for j in range(4):
                    p = filled(dve, ("ada", m, j))
                    after()
                    step(v.tensor_tensor(junk2[:, :].rearrange("p (k n) -> p k n", k=4), p.rearrange("p (k n) -> p k n", k=4),
                                               bcast(ident.unsqueeze(1), [P, 4, P]), ALU.mult))
                    after()
                    dst = mod[:, m, 1, 4 * j:4 * j + 4] if j < 2 else stat[:, 224 + 4 * (j - 2):228 + 4 * (j - 2)]
                    v.tensor_reduce(dst, junk2[:, :].rearrange("p (k n) -> p k n", k=4), AX, ALU.add).then_inc(free(("ada", m, j)), 1)
                    evacuated(dve, ("ada", m, j))
                v.scalar_tensor_tensor(mod[:, m, 0], stat[:, 224:232], 1.0, MOD_GAIN[m], ALU.add, ALU.mult).then_inc(s["mod_ready"], 1)

            def ffn(i):
                for u in range(FFN_UNITS):
                    for q in range(4):
                        if i:
                            continue
                        n = 22 * (q // 2) + 2 * u + q % 2
                        buf = ftmp[:, u % 2, q]
                        dve.wait_ge(s["conv_pre"], 4 * u + q + 1)
                        p = ps[:, bank_use[("up", i, u, q)][0]]
                        step(v.scalar_tensor_tensor(buf[:, 1:S], p[:, 0:S - 1], vec[:, CONV + 44 + n:CONV + 45 + n],
                                                          buf[:, 1:S], ALU.mult, ALU.add))
                        after()
                        v.scalar_tensor_tensor(buf[:, 2:S], p[:, 0:S - 2], vec[:, CONV + n:CONV + 1 + n],
                                               buf[:, 2:S], ALU.mult, ALU.add).then_inc(free(("up", i, u, q)), 1)
                    for q in range(2):
                        if i == 0:
                            dve.wait_ge(s["hid_gate"], 2 * u + q + 1)
                            evacuated(dve, ("up", i, u, 2 + q))
                            v.tensor_tensor(hid[:, 2 * u + q], ftmp[:, u % 2, q], ftmp[:, u % 2, 2 + q], ALU.mult)\
                                .then_inc(s["hid_done"], 1)
                        else:
                            evacuated(dve, ("up", i, u, q))
                            p = filled(dve, ("up", i, u, 2 + q))
                            v.tensor_tensor(hid[:, 2 * u + q], ftmp[:, u % 2, q], p, ALU.mult).then_inc(free(("up", i, u, 2 + q)), 1)

            def rope(src, t, a, b, heads, read=None):
                cos, sin, nsin = [rope_t[:, i, t] for i in range(3)]
                sv = src.rearrange("p (h q d) -> p h q d", h=heads, q=2)
                av = a.rearrange("p (h q d) -> p h q d", h=heads, q=2)
                bv = b.rearrange("p (h q d) -> p h q d", h=heads, q=2)
                step(v.tensor_tensor(av, sv, bcast(cos.unsqueeze(1).unsqueeze(1), [P, heads, 2, HD // 2]), ALU.mult))
                step(v.tensor_tensor(bv[:, :, 0], sv[:, :, 1], bcast(nsin.unsqueeze(1), [P, heads, HD // 2]), ALU.mult))
                ins = v.tensor_tensor(bv[:, :, 1], sv[:, :, 0], bcast(sin.unsqueeze(1), [P, heads, HD // 2]), ALU.mult)
                if read is None:
                    step(ins)
                else:
                    ins.then_inc(free(read), 1)
                    evacuated(dve, read)
                after()

            def raw_squares(t, h0):
                w = raw[:, t, h0:h0 + 8, :]
                sq = junk[:, 0:HALF].rearrange("p (h d) -> p h d", h=8)
                step(v.tensor_tensor(sq, w, w, ALU.mult))
                after()
                v.tensor_reduce(stat[:, 32 + 24 * t + h0:40 + 24 * t + h0], sq, AX, ALU.add).then_inc(s["raw_done"], 1)
                raw_sums[0] += 1
                dve.wait_ge(s["raw_done"], raw_sums[0])

            raw_sums = [0]

            def attention(name, bias_ready, finish):
                unit_of, n_units, (L, PB, PT), base = ATT[name]
                for i in range(n_units + 3):
                    if i < n_units:
                        u = unit_of(i)
                        bias_ready(i)
                        p = filled(dve, (name, "S", i))
                        if i >= 2:
                            dve.wait_ge(s["p_ready"], base + i - 1)
                        v.tensor_tensor_reduce(L[:, i % 2, 0:u["n"]], p[:, 0:u["n"]], u["bias"], -SCALE, 3e38,
                                               ALU.add, ALU.min, neg_max[:, i % 4:i % 4 + 1]).then_inc(free((name, "S", i)), 1)
                    if 1 <= i <= n_units and (i - 1) % 2 == 1:
                        j = i - 1
                        if j >= 2:
                            dve.wait_ge(s["pv_done"], base + j - 1)
                        n = unit_of(j)["n"]
                        pt = filled(dve, (name, "T", j))
                        v.tensor_copy(PT[:, j % 2, 0:n], pt[:, 0:n]).then_inc(free((name, "T", j)), 1)
                    if i >= 3 and (i - 3) % 8 == 7:
                        finish((i - 3) // 8, base)

            v.memset(eps[:, :], EPS).then_inc(s["e_done"], 1)
            p = filled(dve, "vec")
            v.tensor_copy(vec[:, :], p[:, 0:304]).then_inc(free("vec"), 1)
            dve.wait_ge(s["consts_in"], 32)
            step(v.tensor_copy(masks[:, :, :], mask_rows))
            dve.wait_ge(s["c_act_done"], 1)
            v.tensor_copy(c_rep[:, :, :], bcast(c_act[:, :].unsqueeze(2), [P, KT, P])).then_inc(s["c_rep_done"], 1)
            norm(0)
            n = 0
            for name in ROPED:
                for t in range(NT):
                    p = filled(dve, (name, t))
                    if n >= 2:
                        pn, pt = ROPED[(n - 2) // NT], (n - 2) % NT
                        filled(dve, (pn, "T", pt))
                    a, b, o = rope_a[:, n % 2], rope_b[:, n % 2], rope_o[:, n % 2]
                    if name == "kk":
                        step(v.tensor_copy(av_tok[:, t], p[:, 64:128]))
                        step(v.tensor_scalar(iw[:, t], p[:, 192:200], (RH * HD) ** -0.5, None, ALU.mult))
                        for j, c in enumerate((0, 128)):
                            rope(p[:, c:c + 64], t, a[:, 64 * j:64 * j + 64], b[:, 64 * j:64 * j + 64], 1, (name, t) if j else None)
                        av = a[:, 0:128].rearrange("p (j d) -> p j d", j=2).unsqueeze(2)
                        bv = b[:, 0:128].rearrange("p (j d) -> p j d", j=2).unsqueeze(2)
                        v.tensor_tensor(o[:, 0:256].rearrange("p (j q d) -> p j q d", j=2, q=2), bcast(av, [P, 2, 2, HD]),
                                        bcast(bv, [P, 2, 2, HD]), ALU.add).then_inc(s["rope_done"], 1)
                    else:
                        rope(p, t, a, b, 8, (name, t))
                        v.tensor_tensor(o, a, b, ALU.add).then_inc(s["rope_done"], 1)
                    n += 1
            i = 0
            for t in range(1, NT):
                n = (t + 1) * P
                w = isc[:, t - 1, 0:n]
                for h in range(RH):
                    evacuated(dve, ("index", t, h))
                    if h:
                        dve.wait_ge(s["rel_used"], i)
                        v.scalar_tensor_tensor(w, rel[:, i % 2, 0:n], iw[:, t, h:h + 1], w, ALU.mult, ALU.add).then_inc(s["rel_used"], 1)
                    else:
                        v.tensor_scalar(w, rel[:, i % 2, 0:n], iw[:, t, h:h + 1], None, ALU.mult).then_inc(s["rel_used"], 1)
                    i += 1
                dve.wait_ge(s["rel_used"], i)
                step(v.tensor_tensor(w[:, t * P:n], w[:, t * P:n], strip[:, 3 * P:], ALU.add))
                after()
            for t in range(1, NT):
                n = (t + 1) * P
                w = isc[:, t - 1, 0:n]
                for r in range(TOPK // 8):
                    step(v.max(best[:, :], w))
                    after()
                    step(v.match_replace(w, best[:, :], w, REPLACED))
                    after()
                v.tensor_scalar(sel_bias[:, t - 1, 0:n], w, REPLACED / 2, NEG, ALU.is_ge, ALU.mult).then_inc(s["picked"], 1)
            for t in range(NT):
                dve.wait_ge(s["ret_square"], t + 1)
                v.tensor_reduce(stat[:, 32 + 8 * t:40 + 8 * t], junk[:, 0:512].rearrange("p (h d) -> p h d", h=RH), AX, ALU.add)\
                    .then_inc(s["ret_rms"], 1)
            dve.wait_ge(s["ret_square"], NT + 1)
            step(v.reciprocal(stat[:, 96:128], stat[:, 64:96]))
            after()
            for t in range(NT):
                p = filled(dve, ("ret_o", t))
                v.tensor_tensor(mixed[:, t, 0:512].rearrange("p (h d) -> p h d", h=RH), p.rearrange("p (h d) -> p h d", h=RH),
                                bcast(stat[:, 96 + 8 * t:104 + 8 * t].unsqueeze(2), [P, RH, HD]), ALU.mult)\
                    .then_inc(free(("ret_o", t)), 1)

            def dsa_bias(i):
                if i % RH == 0 and i // RH >= 1:
                    dve.wait_ge(s["picked"], i // RH)

            def dsa_finish(g, base):
                dve.wait_ge(s["p_ready"], base + 8 * (g + 1))
                dve.wait_ge(s["pv_done"], base + 8 * (g + 1))
                step(v.reciprocal(rden[:, g % 2], den[:, g % 2]))
                after()
                p = ps[:, bank_use[("dsa", "O", g)][0]]
                v.tensor_tensor(mixed[:, g, 512:1024].rearrange("p (h d) -> p h d", h=RH), p.rearrange("p (h d) -> p h d", h=RH),
                                bcast(rden[:, g % 2].unsqueeze(2), [P, RH, HD]), ALU.mult).then_inc(free(("dsa", "O", g)), 1)

            attention("dsa", dsa_bias, dsa_finish)
            in_t("mix1")
            post_norm(0, 0, y1, tok_keys("mix1"))
            norm(1)
            ffn(0)
            post_norm(1, 1, yf, down_keys(0))
            ada(0)
            norm(2)
            for u in range(2):
                for j in range(4):
                    fl = f_work[2][:, j * S:(j + 1) * S]
                    dve.wait_ge(s["f_abs"], u + 1)
                    p = filled(dve, ("hf", u, j))
                    h = 4 * u + j
                    v.scalar_tensor_tensor(HG[:, h], p, 0.0, fl, ALU.min, ALU.subtract).then_inc(s["logf_done"], 1)
                    dve.wait_ge(s["logf_done"], h + 1)
                    v.tensor_tensor(HK[:, h], HG[:, h], p, ALU.subtract).then_inc(free(("hf", u, j)), 1)
            for h in range(HH):
                v.tensor_tensor_scan(HG[:, h], keep, HG[:, h], 0.0, ALU.mult, ALU.add).then_inc(s["g_done"], 1)

            def attn_diag(h, lv):
                p = filled(dve, ("diag", h, lv))
                if h >= 2 and lv == 0:
                    filled(dve, ("ho", h - 2))
                A = attn[:, h % 2].rearrange("p s n -> p (s n)")
                dst = bass.AP(A.tensor, A.offset, [A.ap[0], [S + P, NT], [1, P]])
                m = bcast(masks[:, lv, :].unsqueeze(1), [P, NT, P])
                evacuated_prev(h, lv)
                v.copy_predicated(dst, m, p.rearrange("p (s n) -> p s n", s=NT)).then_inc(free(("diag", h, lv)), 1)

            def evacuated_prev(h, lv):
                if lv:
                    evacuated(dve, ("diag", h, lv - 1))

            for h in range(HH + 1):
                if h < HH:
                    dve.wait_ge(s["g_done"], h + 1)
                    G = HG[:, h].rearrange("p (t n) -> p t n", t=NT)
                    if h:
                        dve.wait_ge(s["eq_done"], 7 * h)
                    v.tensor_tensor(tot[:, 0:1], G[:, 0, P - 1:P], G[:, 1, P - 1:P], ALU.add).then_inc(s["tabs_done"], 1)
                    dve.wait_ge(s["d_exp"], h + 1)
                    dve.wait_ge(s["k_done"], 2)
                    L = lvl[h % 2]
                    for lv in range(LEVELS):
                        c = 1 << lv
                        for q, src in ((0, HK), (1, HQ)):
                            d = L[:, lv].rearrange("p (b q c) -> p b q c", q=2, c=c)[:, :, q]
                            w = src[:, h].rearrange("p (b q c) -> p b q c", q=2, c=c)[:, :, q]
                            v.tensor_tensor(d, d, w, ALU.mult).then_inc(s["qk_done"], 1)
                    dve.wait_ge(s["eq_done"], 7 * (h + 1))
                    K = HK[:, h].rearrange("p (t n) -> p t n", t=NT)
                    Q = HQ[:, h].rearrange("p (t n) -> p t n", t=NT)
                    v.tensor_tensor(q1[:, 0:2], q1[:, 0:2], Q[:, 1:3], ALU.mult).then_inc(s["q1_done"], 1)
                    v.tensor_tensor(q1[:, 2:4], q1[:, 2:4], bcast(Q[:, 3:4], [P, 2, P]), ALU.mult).then_inc(s["q1_done"], 1)
                    v.tensor_tensor(k1[:, 0:3], k1[:, 0:3], K[:, 0:3], ALU.mult).then_inc(s["q1_done"], 1)
                    v.tensor_tensor(k1[:, 3], k1[:, 3], K[:, 0], ALU.mult).then_inc(s["q1_done"], 1)
                    dve.wait_ge(s["attn_zero"], 1)
                    for lv in range(LEVELS + 1):
                        attn_diag(h, lv)
                if h >= 1:
                    p = filled(dve, ("ho", h - 1))
                    v.tensor_copy(v_tok[:, :, (h - 1) * P:h * P], p.rearrange("p (t n) -> p t n", t=NT)).then_inc(free(("ho", h - 1)), 1)
            dve.wait_ge(s["ho_rms"], 1)
            step(v.reciprocal(stat[:, 160:192], stat[:, 128:160]))
            after()
            dve.wait_ge(s["sg_done"], 8)
            for t in range(NT):
                w = v_tok[:, t].rearrange("p (h d) -> p h d", h=HH)
                v.tensor_tensor(w, w, bcast(stat[:, 160 + 8 * t:168 + 8 * t].unsqueeze(2), [P, HH, P]), ALU.mult).then_inc(s["ho_scaled"], 1)
            in_t("mix2")
            post_gate(2, 0, y2, tok_keys("mix2"))
            ada(1)
            norm(3)
            ffn(1)
            post_gate(3, 1, yf, down_keys(1))
            ada(2)
            ada(4)
            norm(4)
            for j in range(4):
                p = filled(dve, ("kvc", j))
                src = bass.AP(p.tensor, p.offset, [p.ap[0], [16, NCMP], [1, 32]])
                pos = vec[:, POS + 32 * (j // 2):POS + 32 * (j // 2) + 32]
                v.tensor_tensor(win[:, j], src, bcast(pos.unsqueeze(1), [P, NCMP, 32]), ALU.add).then_inc(free(("kvc", j)), 1)
            for u in range(2):
                for t in range(NT):
                    evacuated(dve, ("kvs", u, t))
                    if u == 1:
                        raw_squares(t, 16)
            for u in range(2):
                for t in range(NT):
                    evacuated(dve, ("nq", u, t))
                    raw_squares(t, 8 * u)
            for t in range(NT):
                evacuated(dve, ("nq", 2, t))
            step(v.tensor_scalar(gates_e[:, :, :], gates_e[:, :, :], 1.0, None, ALU.add))
            after()
            step(v.reciprocal(gates[:, :, :], gates_e[:, :, :]))
            dve.wait_ge(s["raw_rms"], 1)
            step(v.reciprocal(stat[:, 32:128], stat[:, 128:224]))
            after()
            p = filled(dve, "cmp2")
            step(v.tensor_copy(kc_raw, p[0:NCMP, 0:256]))
            v.tensor_copy(vc_tok[0:NCMP, :, :], p[0:NCMP, 256:512].rearrange("p (h d) -> p h d", h=4)).then_inc(free("cmp2"), 1)
            after()
            step(v.tensor_tensor(kc_tok, kc_raw.rearrange("p (h d) -> p h d", h=4), kc_raw.rearrange("p (h d) -> p h d", h=4), ALU.mult))
            after()
            v.tensor_reduce(stat[0:NCMP, 244:248], kc_tok, AX, ALU.add).then_inc(s["cmp_sq"], 1)
            dve.wait_ge(s["cmp_rms"], 1)
            step(v.reciprocal(stat[0:NCMP, 252:256], stat[0:NCMP, 248:252]))
            after()
            step(v.tensor_tensor(kc_tok, kc_raw.rearrange("p (h d) -> p h d", h=4),
                                       bcast(stat[0:NCMP, 252:256].unsqueeze(2), [NCMP, 4, HD]), ALU.mult))
            after()
            dve.wait_ge(s["cmp_pos_in"], 64)
            v.tensor_tensor(kc_tok, kc_tok, bcast(cmp_norm[0:NCMP, :].unsqueeze(1), [NCMP, 4, HD]), ALU.mult).then_inc(s["cmp_tok"], 1)
            p = filled(dve, "cmpT")
            v.tensor_copy(kc_t[:, :, 0:NCMP], p[:, 0:64].rearrange("p (c i) -> p c i", c=2)[:, :, 0:NCMP]).then_inc(free("cmpT"), 1)
            for t in range(NT):
                for j in range(3):
                    i = 3 * t + j
                    if i >= 2:
                        filled(dve, ("nT", (i - 2) // 3, 2 + (i - 2) % 3))
                    a = n_a[:, i % 2]
                    if j < 2:
                        for ko in range(2):
                            src = raw[:, t, 8 * j + 4 * ko:8 * j + 4 * ko + 4, :]
                            dst = a.rearrange("p (g q d) -> p g q d", g=4, q=2)[:, :, ko]
                            r = stat[:, 32 + 24 * t + 8 * j + 4 * ko:36 + 24 * t + 8 * j + 4 * ko]
                            ins = v.tensor_tensor(dst, src, bcast(r.unsqueeze(2), [P, 4, HD]), ALU.mult)
                            if ko == 0:
                                step(ins)
                        after()
                        ins.then_inc(s["raw_norm"], 1)
                    else:
                        r = stat[:, 48 + 24 * t:56 + 24 * t]
                        v.tensor_tensor(a.rearrange("p (h d) -> p h d", h=8), raw[:, t, 16:24, :], bcast(r.unsqueeze(2), [P, 8, HD]),
                                        ALU.mult).then_inc(s["raw_norm"], 1)
                    dve.wait_ge(s["gained"], i + 1)
                    rope(a, t, n_b[:, i % 2], n_o[:, i % 2], 8)
                    v.tensor_tensor(n_o[:, i % 2], n_b[:, i % 2], n_o[:, i % 2], ALU.add).then_inc(s["rope2_done"], 1)
                for j in (1, 3):
                    p = filled(dve, ("nT", t, j))
                    dst = [qn_t[:, 0:4], qn_t[:, 4:8], qr_t[:, 0:4], qr_t[:, 4:8], k_t][j]
                    v.tensor_copy(dst[:, :, t * P:(t + 1) * P], p.rearrange("p (k n) -> p k n", k=4)).then_inc(free(("nT", t, j)), 1)
            for i in range(len(GROUPS) + 2):
                if i < len(GROUPS):
                    t, kp = GROUPS[i]
                    L = cl[:, i % 2]
                    if i >= 2:
                        dve.wait_ge(s["cmp_p"], i - 1)
                    for q in range(2):
                        p = filled(dve, ("cS", i, q))
                        v.tensor_tensor(L[:, 4 * q:4 * q + 4], p[:, 0:128].rearrange("p (g c) -> p g c", g=4)[:, :, 0:NCMP],
                                        bcast(cmp_bias[:, t].unsqueeze(1), [P, 4, NCMP]), ALU.add).then_inc(free(("cS", i, q)), 1)
                    for q in range(2):
                        evacuated(dve, ("cS", i, q))
                    step(v.tensor_reduce(fac[:, 32:40], L, AX, ALU.max))
                    after()
                    v.tensor_tensor(L, L, bcast(fac[:, 32:40].unsqueeze(2), [P, 8, NCMP]), ALU.subtract).then_inc(s["cmp_l"], 1)
                if 1 <= i <= len(GROUPS):
                    t, kp = GROUPS[i - 1]
                    f = fac[:, 48 + 8 * ((i - 1) % 2):56 + 8 * ((i - 1) % 2)]
                    dve.wait_ge(s["cmp_p"], i)
                    step(v.tensor_reduce(fac[:, 40:48], cp[:, (i - 1) % 2], AX, ALU.add))
                    after()
                    step(v.reciprocal(fac[:, 40:48], fac[:, 40:48]))
                    after()
                    step(v.scalar_tensor_tensor(f, fac[:, 40:48], row_valid[:, t:t + 1], gates[:, t, 8 * kp:8 * kp + 8],
                                                      ALU.mult, ALU.mult))
                if i >= 2:
                    t, kp = GROUPS[i - 2]
                    f = fac[:, 48 + 8 * (i % 2):56 + 8 * (i % 2)]
                    p = filled(dve, ("cO", i - 2))
                    after()
                    v.tensor_tensor(nsa_tok[:, t, kp * 512:(kp + 1) * 512].rearrange("p (h d) -> p h d", h=8),
                                    p.rearrange("p (h d) -> p h d", h=8), bcast(f.unsqueeze(2), [P, 8, HD]), ALU.mult)\
                        .then_inc(free(("cO", i - 2)), 1)
            evacuated(dve, ("cO", len(GROUPS) - 1))
            evacuated(dve, ("cO", len(GROUPS) - 2))

            def nsa_finish(g, base):
                t, kp, br = NSA_GROUPS[g]
                dve.wait_ge(s["p_ready"], base + 8 * (g + 1))
                dve.wait_ge(s["pv_done"], base + 8 * (g + 1))
                step(v.reciprocal(rden[:, g % 2], den[:, g % 2]))
                after()
                step(v.tensor_tensor(rden[:, g % 2], rden[:, g % 2], gates[:, t, 16 + 16 * br + 8 * kp:24 + 16 * br + 8 * kp], ALU.mult))
                after()
                if g >= 2:
                    dve.wait_ge(s["nsa_added"], g - 1)
                p = ps[:, bank_use[("nsa", "O", g)][0]]
                v.tensor_tensor(n_tmp[:, g % 2].rearrange("p (h d) -> p h d", h=8), p.rearrange("p (h d) -> p h d", h=8),
                                bcast(rden[:, g % 2].unsqueeze(2), [P, 8, HD]), ALU.mult).then_inc(free(("nsa", "O", g)), 1)

            attention("nsa", lambda i: None, nsa_finish)
            in_t("mix3")
            post_gate(4, 2, y3, tok_keys("mix3"))
            ada(3)
            norm(5)
            ffn(2)
            post_gate(5, 3, yf, down_keys(2))

        @block.tensor
        def _(pe):
            mm = nc.tensor.matmul
            tr = nc.tensor.transpose

            pe.wait_ge(s["consts_in"], 32)
            pe.wait_ge(s["rows_in"], ROWS_IN)
            b = open_bank("vec")
            tr(b[:, 0:64], vec_rows, ident[0:64, 0:64])
            tr(b[:, 64:152], conv_rows[0], ident[0:88, 0:88])
            tr(b[:, 152:240], conv_rows[1], ident[0:88, 0:88])
            tr(b[:, 240:272], pos_rows[:, 0:128], ident[0:32, 0:32])
            tr(b[:, 272:304], pos_rows[:, 128:256], ident[0:32, 0:32]).then_inc(full("vec"), 1)

            def turn(src, key):
                b = open_bank(key)
                for t in range(NT):
                    ins = tr(b[:, t * P:(t + 1) * P], src(t), ident)
                ins.then_inc(full(key), 1)

            def norm(i):
                pe.wait_ge(s["xn_ready"], NT * (i + 1))
                for kt in range(KT):
                    turn(lambda t: XN[i][:, t, kt * P:(kt + 1) * P], ("xT", i, kt))
                for kt in range(KT):
                    evacuated(pe, ("xT", i, kt))

            def tok_bank(w, h, t, key, n):
                b = open_bank(key)
                for k in range(KT):
                    ins = mm(b[:, 0:n], h[:, k, t * P:(t + 1) * P], w[:, k, :], start=(k == 0), stop=(k == KT - 1))
                ins.then_inc(full(key), 1)

            def tok_gemm(name, h, n_units, width=lambda u: 512):
                for u in range(n_units):
                    n = width(u)
                    w = arrived(pe, (name, u))[:, 0:KT * n].rearrange("p (k n) -> p k n", k=KT)
                    for t in range(NT):
                        tok_bank(w, h, t, (name, u, t), n)

            def feat_gemm(ukey, h, keys):
                w = arrived(pe, ukey)[:, 0:KT * 512].rearrange("p (k n) -> p k n", k=KT)
                for j, key in enumerate(keys):
                    b = open_bank(key)
                    for k in range(KT):
                        ins = mm(b, w[:, k, j * P:(j + 1) * P], h[:, k, :], start=(k == 0), stop=(k == KT - 1))
                    ins.then_inc(full(key), 1)

            def ffn(i):
                for u in range(FFN_UNITS):
                    feat_gemm(("up", i, u), h_t, [("up", i, u, j) for j in range(4)])
                bs = [open_bank(("down", i, j)) for j in range(8)]
                for g, (k0, n) in enumerate(down_groups):
                    w = arrived(pe, ("down", i, g))[:, 0:n * D].rearrange("p (k n) -> p k n", k=n)
                    if i == 0:
                        pe.wait_ge(s["hid_done"], k0 + n)
                    else:
                        for k in range(k0, k0 + n):
                            evacuated(pe, ("up", i, k // 2, 2 + k % 2))
                    last = g == len(down_groups) - 1
                    for t in range(NT):
                        for half in range(2):
                            for k in range(n):
                                ins = mm(bs[2 * t + half], hid[:, k0 + k, t * P:(t + 1) * P], w[:, k, half * HALF:(half + 1) * HALF],
                                         start=(k0 + k == 0), stop=(k0 + k == FT - 1))
                            if last:
                                ins.then_inc(full(("down", i, 2 * t + half)), 1)
                    if not last:
                        ins.then_inc(s["down_step"], 1)

            def ada(m):
                pe.wait_ge(s["c_rep_done"], 1)
                pe.wait_ge(s["ones_done"], 1)
                n = ada_cols(m)
                bs = [open_bank(("ada", m, j)) for j in range(n)]
                for k in range(KT):
                    w = arrived(pe, ("ada", m, k))
                    for j in range(n):
                        ins = mm(bs[j], c_rep[:, k, :], w[:, j * HALF:(j + 1) * HALF], start=(k == 0), stop=(k == KT - 1))
                        if k == KT - 1:
                            ins.then_inc(full(("ada", m, j)), 1)
                    if 2 * k < n:
                        for j in range(2):
                            ins = mm(bs[2 * k + j], ones[:, :], w[0:1, 3072 + j * HALF:3072 + (j + 1) * HALF], start=False, stop=False)
                    if k < KT - 1:
                        ins.then_inc(s["ada_step"], 1)

            def attention(name, ready):
                unit_of, n_units, (L, PB, PT), base = ATT[name]
                for i in range(n_units + 2):
                    if i < n_units:
                        u = unit_of(i)
                        b = open_bank((name, "S", i))
                        mm(b[:, 0:u["n"]], u["q"], u["k"], start=True, stop=True).then_inc(full((name, "S", i)), 1)
                    if 1 <= i <= n_units:
                        u = unit_of(i - 1)
                        pe.wait_ge(s["p_ready"], base + i)
                        b = open_bank((name, "T", i - 1))
                        for c in range(u["n"] // P):
                            ins = tr(b[:, c * P:(c + 1) * P], PB[:, (i - 1) % 2, c * P:(c + 1) * P], ident)
                        ins.then_inc(full((name, "T", i - 1)), 1)
                    if i >= 2:
                        j = i - 2
                        u = unit_of(j)
                        okey = (name, "O", j // 8)
                        b = open_bank(okey) if j % 8 == 0 else ps[:, bank_use[okey][0]]
                        evacuated(pe, (name, "T", j))
                        nb = u["n"] // P
                        for c in range(nb):
                            ins = mm(b[:, u["slot"] * HD:(u["slot"] + 1) * HD], PT[:, j % 2, c * P:(c + 1) * P], u["v"](c),
                                     start=(c == 0), stop=(c == nb - 1))
                        ins.then_inc(s["pv_done"], 1)

            def out_gemm(name, src, wait):
                wait()
                for kt in range(KT):
                    turn(lambda t: src[:, t, kt * P:(kt + 1) * P], (name, "T", kt))
                for kt in range(KT):
                    evacuated(pe, (name, "T", kt))
                tok_gemm(name, h_t, 2)

            norm(0)
            lagged = []
            n_roped = 0
            for name in P1_ORDER:
                n = sum(c for _, c in P1[name])
                w = arrived(pe, name)[:, 0:KT * n].rearrange("p (k n) -> p k n", k=KT)
                for t in range(NT):
                    tok_bank(w, h_t, t, (name, t), n)
                    if lagged:
                        ln, lt = lagged.pop(0)
                        i = n_roped
                        n_roped += 1
                        pe.wait_ge(s["rope_done"], i + 1)
                        b = open_bank((ln, "T", lt))
                        nb = 2 if ln == "kk" else 4
                        for c in range(nb):
                            ins = tr(b[:, c * P:(c + 1) * P], rope_o[:, i % 2, c * P:(c + 1) * P], ident)
                        ins.then_inc(full((ln, "T", lt)), 1)
                    if name in ROPED:
                        lagged.append((name, t))
            for t in range(1, NT):
                for h in range(RH):
                    q = slice(64 * (h % 2), 64 * (h % 2) + 64)
                    if h == 0 and t == 1:
                        for nm in ("iq", "kk"):
                            for tt in range(NT):
                                evacuated(pe, (nm, "T", tt))
                    b = open_bank(("index", t, h))
                    mm(b[:, 0:(t + 1) * P], T1["iq"][q, h // 2, t * P:(t + 1) * P], T1["kk"][q, 1, 0:(t + 1) * P],
                       start=True, stop=True).then_inc(full(("index", t, h)), 1)
            for nm in ("rk", "rq", "aq"):
                for tt in range(NT):
                    evacuated(pe, (nm, "T", tt))
            for tt in range(NT):
                evacuated(pe, ("rv", tt))
            for h in range(RH + 1):
                if h < RH:
                    q = slice(64 * (h % 2), 64 * (h % 2) + 64)
                    for m in range(NT):
                        b = open_bank(("ret_s", h, m))
                        mm(b[:, 0:S - m * P], T1["rk"][q, h // 2, m * P:(m + 1) * P], T1["rq"][q, h // 2, m * P:S],
                           start=True, stop=True).then_inc(full(("ret_s", h, m)), 1)
                if h >= 1:
                    g = h - 1
                    if h == 1:
                        obs = [open_bank(("ret_o", t)) for t in range(NT)]
                    pe.wait_ge(s["decayed"], h)
                    for t in range(NT):
                        for m in range(t + 1):
                            o = [0, 512, 896, 1152][m] + (t - m) * P
                            ins = mm(obs[t][:, g * HD:(g + 1) * HD], sT[:, g % 2, o:o + P], rv_tok[:, m, g * HD:(g + 1) * HD],
                                     start=(m == 0), stop=(m == t))
                        if h == RH:
                            ins.then_inc(full(("ret_o", t)), 1)
                    if h < RH:
                        ins.then_inc(s["ret_pv"], 1)
            attention("dsa", None)

            def wait_mix1():
                pe.wait_ge(s["mixed_ready"], NT)
                for g in range(NT):
                    evacuated(pe, ("dsa", "O", g))

            out_gemm("mix1", mixed, wait_mix1)
            norm(1)
            ffn(0)
            ada(0)
            norm(2)
            for u in range(2):
                feat_gemm(("hq", u), h_t, [("hq", u, j) for j in range(4)])
            tok_gemm("hg", h_t, 2)
            for u in range(2):
                feat_gemm(("hf", u), h_t, [("hf", u, j) for j in range(4)])
            tok_gemm("hi", h_t, 2)
            for u in range(2):
                for t in range(NT):
                    evacuated(pe, ("hi", u, t))
            for h in range(HH + 1):
                if h < HH:
                    L = lvl[h % 2]
                    for lv in range(LEVELS + 1):
                        b = open_bank(("diag", h, lv))
                        if lv:
                            pe.wait_ge(s["qk_done"], 2 * (LEVELS * h + lv))
                        else:
                            pe.wait_ge(s["k_done"], 2)
                        for t in range(NT):
                            c = slice(t * P, (t + 1) * P)
                            k, q = (HK[:, h, c], HQ[:, h, c]) if lv == 0 else (L[:, lv - 1, c], L[:, lv - 1, c])
                            ins = mm(b[:, c], k, q, start=True, stop=True)
                        ins.then_inc(full(("diag", h, lv)), 1)
                    pe.wait_ge(s["q1_done"], 4 * (h + 1))
                    b = open_bank(("far", h, 0))
                    mm(b[:, 0:P], k1[:, 0], q1[:, 0], start=True, stop=True)
                    mm(b[:, P:3 * P], k1[:, 3], q1[:, 1:3].rearrange("p s n -> p (s n)"), start=True, stop=True).then_inc(full(("far", h, 0)), 1)
                    b = open_bank(("far", h, 1))
                    mm(b[:, 0:2 * P], k1[:, 1], q1[:, 1:3].rearrange("p s n -> p (s n)"), start=True, stop=True)
                    mm(b[:, 2 * P:3 * P], k1[:, 2], q1[:, 3], start=True, stop=True).then_inc(full(("far", h, 1)), 1)
                if h >= 1:
                    g = h - 1
                    b = open_bank(("ho", g))
                    evacuated(pe, ("diag", g, LEVELS))
                    evacuated(pe, ("far", g, 0))
                    evacuated(pe, ("far", g, 1))
                    for t in range(NT):
                        for m in range(t + 1):
                            ins = mm(b[:, t * P:(t + 1) * P], attn[:, g % 2, m, t * P:(t + 1) * P], v_tok[:, m, g * P:(g + 1) * P],
                                     start=(m == 0), stop=(m == t))
                    ins.then_inc(full(("ho", g)), 1)
            out_gemm("mix2", v_tok, lambda: pe.wait_ge(s["ho_ready"], NT))
            ada(1)
            norm(3)
            ffn(1)
            ada(2)
            ada(4)
            norm(4)
            feat_gemm("kvc", hkv_t, [("kvc", j) for j in range(4)])
            tok_gemm("kvs", hkv_t, 2)
            tok_gemm("nq", h_t, 3, lambda u: 512 if u < 2 else 48)
            for j in range(4):
                evacuated(pe, ("kvc", j))
            for kv in range(2):
                bs = [open_bank(("cmp1", kv, j)) for j in range(4)]
                for rh in range(2):
                    w = arrived(pe, ("cmp1", kv, rh)).rearrange("p (r n) -> p r n", r=16)
                    for n in range(2):
                        for r in range(16):
                            for q in range(2):
                                d = slice(64 * q, 64 * q + 64)
                                ins = mm(bs[2 * n + q][:, 0:62].rearrange("p (c i) -> p c i", c=2), w[d, r, n * P:(n + 1) * P],
                                         win[d, 2 * kv:2 * kv + 2, :, 16 * rh + r],
                                         start=(rh == 0 and r == 0), stop=(rh == 1 and r == 15))
                                if rh == 1 and r == 15:
                                    ins.then_inc(full(("cmp1", kv, 2 * n + q)), 1)
                    if rh == 0:
                        ins.then_inc(s["vpart"], 1)
            for kv in range(2):
                for j in range(4):
                    evacuated(pe, ("cmp1", kv, j))
            pe.wait_ge(s["w2_in"], 32)
            b = open_bank("cmp2")
            for kv in range(2):
                for kh in range(NSA_KV):
                    c, q = kh // 2, kh % 2
                    for n in range(2):
                        ins = mm(b[0:NCMP, kv * 256 + kh * HD:kv * 256 + (kh + 1) * HD], h1[:, kv, n, q, c], w2_sb[:, kv, n, :],
                                 start=(n == 0), stop=(n == 1))
            ins.then_inc(full("cmp2"), 1)
            pe.wait_ge(s["cmp_tok"], 1)
            b = open_bank("cmpT")
            for c in range(2):
                ins = tr(b[:, 32 * c:32 * c + NCMP], kc_tok[:, 2 * c:2 * c + 2, :].rearrange("p h d -> p (h d)"), ident[0:NCMP, 0:NCMP])
            ins.then_inc(full("cmpT"), 1)
            for t in range(NT):
                for j in range(3):
                    i = 3 * t + j
                    if j < 2:
                        pe.wait_ge(s["gained"], i + 1)
                        b = open_bank(("nT", t, j))
                        for c in range(4):
                            ins = tr(b[:, c * P:(c + 1) * P], n_a[:, i % 2, c * P:(c + 1) * P], ident)
                        ins.then_inc(full(("nT", t, j)), 1)
                    pe.wait_ge(s["rope2_done"], i + 1)
                    key = ("nT", t, 2 + j)
                    b = open_bank(key)
                    for c in range(4):
                        ins = tr(b[:, c * P:(c + 1) * P], n_o[:, i % 2, c * P:(c + 1) * P], ident)
                    ins.then_inc(full(key), 1)
            for t in range(NT):
                for j in range(5):
                    evacuated(pe, ("nT", t, j))
            evacuated(pe, "cmpT")
            for i in range(len(GROUPS) + 2):
                if i < len(GROUPS):
                    t, kp = GROUPS[i]
                    bq = [open_bank(("cS", i, q)) for q in range(2)]
                    for g in range(4):
                        for q in range(2):
                            d = slice(64 * q, 64 * q + 64)
                            ins = mm(bq[q][:, 32 * g:32 * g + NCMP], qn_t[d, kp * 4 + g, t * P:(t + 1) * P], kc_t[d, kp, 0:NCMP],
                                     start=True, stop=True)
                            if g == 3:
                                ins.then_inc(full(("cS", i, q)), 1)
                if 1 <= i <= len(GROUPS):
                    pe.wait_ge(s["cmp_p"], i)
                    for q in range(2):
                        b = open_bank(("cT", i - 1, q))
                        for g in range(4):
                            ins = tr(b[0:NCMP, g * P:(g + 1) * P], cp[:, (i - 1) % 2, 4 * q + g, :], ident)
                        ins.then_inc(full(("cT", i - 1, q)), 1)
                if i >= 2:
                    t, kp = GROUPS[i - 2]
                    for q in range(2):
                        evacuated(pe, ("cT", i - 2, q))
                    b = open_bank(("cO", i - 2))
                    for hh in range(8):
                        ins = mm(b[:, hh * HD:(hh + 1) * HD], cpt[:, i % 2, hh, :], vc_tok[0:NCMP, 2 * kp + hh // 4, :],
                                 start=True, stop=True)
                    ins.then_inc(full(("cO", i - 2)), 1)
            attention("nsa", None)
            out_gemm("mix3", nsa_tok, lambda: pe.wait_ge(s["nsa_added"], len(NSA_GROUPS)))
            ada(3)
            norm(5)
            ffn(2)


_INS = """x mix_norm_pre mix_norm_post w_in w_out ffn_norm_pre ffn_norm_post w_up conv_w conv_b w_down c_2 ada_w_2 ada_b_2
norm_mix_2 norm_ffn_2 hgrn_w_in_2 hgrn_out_norm_2 hgrn_w_out_2 kv_ada_w_2 kv_ada_b_2 kv_norm_2 nsa_w_kv_2
nsa_k_norm_2 cmp_pos_2 cmp_w1_2 cmp_w2_2 nsa_w_q_2 nsa_q_norm_2 nsa_w_out_2 ffn_w_in_2 ffn_w_out_2""".split()


def kernel(**inputs):
    import concourse.bacc as _bacc
    from concourse.bass_utils import run_bass_kernel_spmd as _run

    nc = _bacc.Bacc("TRN2", target_bir_lowering=False, num_devices=1)
    arrays, io = {}, {}
    given = {n: np.ascontiguousarray(inputs[n]) for n in _INS}
    given.update(shape_constants())
    for name, a in given.items():
        arrays[f"in_{name}"] = a
        io[name] = nc.dram_tensor(f"in_{name}", a.shape, mybir.dt.from_np(a.dtype), kind="ExternalInput").ap()
    out = nc.dram_tensor("out_0", (1, S, D), F32, kind="ExternalOutput").ap()
    build(nc, io, out)
    r = _run(nc, [arrays], core_ids=[0])
    return r.results[0]["out_0"]
```

```python
from contextlib import ExitStack

import numpy as np

import concourse.bass as bass
from concourse import mybir

F32 = mybir.dt.float32
F32R = mybir.dt.float32r
I8 = mybir.dt.int8
ALU = mybir.AluOpType
ACT = mybir.ActivationFunctionType
AX = mybir.AxisListType.X

P = 128
S = 512
NT = S // P
D = 1024
KT = D // P
HD = 64
RH = 8
TOPK = 128
DFF = 2816
FT = DFF // P
EPS = 1e-6
NEG = -1e30
REPLACED = -3e38
SCALE = HD ** -0.5
HH = 8
LEVELS = 7
NSA_H, NSA_KV, GROUP = 16, 4, 4
NCMP = 31
RING = 2
SLOT = 4096
FFN_UNITS = FT // 2
HALF = 512
MAP = 16512
PIECE = 1024

ROWS_IN = 16 * 16
VEC_ROWS = [("mix_norm_pre", 8), ("ffn_norm_pre", 8), ("norm_mix_2", 16), ("norm_ffn_2", 16), ("kv_norm_2", 8), ("c_2", 8)]


def shape_constants():
    f = np.float32
    inv = (f(10000.0) ** (-np.arange(0, HD, 2, dtype=f) / f(HD))).astype(f)
    ang = np.arange(S, dtype=f)[:, None] * inv[None, :]
    tok = lambda a: np.ascontiguousarray(a.reshape(NT, P, -1).transpose(1, 0, 2))
    rope = np.stack([tok(np.cos(ang)), tok(np.sin(ang)), tok(-np.sin(ang))], axis=1).astype(f)
    p = np.arange(P)
    j = np.arange(S)
    log_g = np.log(1.0 - 2.0 ** (-5.0 - np.arange(RH)))
    diff = j[None, :] - p[:, None]
    decay = np.where(diff[:, None, :] >= 0, np.exp(log_g[None, :, None] * np.maximum(diff, 0)[:, None, :]), 0.0) * SCALE
    strip = np.where(j[None, :] - 3 * P > p[:, None], NEG, 0.0)
    a, b = p[:, None], p[None, :]
    masks = [a == b]
    for level in range(LEVELS):
        c = 1 << level
        masks.append((a // (2 * c) == b // (2 * c)) & (a % (2 * c) < c) & (b % (2 * c) >= c))
    t = (np.arange(NT)[None, :] * P + p[:, None])
    end = np.arange(NCMP) * 16 + 31
    cmp_bias = np.where(end[None, None, :] <= t[:, :, None], 0.0, NEG)
    keep = np.ones((P, S))
    keep[:, ::P] = 0.0
    small = np.concatenate([np.eye(P), rope.reshape(P, -1), strip, cmp_bias.reshape(P, -1), (t >= 31) * 1.0, keep], axis=1)
    return {"c_small": small.astype(f), "c_decay": decay.astype(f).reshape(P, RH * S),
            "c_masks": np.stack(masks, 1).astype(f)}


def build(nc, io, out):
    ctx = ExitStack()
    with ctx:
        def sb(name, shape, dt=F32):
            return ctx.enter_context(nc.sbuf_tensor(name, shape, dt))

        def sem(name):
            return ctx.enter_context(nc.semaphore(name))

        ps = ctx.enter_context(nc.psum_tensor("ps", [P, 8, HALF], F32))
        h_t = sb("h_t", [P, KT, S])
        arena = sb("arena", [P, 28160])
        def over(name, shape, at):
            return nc.alloc_sbuf_tensor_at(name, shape, F32R, offset=MAP + 4 * at)

        x_hi = over("x_hi", [P, KT, S], 0)
        x_lo = over("x_lo", [P, KT, S], KT * S + 19456)
        w_hi = over("w_hi", [P, 2, PIECE], KT * S + 19456 + 4096)
        w_lo = over("w_lo", [P, 2, PIECE], KT * S + 19456 + 4096 + 2 * PIECE)
        x_tok = sb("x_tok", [P, NT, D])
        ring = sb("ring", [P, RING, SLOT])
        row = sb("row", [P, 2, D])
        ada_acc = sb("ada_acc", [P, 2, HALF])
        small = sb("small", [P, 128 + 3 * 128 + 512 + 124 + 4 + 512])
        masks = sb("masks", [P, LEVELS + 1, P], I8)
        vec = sb("vec", [P, 416])
        mod = sb("mod", [P, 5, 2, KT])
        ones = sb("ones", [P, P])
        out_norm = sb("out_norm", [P, P])
        qk_norm = sb("qk_norm", [P, 3, HD])
        cmp_norm = sb("cmp_norm", [P, HD])
        stat = sb("stat", [P, 256])
        fac = sb("fac", [P, 96])
        small2 = sb("small2", [P, 1040])
        junk = sb("junk", [P, D])
        junk2 = junk[:, HALF:D]
        eps = sb("eps", [P, 1])
        c_act = sb("c_act", [P, KT])
        best = sb("best", [P, 8])

        ident = small[:, 0:128]
        rope_t = small[:, 128:512].rearrange("p (k t d) -> p k t d", k=3, t=NT)
        strip = small[:, 512:1024]
        cmp_bias = small[:, 1024:1148].rearrange("p (t c) -> p t c", t=NT)
        row_valid = small[:, 1148:1152]
        keep = small[:, 1152:1664]

        def carve(sizes):
            at, got = 0, []
            for n in sizes:
                got.append(arena[:, at:at + n])
                at += n
            assert at <= 28160, at
            return got

        bank_full = [sem(f"bank_full{b}") for b in range(8)]
        bank_free = [sem(f"bank_free{b}") for b in range(8)]
        landed = [sem(f"landed{r}") for r in range(2 * RING)]
        names = """consts_in x_in rows_in out_norm_in cmp_pos_in row_in out_done vec_done c_act_done c_rep_done ones_done
            norm_rms xn_ready x_ready down_step ada_step mod_ready gate_ready rope_done iw_done decayed ret_pv
            rel_used picked ret_square ret_rms ret_normed mixed_ready p_ready pv_done o_done y_ready y_square y_rms
            y_scaled act_step dve_step pool_step hid_gate hid_up hid_done v_done sg_done f_abs logf_done k_log k_done
            g_done d_sub d_exp qk_done q1_done attn_diag attn_zero o_raw ho_square ho_rms ho_ready cmp_sq cmp_rms
            cmp_tok cmp_l cmp_p cmp_o raw_done raw_sq raw_rms raw_norm rope2_done gates_exp gates_done branch_out
            nsa_added u_done h1_done e_done conv_pre tabs_done ho_scaled eq_done vpart kvraw w2_in gained whole_done hi_done lo_done piece_done x_split hid_hi acc_done gate_row_in0 gate_row_in1 acc_half""".split()
        s = {n: sem(n) for n in names}

        bank_use, bank_fills, bank_frees, turn = {}, [0] * 8, [0] * 8, [0]

        def plan_bank(key, bank=None, counted=True):
            if bank is None:
                bank = turn[0]
                turn[0] = (bank + 1) % 8
            assert key not in bank_use, key
            bank_use[key] = (bank, bank_fills[bank], bank_frees[bank])
            bank_fills[bank] += counted
            bank_frees[bank] += 1
        FULL, FREE = bank_full, bank_free

        def open_bank(key):
            b, _, free = bank_use[key]
            if free > 0:
                nc.tensor.wait_ge(FREE[b], free)
            return ps[:, b]

        def filled(eng, key):
            b, fill, _ = bank_use[key]
            eng.wait_ge(FULL[b], fill + 1)
            return ps[:, b]

        def full(key):
            return FULL[bank_use[key][0]]

        def free(key):
            return FREE[bank_use[key][0]]

        def evacuated(eng, key):
            b, _, f = bank_use[key]
            eng.wait_ge(FREE[b], f + 1)

        def own_order(eng, own):
            count = [0]

            def step(ins):
                ins.then_inc(own, 1)
                count[0] += 1

            def after():
                if count[0]:
                    eng.wait_ge(own, count[0])

            return step, after

        units, unit_at, slot_dmas = [], {}, [0] * (2 * RING)

        def unit(key, pieces, release, release_first=None):
            n = len(units)
            for h in range(2):
                slot_dmas[2 * (n % RING) + h] += len(pieces[h])
            unit_at[key] = (n % RING, [16 * slot_dmas[2 * (n % RING) + h] for h in range(2)])
            units.append((pieces, (release_first or release, release)))

        def arrived(eng, key, halves=(0, 1)):
            slot, counts = unit_at[key]
            for h in halves:
                eng.wait_ge(landed[2 * slot + h], counts[h])
            return ring[:, slot]

        def in_halves(sl, rows, width):
            return sl.rearrange("p (h x) -> p h x", h=2)[:, :, 0:rows * width].rearrange("p h (k n) -> p h k n", k=rows)

        def columns(w, c0, n, at=0, width=None):
            width = width or n

            def half(h):
                return (lambda sl: in_halves(sl, 4, width)[:, h, :, at:at + n],
                        w[h * HALF:(h + 1) * HALF, c0:c0 + n].rearrange("(k p) n -> p k n", p=P))

            return [half(0)], [half(1)]

        def together(*loads):
            return [sum((load[h] for load in loads), []) for h in range(2)]

        down_groups = [(0, 4), (4, 4), (8, 4), (12, 4), (16, 4), (20, 2)]

        w_in, w_out = io["w_in"][0], io["w_out"][0]
        P1 = {"iq": [(2688, 512)], "kk": [(2560, 128), (3200, 72)], "aq": [(2048, 512)], "rk": [(512, 512)],
              "rq": [(0, 512)], "rv": [(1024, 512)], "rg": [(1536, 512)]}
        P1_ORDER = ["iq", "kk", "aq", "rk", "rq", "rv", "rg"]
        ROPED = ["iq", "kk", "aq", "rk", "rq"]

        plan_bank("vec")

        def plan_norm(i):
            for kt in range(KT):
                plan_bank(("xT", i, kt))

        def plan_tok_gemm(name, pieces_of, n_units):
            for u in range(n_units):
                for t in range(NT):
                    plan_bank((name, u, t))
                unit((name, u), pieces_of(u), ("bank", (name, u, NT - 1)))

        ADA_W = [io["ada_w_2"][m] for m in range(4)] + [io["kv_ada_w_2"]]
        ADA = [(0, j) for j in range(6)] + [(1, j) for j in range(6)] + [(2, j) for j in range(6)] \
            + [(4, j) for j in range(4)] + [(3, j) for j in range(6)]
        ADA_N = {mj: n for n, mj in enumerate(ADA)}
        ada_after = {(0, u): [ADA[u]] for u in range(10)}
        ada_after.update({(1, u): [ADA[12 + u]] for u in range(11)})
        ada_down = {0: ADA[10:12], 1: ADA[23:25]}
        ADA_LATE = ADA[25:]

        def ada_unit(m, j):
            unit(("ada", m, j), columns(ADA_W[m], j * HALF, HALF), ("sem", "acc_done", ADA_N[(m, j)] + 1),
                 ("sem", "acc_half", ADA_N[(m, j)] + 1))

        splits = [0]
        split_at = {}
        piece_end = []
        counted_pieces = [0]

        def plan_piece(key, last_bank=None):
            split_at[key] = splits[0]
            splits[0] += 1
            counted_pieces[0] += last_bank is None
            piece_end.append(last_bank or counted_pieces[0])

        def piece_read(eng, n):
            if isinstance(piece_end[n], int):
                eng.wait_ge(s["piece_done"], piece_end[n])
            else:
                filled(eng, piece_end[n])

        def plan_ffn(i, w_up, w_down):
            for u in range(FFN_UNITS):
                for j in range(4):
                    plan_bank(("up", i, u, j))
                for q in range(4):
                    plan_piece(("up", i, u, q), ("up", i, u, 3) if q == 3 else None)
                unit(("up", i, u), together(columns(w_up, u * 256, 256, 0, 512), columns(w_up, DFF + u * 256, 256, 256, 512)),
                     ("sem", "lo_done", splits[0]), ("sem", "lo_done", splits[0] - 2))
                for m, j in ada_after.get((i, u), []):
                    ada_unit(m, j)
                for m, j in ada_after.get((i, u - 1), []):
                    plan_bank(("ada", m, j))
            for m, j in ada_after.get((i, FFN_UNITS - 1), []):
                plan_bank(("ada", m, j))
            for j in range(8):
                plan_bank(("down", i, j))
            for g, (k0, n) in enumerate(down_groups):
                for k in range(k0, k0 + n):
                    plan_piece(("down", i, k), ("down", i, 7) if k == FT - 1 else None)
                n //= 2
                halves = [[(lambda sl, n=n, h=h: in_halves(sl, n, D)[:, h],
                            w_down[(k0 + h * n) * P:(k0 + h * n + n) * P, :].rearrange("(k p) n -> p k n", p=P))] for h in range(2)]
                unit(("down", i, g), halves, ("sem", "lo_done", splits[0]), ("sem", "lo_done", splits[0] - n))
                for mj in ada_down.get(i, [])[g:g + 1]:
                    ada_unit(*mj)
            for mj in ada_down.get(i, []):
                plan_bank(("ada",) + mj)

        def plan_out(name, w, n_in=KT):
            for kt in range(n_in):
                plan_bank((name, "T", kt))
            plan_tok_gemm(name, lambda u: columns(w, u * 512, 512), 2)

        def plan_attention(name, n_units, okeys):
            for i in range(n_units + 2):
                if i < n_units:
                    plan_bank((name, "S", i), i % 3)
                if 1 <= i <= n_units:
                    plan_bank((name, "T", i - 1), 3 + (i - 1) % 3)
                if i >= 2 and (i - 2) % 8 == 0:
                    plan_bank((name, "O", (i - 2) // 8), 6 + ((i - 2) // 8) % 2, counted=False)

        plan_norm(0)
        lagged = []
        for name in P1_ORDER:
            loads, at = [], 0
            total = sum(n for _, n in P1[name])
            for c0, n in P1[name]:
                loads.append(columns(w_in, c0, n, at, total))
                at += n
            unit(name, together(*loads), ("bank", (name, NT - 1)))
            for t in range(NT):
                plan_bank((name, t))
                if lagged:
                    plan_bank(lagged.pop(0))
                if name in ROPED:
                    lagged.append((name, "T", t))
        for t in range(1, NT):
            for h in range(RH):
                plan_bank(("index", t, h))
        unit("decay", [[(lambda sl, h=h: sl[:, h * 2048:(h + 1) * 2048], io["c_decay"][:, h * 2048:(h + 1) * 2048])] for h in range(2)],
             ("sem", "decayed", RH))
        for h in range(RH + 1):
            if h < RH:
                for m in range(NT):
                    plan_bank(("ret_s", h, m), m)
            if h == 1:
                for t in range(NT):
                    plan_bank(("ret_o", t), 4 + t)
        DSA_UNITS = [(t, h) for t in range(NT) for h in range(RH)]
        plan_attention("dsa", len(DSA_UNITS), None)
        plan_out("mix1", w_out)
        plan_norm(1)
        plan_ffn(0, io["w_up"][0], io["w_down"][0])
        plan_norm(2)
        hw = io["hgrn_w_in_2"][0]
        for u in range(2):
            for j in range(4):
                plan_bank(("hq", u, j))
            unit(("hq", u), columns(hw, u * 512, 512), ("bank", ("hq", u, 3)))
        plan_tok_gemm("hg", lambda u: columns(hw, 3072 + u * 512, 512), 2)
        for u in range(2):
            for j in range(4):
                plan_bank(("hf", u, j))
            unit(("hf", u), columns(hw, 1024 + u * 512, 512), ("bank", ("hf", u, 3)))
        plan_tok_gemm("hi", lambda u: columns(hw, 2048 + u * 512, 512), 2)
        for h in range(HH + 1):
            if h < HH:
                for lv in range(LEVELS + 1):
                    plan_bank(("diag", h, lv), lv % 4)
                for b in range(2):
                    plan_bank(("far", h, b), 4 + b)
            if h >= 1:
                plan_bank(("ho", h - 1), 6 + h % 2)
        plan_out("mix2", io["hgrn_w_out_2"][0])
        plan_norm(3)
        plan_ffn(1, io["ffn_w_in_2"][0], io["ffn_w_out_2"][0])
        plan_norm(4)
        wkv, wq = io["nsa_w_kv_2"], io["nsa_w_q_2"][0]
        for j in range(4):
            plan_bank(("kvc", j))
        unit("kvc", columns(wkv, 0, 512), ("bank", ("kvc", 3)))
        plan_tok_gemm("kvs", lambda u: columns(wkv, 512 + u * 512, 512), 2)
        plan_tok_gemm("nq", lambda u: columns(wq, u * 512, 512 if u < 2 else 48), 3)
        w1 = io["cmp_w1_2"]
        for kv in range(2):
            for j in range(2):
                plan_bank(("cmp1", kv, j))
            unit(("cmp1", kv), [[(lambda sl, h=h: sl[:, h * 2048:(h + 1) * 2048].rearrange("p (r n) -> p r n", r=8),
                                  w1[kv, h * 1024:(h + 1) * 1024, :].rearrange("(r p) n -> p r n", p=P))] for h in range(2)],
                 ("bank", ("cmp1", kv, 1)))
        plan_bank("cmp2")
        plan_bank("cmpT")
        for t in range(NT):
            for j in range(5):
                plan_bank(("nT", t, j))
        GROUPS = [(t, kp) for t in range(NT) for kp in range(2)]
        for i in range(len(GROUPS) + 2):
            if i < len(GROUPS):
                for q in range(2):
                    plan_bank(("cS", i, q), q + 2 * (i % 2))
            if 1 <= i <= len(GROUPS):
                for q in range(2):
                    plan_bank(("cT", i - 1, q), 4 + q)
            if i >= 2:
                plan_bank(("cO", i - 2), 6 + i % 2)
        NSA_GROUPS = [(t, kp, br) for t in range(NT) for kp in range(2) for br in range(2)]
        plan_attention("nsa", 8 * len(NSA_GROUPS), None)
        for m, j in ADA_LATE:
            plan_bank(("ada", m, j))
            ada_unit(m, j)
        plan_out("mix3", io["nsa_w_out_2"][0])
        plan_norm(5)
        plan_ffn(2, io["ffn_w_in_2"][1], io["ffn_w_out_2"][1])

        (a_xn, a_rq, a_rk, a_aq, a_iq, a_kk, a_rv, a_rg, a_av, a_tmp, a_sT, a_isc, a_sel, a_rel) = carve(
            [4096, 2048, 2048, 2048, 2048, 1024, 2048, 2048, 256, 3328, 2560, 1536, 1536, 1024])
        tiles4 = lambda a: a.rearrange("p (k n) -> p k n", k=4)
        xn = tiles4(a_xn)
        T1 = {"rq": tiles4(a_rq), "rk": tiles4(a_rk), "aq": tiles4(a_aq), "iq": tiles4(a_iq),
              "kk": a_kk.rearrange("p (k n) -> p k n", k=2)}
        rv_tok, rg_tok, av_tok = tiles4(a_rv), tiles4(a_rg), tiles4(a_av)
        iw = fac[:, 64:96].rearrange("p (t h) -> p t h", t=NT)
        rope_a, rope_b, rope_o = [a_tmp[:, i * 1024:(i + 1) * 1024].rearrange("p (j n) -> p j n", j=2) for i in range(3)]
        sT = a_sT.rearrange("p (j n) -> p j n", j=2)
        isc = a_isc.rearrange("p (j n) -> p j n", j=3)
        sel_bias = a_sel.rearrange("p (j n) -> p j n", j=3)
        rel = a_rel.rearrange("p (j n) -> p j n", j=2)
        mixed = tiles4(a_xn)
        att_l, att_p, att_pt = rope_a, rope_b, rope_o
        y1 = arena[:, 4096:8192].rearrange("p (k n) -> p k n", k=4)

        f_xn, f_hid, f_tmp = carve([4096, FT * S, 8 * S])
        hid = f_hid.rearrange("p (k n) -> p k n", k=FT)
        ftmp = f_tmp.rearrange("p (j n) -> p j n", j=8)
        hid_hi = x_hi[:, 0:4, :]
        hid_lo = x_hi[:, 4:8, :]
        yf = tiles4(f_xn)

        (h_v, h_sg, h_q, h_k, h_g, h_d0, h_at) = carve([4096, 4096, 4096, 4096, 4096, 3584, 4096])
        v_tok, sg_tok = tiles4(h_v), tiles4(h_sg)
        xn_h = tiles4(h_v)
        HQ, HK, HG = [a.rearrange("p (h n) -> p h n", h=HH) for a in (h_q, h_k, h_g)]
        lvl = [h_d0.rearrange("p (l n) -> p l n", l=LEVELS),
               h_t[:, 0:LEVELS, :]]
        attn = h_at.rearrange("p (j s n) -> p j s n", j=2, s=NT)
        f_work = [arena[:, 20480:22528], arena[:, 22528:24576], arena[:, 24576:26624]]
        k1 = small2[:, 0:512].rearrange("p (s n) -> p s n", s=4)
        q1 = small2[:, 512:1024].rearrange("p (s n) -> p s n", s=4)
        tot = small2[:, 1024:1032]
        y2 = tiles4(h_q)

        (n_xn, n_raw, n_qn, n_qr, n_k, n_v, n_hkv) = carve([4096, 6144, 4096, 4096, 2048, 2048, 4096])
        raw = n_raw.rearrange("p (t h d) -> p t h d", t=NT, h=24)
        qn_t = n_qn.rearrange("p (k n) -> p k n", k=8)
        qr_t = n_qr.rearrange("p (k n) -> p k n", k=8)
        k_t = tiles4(n_k)
        v_nsa = n_v.rearrange("p (t b n) -> p t b n", t=NT, b=2)
        hkv_t = n_hkv.rearrange("p (k n) -> p k n", k=8)
        win = n_qn[:, 0:3968].rearrange("p (kv r h i) -> p kv r h i", kv=2, r=16, h=4)
        h1 = small2[:, 0:496].rearrange("p (kv n h i) -> p kv n h i", kv=2, n=2, h=4)
        kc_raw = small2[0:NCMP, 496:752]
        kc_tok = small2[0:NCMP, 752:1008].rearrange("p (h d) -> p h d", h=4)
        vc_tok = n_hkv[:, 3456:3712].rearrange("p (h d) -> p h d", h=4)
        kc_t = n_hkv[:, 3712:3776].rearrange("p (c i) -> p c i", c=2)
        w2_sb = n_hkv[:, 3776:4032].rearrange("p (kv n d) -> p kv n d", kv=2, n=2)
        nsa_tok = tiles4(n_xn)
        n_a, n_b, n_o = [n_hkv[:, i * 1024:(i + 1) * 1024].rearrange("p (j n) -> p j n", j=2) for i in range(3)]
        cl = n_raw[:, 0:496].rearrange("p (j h c) -> p j h c", j=2, h=8)
        cp = n_raw[:, 512:1008].rearrange("p (j h c) -> p j h c", j=2, h=8)
        cpt = n_raw[0:NCMP, 1024:3072].rearrange("p (j h n) -> p j h n", j=2, h=8)
        n_tmp = n_raw[:, 3072:4096].rearrange("p (j n) -> p j n", j=2)
        gates = n_hkv[:, 3072:3264].rearrange("p (t g) -> p t g", t=NT)
        gates_e = n_hkv[:, 3264:3456].rearrange("p (t g) -> p t g", t=NT)
        y3 = tiles4(n_qn)

        XN = {0: xn, 1: tiles4(f_xn), 2: xn_h, 3: tiles4(f_xn), 4: tiles4(n_xn), 5: tiles4(f_xn)}

        vec_at, at = {}, 0
        for n, r in VEC_ROWS:
            vec_at[n] = at
            at += r
        CONV = 64
        POS = CONV + 176
        BIAS = POS + 64

        def vcol(name, i=0):
            return vec[:, vec_at[name] + 8 * i:vec_at[name] + 8 * i + 8]

        NORM_OUT = {
            0: [(h_t, vcol("mix_norm_pre"), None)], 1: [(h_t, vcol("ffn_norm_pre"), None)],
            2: [(h_t, mod[:, 0, 0], mod[:, 0, 1])], 3: [(h_t, mod[:, 1, 0], mod[:, 1, 1])],
            4: [(h_t, mod[:, 2, 0], mod[:, 2, 1]), (hkv_t, mod[:, 4, 0], mod[:, 4, 1])],
            5: [(h_t, mod[:, 3, 0], mod[:, 3, 1])]}
        MOD_GAIN = {0: vcol("norm_mix_2", 0), 1: vcol("norm_ffn_2", 0), 2: vcol("norm_mix_2", 1),
                    3: vcol("norm_ffn_2", 1), 4: vcol("kv_norm_2")}
        MOD_ORDER = [0, 1, 2, 4, 3]
        MOD_READY = {m: i + 1 for i, m in enumerate(MOD_ORDER)}
        FFN_NORM = {1: 0, 3: 1, 5: 2}
        NORM_MOD = {2: 0, 3: 1, 4: 4, 5: 3}

        vec_rows = arena[0:64, 8192:8320]
        conv_rows = [arena[0:88, 8320:8448], arena[0:88, 8448:8576]]
        bias_rows = arena[0:112, 8832:8960]
        mask_rows = arena[:, 9216:9216 + (LEVELS + 1) * P].rearrange("p (l n) -> p l n", l=LEVELS + 1)
        pos_rows = arena[0:32, 8576:8832]

        def dsa_unit(i):
            t, h = DSA_UNITS[i]
            q = slice(64 * (h % 2), 64 * (h % 2) + 64)
            n = (t + 1) * P
            return dict(q=T1["aq"][q, h // 2, t * P:(t + 1) * P], k=T1["kk"][q, 0, 0:n], n=n,
                        bias=strip[:, 3 * P:] if t == 0 else sel_bias[:, t - 1, 0:n],
                        v=lambda b: av_tok[:, b, :], slot=h)

        def nsa_unit(i):
            t, kp, br = NSA_GROUPS[i // 8]
            g, ko = (i % 8) // 2, i % 2
            q = slice(64 * ko, 64 * ko + 64)
            n = (t + 1) * P
            c = (kp * 2 + ko) * HD
            return dict(q=qr_t[q, kp * 4 + g, t * P:(t + 1) * P], k=k_t[q, 2 * br + kp, 0:n], n=n,
                        bias=strip[:, 3 * P - t * P:],
                        v=lambda b: v_nsa[:, b, br, c:c + HD], slot=ko * 4 + g)

        ATT = {"dsa": (dsa_unit, len(DSA_UNITS), (att_l, att_p, att_pt), 0),
               "nsa": (nsa_unit, 8 * len(NSA_GROUPS), (n_a, n_b, n_o), len(DSA_UNITS))}
        neg_max = stat[:, 160:164]
        den = fac[:, 0:16].rearrange("p (j h) -> p j h", j=2)
        rden = fac[:, 16:32].rearrange("p (j h) -> p j h", j=2)

        def hid_ready(eng, i, k):
            if i == 0:
                eng.wait_ge(s["hid_done"], k + 1)
            else:
                evacuated(eng, ("up", i, k // 2, 2 + k % 2))

        def tok_keys(name):
            return [(u, t, (name, u, t)) for u in range(2) for t in range(NT)]

        def down_keys(i):
            return [(u, t, ("down", i, 2 * t + u)) for u in range(2) for t in range(NT)]

        block = ctx.enter_context(nc.Block())

        @block.sync
        def _(sp):
            for n, (pieces, _) in enumerate(units):
                for h in range(2):
                    if n >= RING:
                        kind = units[n - RING][1][h]
                        if kind[0] == "bank":
                            filled(sp, kind[1])
                        else:
                            sp.wait_ge(s[kind[1]], kind[2])
                    for dst, src in pieces[h]:
                        sp.dma_start(dst(ring[:, n % RING]), src).then_inc(landed[2 * (n % RING) + h], 16)

        @block.gpsimd
        def _(pool):
            g = nc.gpsimd
            g.memset(ones[:, :], 1.0).then_inc(s["ones_done"], 1)

            def load_row(src, i, n):
                pool.dma_start(row[:, i, :], src.partition_broadcast(P)).then_inc(s["row_in"], 16)

            load_row(io["mix_norm_post"][0], 0, 0)
            load_row(io["ffn_norm_post"][0], 1, 0)

            def load_gate(m):
                pool.dma_start(row[:, m % 2, :], io["ada_b_2"][m, 2 * D:3 * D].partition_broadcast(P)).then_inc(s[f"gate_row_in{m % 2}"], 16)

            def add_to_x(stage, y, keys=None):
                for t in range(NT):
                    if keys is None:
                        pool.wait_ge(s["y_scaled"], NT * stage + t + 1)
                    else:
                        for _, tt, key in keys:
                            if tt == t:
                                evacuated(pool, key)
                    g.tensor_tensor(x_tok[:, t], x_tok[:, t], y[:, t], ALU.add).then_inc(s["x_ready"], 1)

            dec = arrived(pool, "decay")
            for h in range(RH):
                for m in range(NT):
                    n = S - m * P
                    evacuated(pool, ("ret_s", h, m))
                    o = [0, 512, 896, 1152][m]
                    ins = g.tensor_tensor(sT[:, h % 2, o:o + n], sT[:, h % 2, o:o + n], dec[:, h * S:h * S + n], ALU.mult)
                    if m == NT - 1:
                        ins.then_inc(s["decayed"], 1)
            for t in range(NT):
                evacuated(pool, ("ret_o", t))
                g.tensor_tensor(mixed[:, t, 0:512], mixed[:, t, 0:512], rg_tok[:, t], ALU.mult).then_inc(s["mixed_ready"], 1)
            add_to_x(0, y1)
            load_gate(0)
            add_to_x(1, yf)
            load_gate(1)
            pool.wait_ge(s["out_norm_in"], 16)
            for u in range(2):
                for t in range(NT):
                    evacuated(pool, ("hg", u, t))
                    w = sg_tok[:, t, u * 512:(u + 1) * 512].rearrange("p (h d) -> p h d", h=4)
                    g.tensor_tensor(w, w, out_norm[:, :].unsqueeze(1).broadcast_to([P, 4, P]), ALU.mult).then_inc(s["sg_done"], 1)
            pool.wait_ge(s["k_done"], 2)
            g.memset(attn[:, :, :, :], 0.0).then_inc(s["attn_zero"], 1)
            for h in range(HH):
                pool.wait_ge(s["g_done"], h + 1)
                if h == 0:
                    pool.wait_ge(s["k_done"], 2)
                if h >= 2:
                    filled(pool, ("diag", h - 2, LEVELS))
                if h == 1:
                    filled(pool, ("hi", 1, NT - 1))
                for lv in range(LEVELS):
                    c = 1 << lv
                    src = HG[:, h].rearrange("p (b q c) -> p b q c", q=2, c=c)
                    dst = lvl[h % 2][:, lv].rearrange("p (b q c) -> p b q c", q=2, c=c)
                    mid = src[:, :, 0, c - 1:c].broadcast_to([P, S // (2 * c), c])
                    g.tensor_tensor(dst[:, :, 0], mid, src[:, :, 0], ALU.subtract).then_inc(s["d_sub"], 1)
                    g.tensor_tensor(dst[:, :, 1], src[:, :, 1], mid, ALU.subtract).then_inc(s["d_sub"], 1)
            for t in range(NT):
                pool.wait_ge(s["ho_scaled"], t + 1)
                g.tensor_tensor(v_tok[:, t], v_tok[:, t], sg_tok[:, t], ALU.mult).then_inc(s["ho_ready"], 1)
            add_to_x(2, y2, tok_keys("mix2"))
            load_gate(2)
            add_to_x(3, yf, down_keys(1))
            load_gate(3)
            for t in range(NT):
                for j in range(3):
                    i = 3 * t + j
                    pool.wait_ge(s["raw_norm"], i + 1)
                    if j < 2:
                        w = n_a[:, i % 2].rearrange("p (h d) -> p h d", h=8)
                        g.tensor_tensor(w, w, qk_norm[:, 0:1, :].broadcast_to([P, 8, HD]), ALU.mult).then_inc(s["gained"], 1)
                    else:
                        w = n_a[:, i % 2].rearrange("p (k h d) -> p k h d", k=2, h=4)
                        g.tensor_tensor(w, w, qk_norm[:, 1:3, :].unsqueeze(2).broadcast_to([P, 2, 4, HD]), ALU.mult).then_inc(s["gained"], 1)
            for i in range(len(NSA_GROUPS)):
                t, kp, br = NSA_GROUPS[i]
                evacuated(pool, ("nsa", "O", i))
                if i >= 1:
                    pool.wait_ge(s["nsa_added"], i)
                w = nsa_tok[:, t, kp * 512:(kp + 1) * 512]
                g.tensor_tensor(w, w, n_tmp[:, i % 2], ALU.add).then_inc(s["nsa_added"], 1)
            add_to_x(4, y3, tok_keys("mix3"))
            add_to_x(5, yf, down_keys(2))
            pool.wait_ge(s["x_ready"], 6 * NT)

        @block.scalar
        def _(act):
            a = nc.scalar
            step, after = own_order(act, s["act_step"])
            act.dma_start(small[:, :], io["c_small"]).then_inc(s["consts_in"], 16)
            act.dma_start(x_tok[:, :, :], io["x"][0].rearrange("(t p) n -> p t n", p=P)).then_inc(s["x_in"], 16)
            act.dma_start(mask_rows, io["c_masks"]).then_inc(s["consts_in"], 16)
            n_rows = 0
            for name, r in VEC_ROWS:
                src = io[name]
                src = src.rearrange("a (k p) -> (a k) p", p=P) if len(src.shape) == 2 else src.rearrange("(k p) -> k p", p=P)
                act.dma_start(vec_rows[vec_at[name]:vec_at[name] + r, :], src).then_inc(s["rows_in"], 16)
                n_rows += 16
            for j in range(3):
                act.dma_start(conv_rows[j // 2][44 * (j % 2):44 * (j % 2) + 44, :],
                              io["conv_w"][0, j].rearrange("(k p) -> k p", p=P)).then_inc(s["rows_in"], 16)
            act.dma_start(conv_rows[1][44:88, :], io["conv_b"][0].rearrange("(k p) -> k p", p=P)).then_inc(s["rows_in"], 16)
            for kv in range(2):
                for q in range(2):
                    act.dma_start(pos_rows[:, kv * 128 + q * 64:kv * 128 + q * 64 + 64], io["cmp_pos_2"][kv]).then_inc(s["rows_in"], 16)
            act.dma_start(bias_rows[0:96, :], io["ada_b_2"].rearrange("m (k p) -> (m k) p", p=P)).then_inc(s["rows_in"], 16)
            act.dma_start(bias_rows[96:112, :], io["kv_ada_b_2"].rearrange("(k p) -> k p", p=P)).then_inc(s["rows_in"], 16)
            assert n_rows + 16 * 10 == ROWS_IN
            act.dma_start(out_norm[:, :], io["hgrn_out_norm_2"][0].partition_broadcast(P)).then_inc(s["out_norm_in"], 16)
            act.dma_start(qk_norm[:, 0, :], io["nsa_q_norm_2"][0].partition_broadcast(P)).then_inc(s["cmp_pos_in"], 16)
            act.dma_start(qk_norm[:, 1, :], io["nsa_k_norm_2"][1].partition_broadcast(P)).then_inc(s["cmp_pos_in"], 16)
            act.dma_start(qk_norm[:, 2, :], io["nsa_k_norm_2"][2].partition_broadcast(P)).then_inc(s["cmp_pos_in"], 16)
            act.dma_start(cmp_norm[:, :], io["nsa_k_norm_2"][0].partition_broadcast(P)).then_inc(s["cmp_pos_in"], 16)

            def norm(i):
                if i == 0:
                    act.wait_ge(s["x_in"], 16)
                for t in range(NT):
                    if i:
                        act.wait_ge(s["x_ready"], NT * (i - 1) + t + 1)
                    step(a.activation(XN[i][:, t], x_tok[:, t], ACT.Square, accum_out=stat[:, t:t + 1]))
                after()
                a.activation(stat[:, 4:8], stat[:, 0:4], ACT.Sqrt, scale=1.0 / D, bias=eps[:, :]).then_inc(s["norm_rms"], 1)
                norm_out(i)

            def norm_out(i):
                if i in FFN_NORM:
                    if i >= 2:
                        act.wait_ge(s["mod_ready"], MOD_READY[NORM_MOD[i]])
                    _, gain, shift = NORM_OUT[i][0]
                    for kt in range(KT):
                        if kt >= 4:
                            act.wait_ge(s["x_split"], (KT + FT) * FFN_NORM[i] + kt - 3)
                        p = filled(act, ("xT", i, kt))
                        a.activation(ftmp[:, kt % 4], p, ACT.Identity, scale=gain[:, kt:kt + 1],
                                     bias=0.0 if shift is None else shift[:, kt:kt + 1]).then_inc(free(("xT", i, kt)), 1)
                    return
                if i >= 2:
                    act.wait_ge(s["mod_ready"], MOD_READY[NORM_MOD[i]])
                for kt in range(0, KT, 2):
                    p = filled(act, ("xT", i, kt))
                    outs = NORM_OUT[i]
                    for j, (dst, gain, shift) in enumerate(outs):
                        ins = a.activation(dst[:, kt], p, ACT.Identity, scale=gain[:, kt:kt + 1],
                                           bias=0.0 if shift is None else shift[:, kt:kt + 1])
                        if j == len(outs) - 1:
                            ins.then_inc(free(("xT", i, kt)), 1)

            def post_rms(i, y, keys):
                for t in range(NT):
                    for _, tt, key in keys:
                        if tt == t:
                            evacuated(act, key)
                    step(a.activation(junk[:, 0:1024], y[:, t], ACT.Square, accum_out=stat[:, 16 + t:17 + t]))
                    after()
                a.activation(stat[:, 20:24], stat[:, 16:20], ACT.Sqrt, scale=1.0 / D, bias=eps[:, :]).then_inc(s["y_rms"], 1)

            def in_t(name):
                for kt in range(0, KT, 2):
                    p = filled(act, (name, "T", kt))
                    a.activation(h_t[:, kt], p, ACT.Copy).then_inc(free((name, "T", kt)), 1)

            def high(key, src):
                n = split_at[key]
                if n >= 2:
                    piece_read(act, n - 2)
                a.activation(w_hi[:, n % 2], src, ACT.Copy).then_inc(s["hi_done"], 1)

            def up_out(i, u):
                for q in range(4):
                    buf = ftmp[:, 4 * (u % 2) + q]
                    if i == 0:
                        n = 22 * (q // 2) + 2 * u + q % 2
                        if u >= 2:
                            act.wait_ge(s["hid_done"], 2 * (u - 1))
                        if u < 2 and q == 0:
                            act.wait_ge(s["x_split"], KT)
                        p = filled(act, ("up", i, u, q))
                        a.activation(buf, p, ACT.Identity, scale=vec[:, CONV + 88 + n:CONV + 89 + n],
                                     bias=vec[:, CONV + 132 + n:CONV + 133 + n]).then_inc(s["conv_pre"], 1)
                    elif q < 2:
                        if u >= 2:
                            evacuated(act, ("up", i, u - 2, 2 + q))
                        p = filled(act, ("up", i, u, q))
                        a.activation(buf, p, ACT.Silu).then_inc(free(("up", i, u, q)), 1)
                if i == 0:
                    for q in range(2):
                        evacuated(act, ("up", i, u, q))
                        a.activation(ftmp[:, 4 * (u % 2) + q], ftmp[:, 4 * (u % 2) + q], ACT.Silu).then_inc(s["hid_gate"], 1)

            def ffn(i):
                for u in range(FFN_UNITS):
                    w = arrived(act, ("up", i, u), (0,))
                    for q in range(2):
                        high(("up", i, u, q), w[:, q * PIECE:(q + 1) * PIECE])
                    if u:
                        up_out(i, u - 1)
                    arrived(act, ("up", i, u), (1,))
                    for q in range(2, 4):
                        high(("up", i, u, q), w[:, q * PIECE:(q + 1) * PIECE])
                up_out(i, FFN_UNITS - 1)
                for g, (k0, n) in enumerate(down_groups):
                    w = arrived(act, ("down", i, g), (0,))
                    for k in range(k0, k0 + n):
                        if k == k0 + n // 2:
                            arrived(act, ("down", i, g), (1,))
                        high(("down", i, k), in_halves(w, n // 2, PIECE)[:, (k - k0) // (n // 2), (k - k0) % (n // 2)])
                        hid_ready(act, i, k)
                        if k == 0:
                            filled(act, ("up", i, FFN_UNITS - 1, 3))
                        if k >= 4:
                            piece_read(act, split_at[("down", i, k - 4)])
                        a.activation(hid_hi[:, k % 4], hid[:, k], ACT.Copy).then_inc(s["hid_hi"], 1)

            def attention(name, after_t):
                unit_of, n_units, (L, PB, PT), base = ATT[name]
                for i in range(n_units + 1):
                    if i < n_units:
                        u = unit_of(i)
                        evacuated(act, (name, "S", i))
                        if i >= 2:
                            filled(act, (name, "T", i - 2))
                        if i % 8 == 0 and i >= 16:
                            evacuated(act, (name, "O", i // 8 - 2))
                        a.activation(PB[:, i % 2, 0:u["n"]], L[:, i % 2, 0:u["n"]], ACT.Exp, scale=-1.0,
                                     bias=neg_max[:, i % 4:i % 4 + 1],
                                     accum_out=den[:, (i // 8) % 2, u["slot"]:u["slot"] + 1]).then_inc(s["p_ready"], 1)
                    if i >= 1 and (i - 1) % 2 == 0:
                        pt_out(act, a, name, i - 1)

            def pt_out(eng, e, name, i):
                unit_of, _, (_, _, PT), base = ATT[name]
                n = unit_of(i)["n"]
                if i >= 2:
                    eng.wait_ge(s["pv_done"], base + i - 1)
                p = filled(eng, (name, "T", i))
                a.activation(PT[:, i % 2, 0:n], p[:, 0:n], ACT.Copy).then_inc(free((name, "T", i)), 1)

            evacuated(act, "vec")
            act.wait_ge(s["e_done"], 1)
            a.activation(c_act[:, :], vcol("c_2"), ACT.Silu).then_inc(s["c_act_done"], 1)
            norm(0)
            for n, name in enumerate(P1_ORDER):
                for t in range(NT):
                    if name == "rv":
                        p = filled(act, (name, t))
                        a.activation(rv_tok[:, t], p, ACT.Copy).then_inc(free((name, t)), 1)
                    if name == "rg":
                        p = filled(act, (name, t))
                        a.activation(rg_tok[:, t], p, ACT.Silu).then_inc(free((name, t)), 1)
                if name in ROPED:
                    for t in range(NT):
                        nb = 2 if name == "kk" else 4
                        p = filled(act, (name, "T", t))
                        a.activation(T1[name][:, :, t * P:(t + 1) * P], p[:, 0:nb * P].rearrange("p (k n) -> p k n", k=nb),
                                     ACT.Copy).then_inc(free((name, "T", t)), 1)
            i = 0
            for t in range(1, NT):
                n = (t + 1) * P
                for h in range(RH):
                    p = filled(act, ("index", t, h))
                    if i >= 2:
                        act.wait_ge(s["rel_used"], i - 1)
                    a.activation(rel[:, i % 2, 0:n], p[:, 0:n], ACT.Relu).then_inc(free(("index", t, h)), 1)
                    i += 1
            for h in range(RH):
                for m in range(NT):
                    n = S - m * P
                    o = [0, 512, 896, 1152][m]
                    if h >= 2 and m == 0:
                        act.wait_ge(s["ret_pv"], h - 1)
                    p = filled(act, ("ret_s", h, m))
                    a.activation(sT[:, h % 2, o:o + n], p[:, 0:n], ACT.Copy).then_inc(free(("ret_s", h, m)), 1)
            for t in range(NT):
                p = filled(act, ("ret_o", t))
                if t >= 1:
                    act.wait_ge(s["ret_rms"], t)
                a.activation(junk[:, 0:512], p, ACT.Square).then_inc(s["ret_square"], 1)
            act.wait_ge(s["ret_rms"], NT)
            a.activation(stat[:, 64:96], stat[:, 32:64], ACT.Sqrt, scale=1.0 / HD, bias=eps[:, :]).then_inc(s["ret_square"], 1)
            attention("dsa", None)
            in_t("mix1")
            post_rms(0, y1, tok_keys("mix1"))
            norm(1)
            ffn(0)
            post_rms(1, yf, down_keys(0))
            norm(2)
            for u in range(2):
                for j in range(4):
                    p = filled(act, ("hq", u, j))
                    a.activation(HQ[:, 4 * u + j], p, ACT.Silu).then_inc(free(("hq", u, j)), 1)
            for u in range(2):
                for t in range(NT):
                    p = filled(act, ("hg", u, t))
                    a.activation(sg_tok[:, t, u * 512:(u + 1) * 512], p, ACT.Silu).then_inc(free(("hg", u, t)), 1)
            for u in range(2):
                fa, fe, fl = f_work
                if u:
                    act.wait_ge(s["logf_done"], 4)
                for j in range(4):
                    p = filled(act, ("hf", u, j))
                    step(a.activation(fa[:, j * S:(j + 1) * S], p, ACT.Abs))
                after()
                step(a.activation(fe, fa, ACT.Exp, scale=-1.0))
                after()
                a.activation(fl, fe, ACT.Ln, bias=1.0).then_inc(s["f_abs"], 1)
                for j in range(4):
                    evacuated(act, ("hf", u, j))
                a.activation(HK[:, 4 * u:4 * u + 4], HK[:, 4 * u:4 * u + 4], ACT.Exp).then_inc(s["k_done"], 1)
            for u in range(2):
                for t in range(NT):
                    p = filled(act, ("hi", u, t))
                    a.activation(v_tok[:, t, u * 512:(u + 1) * 512], p, ACT.Copy).then_inc(free(("hi", u, t)), 1)
            for h in range(HH + 1):
                if h < HH:
                    G = HG[:, h].rearrange("p (t n) -> p t n", t=NT)
                    act.wait_ge(s["d_sub"], 2 * LEVELS * (h + 1))
                    a.activation(lvl[h % 2], lvl[h % 2], ACT.Exp).then_inc(s["d_exp"], 1)
                    if h >= 1:
                        filled(act, ("far", h - 1, 1))
                        act.wait_ge(s["q1_done"], 4 * h)
                    a.activation(q1[:, 0:2], G[:, 1:3], ACT.Exp).then_inc(s["eq_done"], 1)
                    a.activation(q1[:, 3], G[:, 3], ACT.Exp).then_inc(s["eq_done"], 1)
                    act.wait_ge(s["tabs_done"], h + 1)
                    a.activation(q1[:, 2], G[:, 3], ACT.Exp, bias=G[:, 2, P - 1:P]).then_inc(s["eq_done"], 1)
                    for t in range(3):
                        a.activation(k1[:, t], G[:, t], ACT.Exp, scale=-1.0, bias=G[:, t, P - 1:P]).then_inc(s["eq_done"], 1)
                    a.activation(k1[:, 3], G[:, 0], ACT.Exp, scale=-1.0, bias=tot[:, 0:1]).then_inc(s["eq_done"], 1)
                if h >= 1:
                    if h >= 3:
                        filled(act, ("ho", h - 3))
                    p0 = filled(act, ("far", h - 1, 0))
                    a.activation(attn[:, (h - 1) % 2, 0, P:S], p0[:, 0:3 * P], ACT.Copy).then_inc(free(("far", h - 1, 0)), 1)
                    p1 = filled(act, ("far", h - 1, 1))
                    a.activation(attn[:, (h - 1) % 2, 1, 2 * P:S], p1[:, 0:2 * P], ACT.Copy)
                    a.activation(attn[:, (h - 1) % 2, 2, 3 * P:S], p1[:, 2 * P:3 * P], ACT.Copy).then_inc(free(("far", h - 1, 1)), 1)
            for h in range(HH):
                for t in range(NT):
                    evacuated(act, ("ho", h))
                    step(a.activation(junk[:, 0:P], v_tok[:, t, h * P:(h + 1) * P], ACT.Square,
                                            accum_out=stat[:, 96 + 8 * t + h:97 + 8 * t + h]))
                    after()
            a.activation(stat[:, 128:160], stat[:, 96:128], ACT.Sqrt, scale=1.0 / P, bias=eps[:, :]).then_inc(s["ho_rms"], 1)
            in_t("mix2")
            norm(3)
            ffn(1)
            norm(4)
            for u in range(2):
                for t in range(NT):
                    p = filled(act, ("kvs", u, t))
                    a.activation(v_nsa[:, t, u], p[:, 256:512], ACT.Copy).then_inc(s["kvraw"], 1)
                    a.activation(raw[:, t, 16 + 4 * u:20 + 4 * u], p[:, 0:256].rearrange("p (h d) -> p h d", h=4), ACT.Copy)\
                        .then_inc(free(("kvs", u, t)), 1)
            for u in range(2):
                for t in range(NT):
                    p = filled(act, ("nq", u, t))
                    a.activation(raw[:, t, 8 * u:8 * u + 8], p.rearrange("p (h d) -> p h d", h=8), ACT.Copy)\
                        .then_inc(free(("nq", u, t)), 1)
            for t in range(NT):
                p = filled(act, ("nq", 2, t))
                a.activation(gates_e[:, t], p[:, 0:48], ACT.Exp, scale=-1.0).then_inc(free(("nq", 2, t)), 1)
            for kv in range(2):
                act.dma_start(w2_sb[:, kv], io["cmp_w2_2"][kv].rearrange("(n p) d -> p n d", p=P)).then_inc(s["w2_in"], 16)
            act.wait_ge(s["raw_done"], 3 * NT)
            a.activation(stat[:, 128:224], stat[:, 32:128], ACT.Sqrt, scale=1.0 / HD, bias=eps[:, :]).then_inc(s["raw_rms"], 1)
            for kv in range(2):
                for n in range(2):
                    p = filled(act, ("cmp1", kv, n))
                    a.activation(h1[:, kv, n], p[:, 0:4 * NCMP].rearrange("p (h i) -> p h i", h=4), ACT.Silu)\
                        .then_inc(free(("cmp1", kv, n)), 1)
            act.wait_ge(s["cmp_sq"], 1)
            a.activation(stat[0:NCMP, 248:252], stat[0:NCMP, 244:248], ACT.Sqrt, scale=1.0 / HD, bias=eps[0:NCMP, :]).then_inc(s["cmp_rms"], 1)
            for t in range(NT):
                for j in range(0, 5, 2):
                    p = filled(act, ("nT", t, j))
                    dst = [qn_t[:, 0:4], qn_t[:, 4:8], qr_t[:, 0:4], qr_t[:, 4:8], k_t][j]
                    a.activation(dst[:, :, t * P:(t + 1) * P], p.rearrange("p (k n) -> p k n", k=4), ACT.Copy)\
                        .then_inc(free(("nT", t, j)), 1)
            for i in range(len(GROUPS) + 1):
                if i < len(GROUPS):
                    act.wait_ge(s["cmp_l"], i + 1)
                    if i >= 2:
                        filled(act, ("cT", i - 2, 1))
                    a.activation(cp[:, i % 2], cl[:, i % 2], ACT.Exp, scale=SCALE).then_inc(s["cmp_p"], 1)
                if i >= 1:
                    if i >= 3:
                        filled(act, ("cO", i - 3))
                    for q in range(2):
                        p = filled(act, ("cT", i - 1, q))
                        a.activation(cpt[:, (i - 1) % 2, 4 * q:4 * q + 4], p[0:NCMP, :].rearrange("p (g n) -> p g n", g=4),
                                     ACT.Copy).then_inc(free(("cT", i - 1, q)), 1)
            attention("nsa", None)
            in_t("mix3")
            norm(5)
            ffn(2)
            for t in range(NT):
                act.wait_ge(s["x_ready"], 5 * NT + t + 1)
                act.dma_start(out[0, t * P:(t + 1) * P, :], x_tok[:, t]).then_inc(s["out_done"], 16)
            act.wait_ge(s["out_done"], 16 * NT)

        @block.vector
        def _(dve):
            v = nc.vector
            step, after = own_order(dve, s["dve_step"])

            def bcast(ap, shape):
                return ap.broadcast_to(shape)

            def norm(i):
                dve.wait_ge(s["norm_rms"], i + 1)
                step(v.reciprocal(stat[:, 8:12], stat[:, 4:8]))
                after()
                for t in range(NT):
                    v.tensor_scalar(XN[i][:, t], x_tok[:, t], stat[:, 8 + t:9 + t], None, ALU.mult).then_inc(s["xn_ready"], 1)
                if i in FFN_NORM:
                    for kt in range(KT):
                        evacuated(dve, ("xT", i, kt))
                        v.tensor_copy(x_hi[:, kt], ftmp[:, kt % 4]).then_inc(s["whole_done"], 1)
                        dve.wait_ge(s["whole_done"], KT * FFN_NORM[i] + kt + 1)
                        v.tensor_tensor(x_lo[:, kt], ftmp[:, kt % 4], x_hi[:, kt].bitcast(F32), ALU.subtract)\
                            .then_inc(s["x_split"], 1)
                    return
                for kt in range(1, KT, 2):
                    p = filled(dve, ("xT", i, kt))
                    outs = NORM_OUT[i]
                    if i >= 2:
                        dve.wait_ge(s["mod_ready"], MOD_READY[NORM_MOD[i]])
                    for j, (dst, gain, shift) in enumerate(outs):
                        if shift is None:
                            ins = v.tensor_scalar(dst[:, kt], p, gain[:, kt:kt + 1], None, ALU.mult)
                        else:
                            ins = v.tensor_scalar(dst[:, kt], p, gain[:, kt:kt + 1], shift[:, kt:kt + 1], ALU.mult, ALU.add)
                        if j == len(outs) - 1:
                            ins.then_inc(free(("xT", i, kt)), 1)

            def post_norm(stage, i, y, keys):
                for half, t, key in keys:
                    p = filled(dve, key)
                    v.tensor_copy(y[:, t, half * HALF:(half + 1) * HALF], p).then_inc(free(key), 1)
                dve.wait_ge(s["y_rms"], i + 1)
                step(v.reciprocal(stat[:, 24:28], stat[:, 20:24]))
                after()
                dve.wait_ge(s["row_in"], 32)
                for t in range(NT):
                    v.scalar_tensor_tensor(y[:, t], y[:, t], stat[:, 24 + t:25 + t], row[:, i], ALU.mult, ALU.mult)\
                        .then_inc(s["y_scaled"], 1)

            def post_gate(stage, m, y, keys):
                for half, t, key in keys:
                    p = filled(dve, key)
                    evacuated(dve, ("ada", m, 4 + half))
                    v.tensor_tensor(y[:, t, half * HALF:(half + 1) * HALF], p, row[:, m % 2, half * HALF:(half + 1) * HALF],
                                    ALU.mult).then_inc(free(key), 1)

            def in_t(name):
                for kt in range(1, KT, 2):
                    p = filled(dve, (name, "T", kt))
                    v.tensor_copy(h_t[:, kt], p).then_inc(free((name, "T", kt)), 1)

            def ada_sum(m, j):
                n = ADA_N[(m, j)]
                w = arrived(dve, ("ada", m, j), (0,)).rearrange("p (k n) -> p k n", k=KT)
                acc = ada_acc[:, n % 2]
                if n >= 2:
                    filled(dve, ("ada",) + ADA[n - 2])
                step(v.tensor_scalar(acc, w[:, 0], c_act[:, 0:1], None, ALU.mult))
                for k in range(1, KT):
                    after()
                    ins = v.scalar_tensor_tensor(acc, w[:, k], c_act[:, k:k + 1], acc, ALU.mult, ALU.add)
                    if k == 3:
                        ins.then_inc(s["acc_half"], 1)
                        dve.wait_ge(s["acc_half"], n + 1)
                        arrived(dve, ("ada", m, j), (1,))
                    elif k < KT - 1:
                        step(ins)
                ins.then_inc(s["acc_done"], 1)

            def ada_out(m, j):
                p = filled(dve, ("ada", m, j))
                if j >= 4:
                    dve.wait_ge(s[f"gate_row_in{m % 2}"], 16 * (m // 2 + 1))
                    r = row[:, m % 2, (j - 4) * HALF:(j - 3) * HALF]
                    v.tensor_tensor(r, p, r, ALU.add).then_inc(free(("ada", m, j)), 1)
                    return
                after()
                prod = junk2.rearrange("p (k n) -> p k n", k=4)
                step(v.tensor_tensor(prod, p.rearrange("p (k n) -> p k n", k=4), bcast(ident.unsqueeze(1), [P, 4, P]), ALU.mult))
                after()
                raw_col = stat[:, 224 + 4 * (j % 2):228 + 4 * (j % 2)]
                v.tensor_reduce(raw_col, prod, AX, ALU.add).then_inc(free(("ada", m, j)), 1)
                evacuated(dve, ("ada", m, j))
                dst = mod[:, m, 1, 4 * j:4 * j + 4] if j < 2 else raw_col
                step(v.tensor_tensor(dst, raw_col, vec[:, BIAS + 24 * m + 4 * j:BIAS + 24 * m + 4 * j + 4], ALU.add))
                after()
                if j >= 2:
                    ins = v.scalar_tensor_tensor(mod[:, m, 0, 4 * (j - 2):4 * (j - 1)], raw_col, 1.0,
                                                 MOD_GAIN[m][:, 4 * (j - 2):4 * (j - 1)], ALU.add, ALU.mult)
                    if j == 3:
                        ins.then_inc(s["mod_ready"], 1)
                    else:
                        step(ins)

            def low(key, src):
                n = split_at[key]
                dve.wait_ge(s["hi_done"], n + 1)
                v.tensor_tensor(w_lo[:, n % 2], src, w_hi[:, n % 2].bitcast(F32), ALU.subtract).then_inc(s["lo_done"], 1)

            def up_out(i, u):
                for q in range(4):
                    if i:
                        continue
                    n = 22 * (q // 2) + 2 * u + q % 2
                    buf = ftmp[:, 4 * (u % 2) + q]
                    dve.wait_ge(s["conv_pre"], 4 * u + q + 1)
                    p = filled(dve, ("up", i, u, q))
                    step(v.scalar_tensor_tensor(buf[:, 1:S], p[:, 0:S - 1], vec[:, CONV + 44 + n:CONV + 45 + n],
                                                buf[:, 1:S], ALU.mult, ALU.add))
                    after()
                    v.scalar_tensor_tensor(buf[:, 2:S], p[:, 0:S - 2], vec[:, CONV + n:CONV + 1 + n],
                                           buf[:, 2:S], ALU.mult, ALU.add).then_inc(free(("up", i, u, q)), 1)
                for q in range(2):
                    gate, value = ftmp[:, 4 * (u % 2) + q], ftmp[:, 4 * (u % 2) + 2 + q]
                    if i == 0:
                        dve.wait_ge(s["hid_gate"], 2 * u + q + 1)
                        evacuated(dve, ("up", i, u, 2 + q))
                        v.tensor_tensor(hid[:, 2 * u + q], gate, value, ALU.mult).then_inc(s["hid_done"], 1)
                    else:
                        evacuated(dve, ("up", i, u, q))
                        p = filled(dve, ("up", i, u, 2 + q))
                        v.tensor_tensor(hid[:, 2 * u + q], gate, p, ALU.mult).then_inc(free(("up", i, u, 2 + q)), 1)

            def ffn(i):
                for u in range(FFN_UNITS):
                    w = arrived(dve, ("up", i, u), (0,))
                    for q in range(2):
                        low(("up", i, u, q), w[:, q * PIECE:(q + 1) * PIECE])
                    if u:
                        up_out(i, u - 1)
                    arrived(dve, ("up", i, u), (1,))
                    for q in range(2, 4):
                        low(("up", i, u, q), w[:, q * PIECE:(q + 1) * PIECE])
                    for mj in ada_after.get((i, u - 2), []):
                        ada_out(*mj)
                    for mj in ada_after.get((i, u), []):
                        ada_sum(*mj)
                up_out(i, FFN_UNITS - 1)
                for u in (FFN_UNITS - 2, FFN_UNITS - 1):
                    for mj in ada_after.get((i, u), []):
                        ada_out(*mj)
                for g, (k0, n) in enumerate(down_groups):
                    w = arrived(dve, ("down", i, g), (0,))
                    for k in range(k0, k0 + n):
                        if k == k0 + n // 2:
                            arrived(dve, ("down", i, g), (1,))
                        low(("down", i, k), in_halves(w, n // 2, PIECE)[:, (k - k0) // (n // 2), (k - k0) % (n // 2)])
                        dve.wait_ge(s["hid_hi"], FT * i + k + 1)
                        v.tensor_tensor(hid_lo[:, k % 4], hid[:, k], hid_hi[:, k % 4].bitcast(F32), ALU.subtract)\
                            .then_inc(s["x_split"], 1)
                    for mj in ada_down.get(i, [])[g:g + 1]:
                        ada_sum(*mj)

            def rope(src, t, a, b, heads, read=None):
                cos, sin, nsin = [rope_t[:, i, t] for i in range(3)]
                sv = src.rearrange("p (h q d) -> p h q d", h=heads, q=2)
                av = a.rearrange("p (h q d) -> p h q d", h=heads, q=2)
                bv = b.rearrange("p (h q d) -> p h q d", h=heads, q=2)
                step(v.tensor_tensor(av, sv, bcast(cos.unsqueeze(1).unsqueeze(1), [P, heads, 2, HD // 2]), ALU.mult))
                step(v.tensor_tensor(bv[:, :, 0], sv[:, :, 1], bcast(nsin.unsqueeze(1), [P, heads, HD // 2]), ALU.mult))
                ins = v.tensor_tensor(bv[:, :, 1], sv[:, :, 0], bcast(sin.unsqueeze(1), [P, heads, HD // 2]), ALU.mult)
                if read is None:
                    step(ins)
                else:
                    ins.then_inc(free(read), 1)
                    evacuated(dve, read)
                after()

            def raw_squares(t, h0):
                w = raw[:, t, h0:h0 + 8, :]
                sq = junk[:, 0:HALF].rearrange("p (h d) -> p h d", h=8)
                step(v.tensor_tensor(sq, w, w, ALU.mult))
                after()
                v.tensor_reduce(stat[:, 32 + 24 * t + h0:40 + 24 * t + h0], sq, AX, ALU.add).then_inc(s["raw_done"], 1)
                raw_sums[0] += 1
                dve.wait_ge(s["raw_done"], raw_sums[0])

            raw_sums = [0]

            def attention(name, bias_ready, finish):
                unit_of, n_units, (L, PB, PT), base = ATT[name]
                for i in range(n_units + 3):
                    if i < n_units:
                        u = unit_of(i)
                        bias_ready(i)
                        p = filled(dve, (name, "S", i))
                        if i >= 2:
                            dve.wait_ge(s["p_ready"], base + i - 1)
                        v.tensor_tensor_reduce(L[:, i % 2, 0:u["n"]], p[:, 0:u["n"]], u["bias"], -SCALE, 3e38,
                                               ALU.add, ALU.min, neg_max[:, i % 4:i % 4 + 1]).then_inc(free((name, "S", i)), 1)
                    if 1 <= i <= n_units and (i - 1) % 2 == 1:
                        j = i - 1
                        if j >= 2:
                            dve.wait_ge(s["pv_done"], base + j - 1)
                        n = unit_of(j)["n"]
                        pt = filled(dve, (name, "T", j))
                        v.tensor_copy(PT[:, j % 2, 0:n], pt[:, 0:n]).then_inc(free((name, "T", j)), 1)
                    if i >= 3 and (i - 3) % 8 == 7:
                        finish((i - 3) // 8, base)

            v.memset(eps[:, :], EPS).then_inc(s["e_done"], 1)
            p = filled(dve, "vec")
            v.tensor_copy(vec[:, :], p[:, 0:416]).then_inc(free("vec"), 1)
            dve.wait_ge(s["consts_in"], 32)
            step(v.tensor_copy(masks[:, :, :], mask_rows))
            dve.wait_ge(s["c_act_done"], 1)
            norm(0)
            n = 0
            for name in ROPED:
                for t in range(NT):
                    p = filled(dve, (name, t))
                    if n >= 2:
                        pn, pt = ROPED[(n - 2) // NT], (n - 2) % NT
                        filled(dve, (pn, "T", pt))
                    a, b, o = rope_a[:, n % 2], rope_b[:, n % 2], rope_o[:, n % 2]
                    if name == "kk":
                        step(v.tensor_copy(av_tok[:, t], p[:, 64:128]))
                        step(v.tensor_scalar(iw[:, t], p[:, 192:200], (RH * HD) ** -0.5, None, ALU.mult))
                        for j, c in enumerate((0, 128)):
                            rope(p[:, c:c + 64], t, a[:, 64 * j:64 * j + 64], b[:, 64 * j:64 * j + 64], 1, (name, t) if j else None)
                        av = a[:, 0:128].rearrange("p (j d) -> p j d", j=2).unsqueeze(2)
                        bv = b[:, 0:128].rearrange("p (j d) -> p j d", j=2).unsqueeze(2)
                        v.tensor_tensor(o[:, 0:256].rearrange("p (j q d) -> p j q d", j=2, q=2), bcast(av, [P, 2, 2, HD]),
                                        bcast(bv, [P, 2, 2, HD]), ALU.add).then_inc(s["rope_done"], 1)
                    else:
                        rope(p, t, a, b, 8, (name, t))
                        v.tensor_tensor(o, a, b, ALU.add).then_inc(s["rope_done"], 1)
                    n += 1
            i = 0
            for t in range(1, NT):
                n = (t + 1) * P
                w = isc[:, t - 1, 0:n]
                for h in range(RH):
                    evacuated(dve, ("index", t, h))
                    if h:
                        dve.wait_ge(s["rel_used"], i)
                        v.scalar_tensor_tensor(w, rel[:, i % 2, 0:n], iw[:, t, h:h + 1], w, ALU.mult, ALU.add).then_inc(s["rel_used"], 1)
                    else:
                        v.tensor_scalar(w, rel[:, i % 2, 0:n], iw[:, t, h:h + 1], None, ALU.mult).then_inc(s["rel_used"], 1)
                    i += 1
                dve.wait_ge(s["rel_used"], i)
                step(v.tensor_tensor(w[:, t * P:n], w[:, t * P:n], strip[:, 3 * P:], ALU.add))
                after()
            for t in range(1, NT):
                n = (t + 1) * P
                w = isc[:, t - 1, 0:n]
                for r in range(TOPK // 8):
                    step(v.max(best[:, :], w))
                    after()
                    step(v.match_replace(w, best[:, :], w, REPLACED))
                    after()
                v.tensor_scalar(sel_bias[:, t - 1, 0:n], w, REPLACED / 2, NEG, ALU.is_ge, ALU.mult).then_inc(s["picked"], 1)
            for t in range(NT):
                dve.wait_ge(s["ret_square"], t + 1)
                v.tensor_reduce(stat[:, 32 + 8 * t:40 + 8 * t], junk[:, 0:512].rearrange("p (h d) -> p h d", h=RH), AX, ALU.add)\
                    .then_inc(s["ret_rms"], 1)
            dve.wait_ge(s["ret_square"], NT + 1)
            step(v.reciprocal(stat[:, 96:128], stat[:, 64:96]))
            after()
            for t in range(NT):
                p = filled(dve, ("ret_o", t))
                v.tensor_tensor(mixed[:, t, 0:512].rearrange("p (h d) -> p h d", h=RH), p.rearrange("p (h d) -> p h d", h=RH),
                                bcast(stat[:, 96 + 8 * t:104 + 8 * t].unsqueeze(2), [P, RH, HD]), ALU.mult)\
                    .then_inc(free(("ret_o", t)), 1)

            def dsa_bias(i):
                if i % RH == 0 and i // RH >= 1:
                    dve.wait_ge(s["picked"], i // RH)

            def dsa_finish(g, base):
                dve.wait_ge(s["p_ready"], base + 8 * (g + 1))
                dve.wait_ge(s["pv_done"], base + 8 * (g + 1))
                step(v.reciprocal(rden[:, g % 2], den[:, g % 2]))
                after()
                p = ps[:, bank_use[("dsa", "O", g)][0]]
                v.tensor_tensor(mixed[:, g, 512:1024].rearrange("p (h d) -> p h d", h=RH), p.rearrange("p (h d) -> p h d", h=RH),
                                bcast(rden[:, g % 2].unsqueeze(2), [P, RH, HD]), ALU.mult).then_inc(free(("dsa", "O", g)), 1)

            attention("dsa", dsa_bias, dsa_finish)
            in_t("mix1")
            post_norm(0, 0, y1, tok_keys("mix1"))
            norm(1)
            ffn(0)
            post_norm(1, 1, yf, down_keys(0))
            for mj in ada_down[0]:
                ada_out(*mj)
            norm(2)
            for u in range(2):
                for j in range(4):
                    fl = f_work[2][:, j * S:(j + 1) * S]
                    dve.wait_ge(s["f_abs"], u + 1)
                    p = filled(dve, ("hf", u, j))
                    h = 4 * u + j
                    v.scalar_tensor_tensor(HG[:, h], p, 0.0, fl, ALU.min, ALU.subtract).then_inc(s["logf_done"], 1)
                    dve.wait_ge(s["logf_done"], h + 1)
                    v.tensor_tensor(HK[:, h], HG[:, h], p, ALU.subtract).then_inc(free(("hf", u, j)), 1)
            for h in range(HH):
                v.tensor_tensor_scan(HG[:, h], keep, HG[:, h], 0.0, ALU.mult, ALU.add).then_inc(s["g_done"], 1)

            def attn_diag(h, lv):
                p = filled(dve, ("diag", h, lv))
                if h >= 2 and lv == 0:
                    filled(dve, ("ho", h - 2))
                A = attn[:, h % 2].rearrange("p s n -> p (s n)")
                dst = bass.AP(A.tensor, A.offset, [A.ap[0], [S + P, NT], [1, P]])
                m = bcast(masks[:, lv, :].unsqueeze(1), [P, NT, P])
                evacuated_prev(h, lv)
                v.copy_predicated(dst, m, p.rearrange("p (s n) -> p s n", s=NT)).then_inc(free(("diag", h, lv)), 1)

            def evacuated_prev(h, lv):
                if lv:
                    evacuated(dve, ("diag", h, lv - 1))

            for h in range(HH + 1):
                if h < HH:
                    dve.wait_ge(s["g_done"], h + 1)
                    G = HG[:, h].rearrange("p (t n) -> p t n", t=NT)
                    if h:
                        dve.wait_ge(s["eq_done"], 7 * h)
                    v.tensor_tensor(tot[:, 0:1], G[:, 0, P - 1:P], G[:, 1, P - 1:P], ALU.add).then_inc(s["tabs_done"], 1)
                    dve.wait_ge(s["d_exp"], h + 1)
                    dve.wait_ge(s["k_done"], 2)
                    L = lvl[h % 2]
                    for lv in range(LEVELS):
                        c = 1 << lv
                        for q, src in ((0, HK), (1, HQ)):
                            d = L[:, lv].rearrange("p (b q c) -> p b q c", q=2, c=c)[:, :, q]
                            w = src[:, h].rearrange("p (b q c) -> p b q c", q=2, c=c)[:, :, q]
                            v.tensor_tensor(d, d, w, ALU.mult).then_inc(s["qk_done"], 1)
                    dve.wait_ge(s["eq_done"], 7 * (h + 1))
                    K = HK[:, h].rearrange("p (t n) -> p t n", t=NT)
                    Q = HQ[:, h].rearrange("p (t n) -> p t n", t=NT)
                    v.tensor_tensor(q1[:, 0:2], q1[:, 0:2], Q[:, 1:3], ALU.mult).then_inc(s["q1_done"], 1)
                    v.tensor_tensor(q1[:, 2:4], q1[:, 2:4], bcast(Q[:, 3:4], [P, 2, P]), ALU.mult).then_inc(s["q1_done"], 1)
                    v.tensor_tensor(k1[:, 0:3], k1[:, 0:3], K[:, 0:3], ALU.mult).then_inc(s["q1_done"], 1)
                    v.tensor_tensor(k1[:, 3], k1[:, 3], K[:, 0], ALU.mult).then_inc(s["q1_done"], 1)
                    dve.wait_ge(s["attn_zero"], 1)
                    for lv in range(LEVELS + 1):
                        attn_diag(h, lv)
                if h >= 1:
                    p = filled(dve, ("ho", h - 1))
                    v.tensor_copy(v_tok[:, :, (h - 1) * P:h * P], p.rearrange("p (t n) -> p t n", t=NT)).then_inc(free(("ho", h - 1)), 1)
            dve.wait_ge(s["ho_rms"], 1)
            step(v.reciprocal(stat[:, 160:192], stat[:, 128:160]))
            after()
            dve.wait_ge(s["sg_done"], 8)
            for t in range(NT):
                w = v_tok[:, t].rearrange("p (h d) -> p h d", h=HH)
                v.tensor_tensor(w, w, bcast(stat[:, 160 + 8 * t:168 + 8 * t].unsqueeze(2), [P, HH, P]), ALU.mult).then_inc(s["ho_scaled"], 1)
            in_t("mix2")
            post_gate(2, 0, y2, tok_keys("mix2"))
            norm(3)
            ffn(1)
            post_gate(3, 1, yf, down_keys(1))
            for mj in ada_down[1]:
                ada_out(*mj)
            norm(4)
            for j in range(4):
                p = filled(dve, ("kvc", j))
                for q in range(2):
                    for par in range(2):
                        d = slice(64 * par, 64 * par + 64)
                        w = p[64 * q:64 * q + 64, :]
                        src = bass.AP(w.tensor, w.offset + par, [w.ap[0], [2, 16], [16, NCMP]])
                        pos = vec[d, POS + 32 * (j // 2):POS + 32 * (j // 2) + 32].rearrange("p (r e) -> p r e", e=2)[:, :, par:par + 1]
                        ins = v.tensor_tensor(win[d, j // 2, :, 2 * (j % 2) + q, :], src, bcast(pos, [64, 16, NCMP]), ALU.add)
                        if (q, par) == (1, 1):
                            ins.then_inc(free(("kvc", j)), 1)
                        else:
                            ins.then_inc(s["u_done"], 1)
            for u in range(2):
                for t in range(NT):
                    evacuated(dve, ("kvs", u, t))
                    if u == 1:
                        raw_squares(t, 16)
            for u in range(2):
                for t in range(NT):
                    evacuated(dve, ("nq", u, t))
                    raw_squares(t, 8 * u)
            for t in range(NT):
                evacuated(dve, ("nq", 2, t))
            step(v.tensor_scalar(gates_e[:, :, :], gates_e[:, :, :], 1.0, None, ALU.add))
            after()
            step(v.reciprocal(gates[:, :, :], gates_e[:, :, :]))
            dve.wait_ge(s["raw_rms"], 1)
            step(v.reciprocal(stat[:, 32:128], stat[:, 128:224]))
            after()
            p = filled(dve, "cmp2")
            step(v.tensor_copy(kc_raw, p[0:NCMP, 0:256]))
            v.tensor_copy(vc_tok[0:NCMP, :, :], p[0:NCMP, 256:512].rearrange("p (h d) -> p h d", h=4)).then_inc(free("cmp2"), 1)
            after()
            step(v.tensor_tensor(kc_tok, kc_raw.rearrange("p (h d) -> p h d", h=4), kc_raw.rearrange("p (h d) -> p h d", h=4), ALU.mult))
            after()
            v.tensor_reduce(stat[0:NCMP, 244:248], kc_tok, AX, ALU.add).then_inc(s["cmp_sq"], 1)
            dve.wait_ge(s["cmp_rms"], 1)
            step(v.reciprocal(stat[0:NCMP, 252:256], stat[0:NCMP, 248:252]))
            after()
            step(v.tensor_tensor(kc_tok, kc_raw.rearrange("p (h d) -> p h d", h=4),
                                       bcast(stat[0:NCMP, 252:256].unsqueeze(2), [NCMP, 4, HD]), ALU.mult))
            after()
            dve.wait_ge(s["cmp_pos_in"], 64)
            v.tensor_tensor(kc_tok, kc_tok, bcast(cmp_norm[0:NCMP, :].unsqueeze(1), [NCMP, 4, HD]), ALU.mult).then_inc(s["cmp_tok"], 1)
            p = filled(dve, "cmpT")
            v.tensor_copy(kc_t[:, :, 0:NCMP], p[:, 0:64].rearrange("p (c i) -> p c i", c=2)[:, :, 0:NCMP]).then_inc(free("cmpT"), 1)
            for t in range(NT):
                for j in range(3):
                    i = 3 * t + j
                    if i >= 2:
                        filled(dve, ("nT", (i - 2) // 3, 2 + (i - 2) % 3))
                    a = n_a[:, i % 2]
                    if j < 2:
                        for ko in range(2):
                            src = raw[:, t, 8 * j + 4 * ko:8 * j + 4 * ko + 4, :]
                            dst = a.rearrange("p (g q d) -> p g q d", g=4, q=2)[:, :, ko]
                            r = stat[:, 32 + 24 * t + 8 * j + 4 * ko:36 + 24 * t + 8 * j + 4 * ko]
                            ins = v.tensor_tensor(dst, src, bcast(r.unsqueeze(2), [P, 4, HD]), ALU.mult)
                            if ko == 0:
                                step(ins)
                        after()
                        ins.then_inc(s["raw_norm"], 1)
                    else:
                        r = stat[:, 48 + 24 * t:56 + 24 * t]
                        v.tensor_tensor(a.rearrange("p (h d) -> p h d", h=8), raw[:, t, 16:24, :], bcast(r.unsqueeze(2), [P, 8, HD]),
                                        ALU.mult).then_inc(s["raw_norm"], 1)
                    dve.wait_ge(s["gained"], i + 1)
                    rope(a, t, n_b[:, i % 2], n_o[:, i % 2], 8)
                    v.tensor_tensor(n_o[:, i % 2], n_b[:, i % 2], n_o[:, i % 2], ALU.add).then_inc(s["rope2_done"], 1)
                for j in (1, 3):
                    p = filled(dve, ("nT", t, j))
                    dst = [qn_t[:, 0:4], qn_t[:, 4:8], qr_t[:, 0:4], qr_t[:, 4:8], k_t][j]
                    v.tensor_copy(dst[:, :, t * P:(t + 1) * P], p.rearrange("p (k n) -> p k n", k=4)).then_inc(free(("nT", t, j)), 1)
            for i in range(len(GROUPS) + 2):
                if i < len(GROUPS):
                    t, kp = GROUPS[i]
                    L = cl[:, i % 2]
                    if i >= 2:
                        dve.wait_ge(s["cmp_p"], i - 1)
                    for q in range(2):
                        p = filled(dve, ("cS", i, q))
                        v.tensor_tensor(L[:, 4 * q:4 * q + 4], p[:, 0:128].rearrange("p (g c) -> p g c", g=4)[:, :, 0:NCMP],
                                        bcast(cmp_bias[:, t].unsqueeze(1), [P, 4, NCMP]), ALU.add).then_inc(free(("cS", i, q)), 1)
                    for q in range(2):
                        evacuated(dve, ("cS", i, q))
                    step(v.tensor_reduce(fac[:, 32:40], L, AX, ALU.max))
                    after()
                    v.tensor_tensor(L, L, bcast(fac[:, 32:40].unsqueeze(2), [P, 8, NCMP]), ALU.subtract).then_inc(s["cmp_l"], 1)
                if 1 <= i <= len(GROUPS):
                    t, kp = GROUPS[i - 1]
                    f = fac[:, 48 + 8 * ((i - 1) % 2):56 + 8 * ((i - 1) % 2)]
                    dve.wait_ge(s["cmp_p"], i)
                    step(v.tensor_reduce(fac[:, 40:48], cp[:, (i - 1) % 2], AX, ALU.add))
                    after()
                    step(v.reciprocal(fac[:, 40:48], fac[:, 40:48]))
                    after()
                    step(v.scalar_tensor_tensor(f, fac[:, 40:48], row_valid[:, t:t + 1], gates[:, t, 8 * kp:8 * kp + 8],
                                                      ALU.mult, ALU.mult))
                if i >= 2:
                    t, kp = GROUPS[i - 2]
                    f = fac[:, 48 + 8 * (i % 2):56 + 8 * (i % 2)]
                    p = filled(dve, ("cO", i - 2))
                    after()
                    v.tensor_tensor(nsa_tok[:, t, kp * 512:(kp + 1) * 512].rearrange("p (h d) -> p h d", h=8),
                                    p.rearrange("p (h d) -> p h d", h=8), bcast(f.unsqueeze(2), [P, 8, HD]), ALU.mult)\
                        .then_inc(free(("cO", i - 2)), 1)
            evacuated(dve, ("cO", len(GROUPS) - 1))
            evacuated(dve, ("cO", len(GROUPS) - 2))

            def nsa_finish(g, base):
                t, kp, br = NSA_GROUPS[g]
                dve.wait_ge(s["p_ready"], base + 8 * (g + 1))
                dve.wait_ge(s["pv_done"], base + 8 * (g + 1))
                step(v.reciprocal(rden[:, g % 2], den[:, g % 2]))
                after()
                step(v.tensor_tensor(rden[:, g % 2], rden[:, g % 2], gates[:, t, 16 + 16 * br + 8 * kp:24 + 16 * br + 8 * kp], ALU.mult))
                after()
                if g >= 2:
                    dve.wait_ge(s["nsa_added"], g - 1)
                p = ps[:, bank_use[("nsa", "O", g)][0]]
                v.tensor_tensor(n_tmp[:, g % 2].rearrange("p (h d) -> p h d", h=8), p.rearrange("p (h d) -> p h d", h=8),
                                bcast(rden[:, g % 2].unsqueeze(2), [P, 8, HD]), ALU.mult).then_inc(free(("nsa", "O", g)), 1)

            attention("nsa", lambda i: None, nsa_finish)
            for mj in ADA_LATE:
                ada_sum(*mj)
                ada_out(*mj)
            in_t("mix3")
            post_gate(4, 2, y3, tok_keys("mix3"))
            norm(5)
            ffn(2)
            post_gate(5, 3, yf, down_keys(2))

        @block.tensor
        def _(pe):
            mm = nc.tensor.matmul
            tr = nc.tensor.transpose

            pe.wait_ge(s["consts_in"], 32)
            pe.wait_ge(s["rows_in"], ROWS_IN)
            b = open_bank("vec")
            tr(b[:, 0:64], vec_rows, ident[0:64, 0:64])
            tr(b[:, 64:152], conv_rows[0], ident[0:88, 0:88])
            tr(b[:, 152:240], conv_rows[1], ident[0:88, 0:88])
            tr(b[:, 240:272], pos_rows[:, 0:128], ident[0:32, 0:32])
            tr(b[:, 272:304], pos_rows[:, 128:256], ident[0:32, 0:32])
            tr(b[:, 304:416], bias_rows, ident[0:112, 0:112]).then_inc(full("vec"), 1)

            def turn(src, key):
                b = open_bank(key)
                for t in range(NT):
                    ins = tr(b[:, t * P:(t + 1) * P], src(t), ident)
                ins.then_inc(full(key), 1)

            def norm(i):
                pe.wait_ge(s["xn_ready"], NT * (i + 1))
                for kt in range(KT):
                    turn(lambda t: XN[i][:, t, kt * P:(kt + 1) * P], ("xT", i, kt))
                if i in FFN_NORM:
                    pe.wait_ge(s["x_split"], (KT + FT) * FFN_NORM[i] + KT)
                    return
                for kt in range(KT):
                    evacuated(pe, ("xT", i, kt))

            def tok_bank(w, h, t, key, n):
                b = open_bank(key)
                for k in range(KT):
                    ins = mm(b[:, 0:n], h[:, k, t * P:(t + 1) * P], w[:, k // 4, k % 4, :], start=(k == 0), stop=(k == KT - 1))
                ins.then_inc(full(key), 1)

            def tok_gemm(name, h, n_units, width=lambda u: 512):
                for u in range(n_units):
                    n = width(u)
                    w = in_halves(arrived(pe, (name, u)), 4, n)
                    for t in range(NT):
                        tok_bank(w, h, t, (name, u, t), n)

            def feat_gemm(ukey, h, keys):
                w = arrived(pe, ukey)[:, 0:KT * 512].rearrange("p (k n) -> p k n", k=KT)
                for j, key in enumerate(keys):
                    b = open_bank(key)
                    for k in range(KT):
                        ins = mm(b, w[:, k, j * P:(j + 1) * P], h[:, k, :], start=(k == 0), stop=(k == KT - 1))
                    ins.then_inc(full(key), 1)

            def ada_row(m, j):
                pe.wait_ge(s["acc_done"], ADA_N[(m, j)] + 1)
                pe.wait_ge(s["ones_done"], 1)
                b = open_bank(("ada", m, j))
                mm(b, ones[:, :], ada_acc[:, ADA_N[(m, j)] % 2], start=True, stop=True).then_inc(full(("ada", m, j)), 1)

            def ffn(i):
                for u in range(FFN_UNITS):
                    keys = [("up", i, u, j) for j in range(4)]
                    bs = [open_bank(key) for key in keys]
                    for q in range(4):
                        n = split_at[("up", i, u, q)]
                        pe.wait_ge(s["lo_done"], n + 1)
                        wh, wl = [w[:, n % 2].rearrange("p (k n) -> p k n", k=2) for w in (w_hi, w_lo)]
                        for j in range(4):
                            c = slice(j * P, (j + 1) * P)
                            for k in range(2):
                                first, last = (q, k) == (0, 0), (q, k) == (3, 1)
                                mm(bs[j], wh[:, k, c], x_hi[:, 2 * q + k], start=first, stop=False)
                                mm(bs[j], wh[:, k, c], x_lo[:, 2 * q + k], start=False, stop=False)
                                ins = mm(bs[j], wl[:, k, c], x_hi[:, 2 * q + k], start=False, stop=last)
                            if q == 3 and j < 3:
                                ins.then_inc(full(keys[j]), 1)
                        if q < 3:
                            ins.then_inc(s["piece_done"], 1)
                    ins.then_inc(full(keys[3]), 1)
                    for mj in ada_after.get((i, u - 1), []):
                        ada_row(*mj)
                for mj in ada_after.get((i, FFN_UNITS - 1), []):
                    ada_row(*mj)
                bs = [open_bank(("down", i, j)) for j in range(8)]
                for k in range(FT):
                    n = split_at[("down", i, k)]
                    pe.wait_ge(s["lo_done"], n + 1)
                    pe.wait_ge(s["x_split"], (KT + FT) * i + KT + k + 1)
                    for t in range(NT):
                        c = slice(t * P, (t + 1) * P)
                        for half in range(2):
                            f = slice(half * HALF, (half + 1) * HALF)
                            b = bs[2 * t + half]
                            mm(b, hid_hi[:, k % 4, c], w_hi[:, n % 2, f], start=(k == 0), stop=False)
                            mm(b, hid_hi[:, k % 4, c], w_lo[:, n % 2, f], start=False, stop=False)
                            ins = mm(b, hid_lo[:, k % 4, c], w_hi[:, n % 2, f], start=False, stop=(k == FT - 1))
                            if k == FT - 1:
                                ins.then_inc(full(("down", i, 2 * t + half)), 1)
                    if k < FT - 1:
                        ins.then_inc(s["piece_done"], 1)
                for mj in ada_down.get(i, []):
                    ada_row(*mj)

            def attention(name, ready):
                unit_of, n_units, (L, PB, PT), base = ATT[name]
                for i in range(n_units + 2):
                    if i < n_units:
                        u = unit_of(i)
                        b = open_bank((name, "S", i))
                        mm(b[:, 0:u["n"]], u["q"], u["k"], start=True, stop=True).then_inc(full((name, "S", i)), 1)
                    if 1 <= i <= n_units:
                        u = unit_of(i - 1)
                        pe.wait_ge(s["p_ready"], base + i)
                        b = open_bank((name, "T", i - 1))
                        for c in range(u["n"] // P):
                            ins = tr(b[:, c * P:(c + 1) * P], PB[:, (i - 1) % 2, c * P:(c + 1) * P], ident)
                        ins.then_inc(full((name, "T", i - 1)), 1)
                    if i >= 2:
                        j = i - 2
                        u = unit_of(j)
                        okey = (name, "O", j // 8)
                        b = open_bank(okey) if j % 8 == 0 else ps[:, bank_use[okey][0]]
                        evacuated(pe, (name, "T", j))
                        nb = u["n"] // P
                        for c in range(nb):
                            ins = mm(b[:, u["slot"] * HD:(u["slot"] + 1) * HD], PT[:, j % 2, c * P:(c + 1) * P], u["v"](c),
                                     start=(c == 0), stop=(c == nb - 1))
                        ins.then_inc(s["pv_done"], 1)

            def out_gemm(name, src, wait):
                wait()
                for kt in range(KT):
                    turn(lambda t: src[:, t, kt * P:(kt + 1) * P], (name, "T", kt))
                for kt in range(KT):
                    evacuated(pe, (name, "T", kt))
                tok_gemm(name, h_t, 2)

            norm(0)
            lagged = []
            n_roped = 0
            for name in P1_ORDER:
                n = sum(c for _, c in P1[name])
                w = in_halves(arrived(pe, name), 4, n)
                for t in range(NT):
                    tok_bank(w, h_t, t, (name, t), n)
                    if lagged:
                        ln, lt = lagged.pop(0)
                        i = n_roped
                        n_roped += 1
                        pe.wait_ge(s["rope_done"], i + 1)
                        b = open_bank((ln, "T", lt))
                        nb = 2 if ln == "kk" else 4
                        for c in range(nb):
                            ins = tr(b[:, c * P:(c + 1) * P], rope_o[:, i % 2, c * P:(c + 1) * P], ident)
                        ins.then_inc(full((ln, "T", lt)), 1)
                    if name in ROPED:
                        lagged.append((name, t))
            for t in range(1, NT):
                for h in range(RH):
                    q = slice(64 * (h % 2), 64 * (h % 2) + 64)
                    if h == 0 and t == 1:
                        for nm in ("iq", "kk"):
                            for tt in range(NT):
                                evacuated(pe, (nm, "T", tt))
                    b = open_bank(("index", t, h))
                    mm(b[:, 0:(t + 1) * P], T1["iq"][q, h // 2, t * P:(t + 1) * P], T1["kk"][q, 1, 0:(t + 1) * P],
                       start=True, stop=True).then_inc(full(("index", t, h)), 1)
            for nm in ("rk", "rq", "aq"):
                for tt in range(NT):
                    evacuated(pe, (nm, "T", tt))
            for tt in range(NT):
                evacuated(pe, ("rv", tt))
            for h in range(RH + 1):
                if h < RH:
                    q = slice(64 * (h % 2), 64 * (h % 2) + 64)
                    for m in range(NT):
                        b = open_bank(("ret_s", h, m))
                        mm(b[:, 0:S - m * P], T1["rk"][q, h // 2, m * P:(m + 1) * P], T1["rq"][q, h // 2, m * P:S],
                           start=True, stop=True).then_inc(full(("ret_s", h, m)), 1)
                if h >= 1:
                    g = h - 1
                    if h == 1:
                        obs = [open_bank(("ret_o", t)) for t in range(NT)]
                    pe.wait_ge(s["decayed"], h)
                    for t in range(NT):
                        for m in range(t + 1):
                            o = [0, 512, 896, 1152][m] + (t - m) * P
                            ins = mm(obs[t][:, g * HD:(g + 1) * HD], sT[:, g % 2, o:o + P], rv_tok[:, m, g * HD:(g + 1) * HD],
                                     start=(m == 0), stop=(m == t))
                        if h == RH:
                            ins.then_inc(full(("ret_o", t)), 1)
                    if h < RH:
                        ins.then_inc(s["ret_pv"], 1)
            attention("dsa", None)

            def wait_mix1():
                pe.wait_ge(s["mixed_ready"], NT)
                for g in range(NT):
                    evacuated(pe, ("dsa", "O", g))

            out_gemm("mix1", mixed, wait_mix1)
            norm(1)
            ffn(0)
            norm(2)
            for u in range(2):
                feat_gemm(("hq", u), h_t, [("hq", u, j) for j in range(4)])
            tok_gemm("hg", h_t, 2)
            for u in range(2):
                feat_gemm(("hf", u), h_t, [("hf", u, j) for j in range(4)])
            tok_gemm("hi", h_t, 2)
            for u in range(2):
                for t in range(NT):
                    evacuated(pe, ("hi", u, t))
            for h in range(HH + 1):
                if h < HH:
                    L = lvl[h % 2]
                    for lv in range(LEVELS + 1):
                        b = open_bank(("diag", h, lv))
                        if lv:
                            pe.wait_ge(s["qk_done"], 2 * (LEVELS * h + lv))
                        else:
                            pe.wait_ge(s["k_done"], 2)
                        for t in range(NT):
                            c = slice(t * P, (t + 1) * P)
                            k, q = (HK[:, h, c], HQ[:, h, c]) if lv == 0 else (L[:, lv - 1, c], L[:, lv - 1, c])
                            ins = mm(b[:, c], k, q, start=True, stop=True)
                        ins.then_inc(full(("diag", h, lv)), 1)
                    pe.wait_ge(s["q1_done"], 4 * (h + 1))
                    b = open_bank(("far", h, 0))
                    mm(b[:, 0:P], k1[:, 0], q1[:, 0], start=True, stop=True)
                    mm(b[:, P:3 * P], k1[:, 3], q1[:, 1:3].rearrange("p s n -> p (s n)"), start=True, stop=True).then_inc(full(("far", h, 0)), 1)
                    b = open_bank(("far", h, 1))
                    mm(b[:, 0:2 * P], k1[:, 1], q1[:, 1:3].rearrange("p s n -> p (s n)"), start=True, stop=True)
                    mm(b[:, 2 * P:3 * P], k1[:, 2], q1[:, 3], start=True, stop=True).then_inc(full(("far", h, 1)), 1)
                if h >= 1:
                    g = h - 1
                    b = open_bank(("ho", g))
                    evacuated(pe, ("diag", g, LEVELS))
                    evacuated(pe, ("far", g, 0))
                    evacuated(pe, ("far", g, 1))
                    for t in range(NT):
                        for m in range(t + 1):
                            ins = mm(b[:, t * P:(t + 1) * P], attn[:, g % 2, m, t * P:(t + 1) * P], v_tok[:, m, g * P:(g + 1) * P],
                                     start=(m == 0), stop=(m == t))
                    ins.then_inc(full(("ho", g)), 1)
            out_gemm("mix2", v_tok, lambda: pe.wait_ge(s["ho_ready"], NT))
            norm(3)
            ffn(1)
            norm(4)
            feat_gemm("kvc", hkv_t, [("kvc", j) for j in range(4)])
            tok_gemm("kvs", hkv_t, 2)
            tok_gemm("nq", h_t, 3, lambda u: 512 if u < 2 else 48)
            pe.wait_ge(s["u_done"], 12)
            for j in range(4):
                evacuated(pe, ("kvc", j))
            for kv in range(2):
                w = arrived(pe, ("cmp1", kv)).rearrange("p (r n) -> p r n", r=16)
                for n in range(2):
                    b = open_bank(("cmp1", kv, n))
                    for r in range(16):
                        ins = mm(b[:, 0:4 * NCMP], w[:, r, n * P:(n + 1) * P], win[:, kv, r].rearrange("p h i -> p (h i)"),
                                 start=(r == 0), stop=(r == 15))
                    ins.then_inc(full(("cmp1", kv, n)), 1)
            for kv in range(2):
                for j in range(2):
                    evacuated(pe, ("cmp1", kv, j))
            pe.wait_ge(s["w2_in"], 32)
            b = open_bank("cmp2")
            for kv in range(2):
                for kh in range(NSA_KV):
                    for n in range(2):
                        ins = mm(b[0:NCMP, kv * 256 + kh * HD:kv * 256 + (kh + 1) * HD], h1[:, kv, n, kh], w2_sb[:, kv, n, :],
                                 start=(n == 0), stop=(n == 1))
            ins.then_inc(full("cmp2"), 1)
            pe.wait_ge(s["cmp_tok"], 1)
            b = open_bank("cmpT")
            for c in range(2):
                ins = tr(b[:, 32 * c:32 * c + NCMP], kc_tok[:, 2 * c:2 * c + 2, :].rearrange("p h d -> p (h d)"), ident[0:NCMP, 0:NCMP])
            ins.then_inc(full("cmpT"), 1)
            for t in range(NT):
                for j in range(3):
                    i = 3 * t + j
                    if j < 2:
                        pe.wait_ge(s["gained"], i + 1)
                        b = open_bank(("nT", t, j))
                        for c in range(4):
                            ins = tr(b[:, c * P:(c + 1) * P], n_a[:, i % 2, c * P:(c + 1) * P], ident)
                        ins.then_inc(full(("nT", t, j)), 1)
                    pe.wait_ge(s["rope2_done"], i + 1)
                    key = ("nT", t, 2 + j)
                    b = open_bank(key)
                    for c in range(4):
                        ins = tr(b[:, c * P:(c + 1) * P], n_o[:, i % 2, c * P:(c + 1) * P], ident)
                    ins.then_inc(full(key), 1)
            for t in range(NT):
                for j in range(5):
                    evacuated(pe, ("nT", t, j))
            evacuated(pe, "cmpT")
            for i in range(len(GROUPS) + 2):
                if i < len(GROUPS):
                    t, kp = GROUPS[i]
                    bq = [open_bank(("cS", i, q)) for q in range(2)]
                    for g in range(4):
                        for q in range(2):
                            d = slice(64 * q, 64 * q + 64)
                            ins = mm(bq[q][:, 32 * g:32 * g + NCMP], qn_t[d, kp * 4 + g, t * P:(t + 1) * P], kc_t[d, kp, 0:NCMP],
                                     start=True, stop=True)
                            if g == 3:
                                ins.then_inc(full(("cS", i, q)), 1)
                if 1 <= i <= len(GROUPS):
                    pe.wait_ge(s["cmp_p"], i)
                    for q in range(2):
                        b = open_bank(("cT", i - 1, q))
                        for g in range(4):
                            ins = tr(b[0:NCMP, g * P:(g + 1) * P], cp[:, (i - 1) % 2, 4 * q + g, :], ident)
                        ins.then_inc(full(("cT", i - 1, q)), 1)
                if i >= 2:
                    t, kp = GROUPS[i - 2]
                    for q in range(2):
                        evacuated(pe, ("cT", i - 2, q))
                    b = open_bank(("cO", i - 2))
                    for hh in range(8):
                        ins = mm(b[:, hh * HD:(hh + 1) * HD], cpt[:, i % 2, hh, :], vc_tok[0:NCMP, 2 * kp + hh // 4, :],
                                 start=True, stop=True)
                    ins.then_inc(full(("cO", i - 2)), 1)
            attention("nsa", None)
            for mj in ADA_LATE:
                ada_row(*mj)
            out_gemm("mix3", nsa_tok, lambda: pe.wait_ge(s["nsa_added"], len(NSA_GROUPS)))
            norm(5)
            ffn(2)


_INS = """x mix_norm_pre mix_norm_post w_in w_out ffn_norm_pre ffn_norm_post w_up conv_w conv_b w_down c_2 ada_w_2 ada_b_2
norm_mix_2 norm_ffn_2 hgrn_w_in_2 hgrn_out_norm_2 hgrn_w_out_2 kv_ada_w_2 kv_ada_b_2 kv_norm_2 nsa_w_kv_2
nsa_k_norm_2 cmp_pos_2 cmp_w1_2 cmp_w2_2 nsa_w_q_2 nsa_q_norm_2 nsa_w_out_2 ffn_w_in_2 ffn_w_out_2""".split()


def kernel(**inputs):
    import concourse.bacc as _bacc
    from concourse.bass_utils import run_bass_kernel_spmd as _run

    nc = _bacc.Bacc("TRN2", target_bir_lowering=False, num_devices=1)
    arrays, io = {}, {}
    given = {n: np.ascontiguousarray(inputs[n]) for n in _INS}
    given.update(shape_constants())
    for name, a in given.items():
        arrays[f"in_{name}"] = a
        io[name] = nc.dram_tensor(f"in_{name}", a.shape, mybir.dt.from_np(a.dtype), kind="ExternalInput").ap()
    out = nc.dram_tensor("out_0", (1, S, D), F32, kind="ExternalOutput").ap()
    build(nc, io, out)
    r = _run(nc, [arrays], core_ids=[0])
    return r.results[0]["out_0"]
```

```python
from contextlib import ExitStack

import numpy as np

import concourse.bass as bass
from concourse import mybir

F32 = mybir.dt.float32
F32R = mybir.dt.float32r
I8 = mybir.dt.int8
ALU = mybir.AluOpType
ACT = mybir.ActivationFunctionType
AX = mybir.AxisListType.X

P = 128
S = 512
NT = S // P
D = 1024
KT = D // P
HD = 64
RH = 8
TOPK = 128
DFF = 2816
FT = DFF // P
EPS = 1e-6
NEG = -1e30
REPLACED = -3e38
SCALE = HD ** -0.5
HH = 8
LEVELS = 7
NSA_H, NSA_KV, GROUP = 16, 4, 4
NCMP = 31
RING = 2
SLOT = 4096
FFN_UNITS = FT // 2
HALF = 512
MAP = 16512
PIECE = 1024

ROWS_IN = 16 * 16
VEC_ROWS = [("mix_norm_pre", 8), ("ffn_norm_pre", 8), ("norm_mix_2", 16), ("norm_ffn_2", 16), ("kv_norm_2", 8), ("c_2", 8)]


def shape_constants():
    f = np.float32
    inv = (f(10000.0) ** (-np.arange(0, HD, 2, dtype=f) / f(HD))).astype(f)
    ang = np.arange(S, dtype=f)[:, None] * inv[None, :]
    tok = lambda a: np.ascontiguousarray(a.reshape(NT, P, -1).transpose(1, 0, 2))
    rope = np.stack([tok(np.cos(ang)), tok(np.sin(ang)), tok(-np.sin(ang))], axis=1).astype(f)
    p = np.arange(P)
    j = np.arange(S)
    log_g = np.log(1.0 - 2.0 ** (-5.0 - np.arange(RH)))
    diff = j[None, :] - p[:, None]
    decay = np.where(diff[:, None, :] >= 0, np.exp(log_g[None, :, None] * np.maximum(diff, 0)[:, None, :]), 0.0) * SCALE
    strip = np.where(j[None, :] - 3 * P > p[:, None], NEG, 0.0)
    a, b = p[:, None], p[None, :]
    masks = [a == b]
    for level in range(LEVELS):
        c = 1 << level
        masks.append((a // (2 * c) == b // (2 * c)) & (a % (2 * c) < c) & (b % (2 * c) >= c))
    t = (np.arange(NT)[None, :] * P + p[:, None])
    end = np.arange(NCMP) * 16 + 31
    cmp_bias = np.where(end[None, None, :] <= t[:, :, None], 0.0, NEG)
    keep = np.ones((P, S))
    keep[:, ::P] = 0.0
    small = np.concatenate([np.eye(P), rope.reshape(P, -1), strip, cmp_bias.reshape(P, -1), (t >= 31) * 1.0, keep], axis=1)
    return {"c_small": small.astype(f), "c_decay": decay.astype(f).reshape(P, RH * S),
            "c_masks": np.stack(masks, 1).astype(f)}


def build(nc, io, out):
    ctx = ExitStack()
    with ctx:
        def sb(name, shape, dt=F32):
            return ctx.enter_context(nc.sbuf_tensor(name, shape, dt))

        def sem(name):
            return ctx.enter_context(nc.semaphore(name))

        ps = ctx.enter_context(nc.psum_tensor("ps", [P, 8, HALF], F32))
        h_t = sb("h_t", [P, KT, S])
        arena = sb("arena", [P, 28160])
        def over(name, shape, at):
            return nc.alloc_sbuf_tensor_at(name, shape, F32R, offset=MAP + 4 * at)

        x_hi = over("x_hi", [P, KT, S], 0)
        x_lo = over("x_lo", [P, KT, S], KT * S + 19456)
        w_hi = over("w_hi", [P, 2, PIECE], KT * S + 19456 + 4096)
        w_lo = over("w_lo", [P, 2, PIECE], KT * S + 19456 + 4096 + 2 * PIECE)
        x0_lo = over("x0_lo", [P, KT, S], KT * S)
        w0_hi = over("w0_hi", [P, 2, PIECE], KT * S + 21824)
        w0_lo = over("w0_lo", [P, 2, PIECE], KT * S + 21824 + 2 * PIECE)
        x2_lo = over("x2_lo", [P, KT, S], KT * S + 24064)
        w2_hi = over("w2_hi", [P, 3, HALF], KT * S + 20480)
        w2_lo = over("w2_lo", [P, 3, HALF], KT * S + 20480 + 3 * HALF)
        x_tok = sb("x_tok", [P, NT, D])
        ring = sb("ring", [P, RING, SLOT])
        row = sb("row", [P, 2, D])
        ada_acc = sb("ada_acc", [P, 2, HALF])
        small = sb("small", [P, 128 + 3 * 128 + 512 + 124 + 4 + 512])
        masks = sb("masks", [P, LEVELS + 1, P], I8)
        vec = sb("vec", [P, 416])
        mod = sb("mod", [P, 5, 2, KT])
        ones = sb("ones", [P, P])
        out_norm = sb("out_norm", [P, P])
        qk_norm = sb("qk_norm", [P, 3, HD])
        cmp_norm = sb("cmp_norm", [P, HD])
        stat = sb("stat", [P, 256])
        fac = sb("fac", [P, 96])
        small2 = sb("small2", [P, 1040])
        junk = sb("junk", [P, D])
        junk2 = junk[:, HALF:D]
        eps = sb("eps", [P, 1])
        c_act = sb("c_act", [P, KT])
        best = sb("best", [P, 3, 8])

        ident = small[:, 0:128]
        rope_t = small[:, 128:512].rearrange("p (k t d) -> p k t d", k=3, t=NT)
        strip = small[:, 512:1024]
        cmp_bias = small[:, 1024:1148].rearrange("p (t c) -> p t c", t=NT)
        row_valid = small[:, 1148:1152]
        keep = small[:, 1152:1664]

        def carve(sizes):
            at, got = 0, []
            for n in sizes:
                got.append(arena[:, at:at + n])
                at += n
            assert at <= 28160, at
            return got

        bank_full = [sem(f"bank_full{b}") for b in range(8)]
        bank_free = [sem(f"bank_free{b}") for b in range(8)]
        landed = [sem(f"landed{r}") for r in range(2 * RING)]
        names = """consts_in x_in rows_in out_norm_in cmp_pos_in row_in out_done c_act_done ones_done norm_rms xn_ready
            x_ready mod_ready rope_done decayed ret_pv rel_used picked ret_square ret_rms mixed_ready p_ready
            pv_done y_rms y_scaled act_step dve_step hid_gate hid_done sg_done f_abs logf_done k_done g_done
            d_sub d_exp qk_done q1_done attn_zero ho_rms ho_ready cmp_sq cmp_rms cmp_tok cmp_l cmp_p raw_done
            raw_rms raw_norm rope2_done nsa_added u_done e_done conv_pre tabs_done ho_scaled eq_done kvraw w2_in
            gained whole_done hi_done lo_done piece_done x_split hid_hi acc_done gate_row_in0 gate_row_in1
            acc_half zero_done keys_zero k_shifted rk_shifted x0_hi x0_split out_hi cmp_zero x_ready_v""".split()
        s = {n: sem(n) for n in names}

        bank_use, bank_fills, bank_frees, turn = {}, [0] * 8, [0] * 8, [0]

        def plan_bank(key, bank=None, counted=True):
            if bank is None:
                bank = turn[0]
                turn[0] = (bank + 1) % 8
            assert key not in bank_use, key
            bank_use[key] = (bank, bank_fills[bank], bank_frees[bank])
            bank_fills[bank] += counted
            bank_frees[bank] += 1
        FULL, FREE = bank_full, bank_free

        def open_bank(key):
            b, _, free = bank_use[key]
            if free > 0:
                nc.tensor.wait_ge(FREE[b], free)
            return ps[:, b]

        def filled(eng, key):
            b, fill, _ = bank_use[key]
            eng.wait_ge(FULL[b], fill + 1)
            return ps[:, b]

        def full(key):
            return FULL[bank_use[key][0]]

        def free(key):
            return FREE[bank_use[key][0]]

        def evacuated(eng, key):
            b, _, f = bank_use[key]
            eng.wait_ge(FREE[b], f + 1)

        def own_order(eng, own):
            count = [0]

            def step(ins):
                ins.then_inc(own, 1)
                count[0] += 1

            def after(but=0):
                if count[0] > but:
                    eng.wait_ge(own, count[0] - but)

            return step, after

        units, unit_at, slot_dmas = [], {}, [0] * (2 * RING)

        def unit(key, pieces, release, release_first=None):
            n = len(units)
            for h in range(2):
                slot_dmas[2 * (n % RING) + h] += len(pieces[h])
            unit_at[key] = (n % RING, [16 * slot_dmas[2 * (n % RING) + h] for h in range(2)])
            units.append((pieces, (release_first or release, release)))

        def arrived(eng, key, halves=(0, 1)):
            slot, counts = unit_at[key]
            for h in halves:
                eng.wait_ge(landed[2 * slot + h], counts[h])
            return ring[:, slot]

        def in_halves(sl, rows, width):
            return sl.rearrange("p (h x) -> p h x", h=2)[:, :, 0:rows * width].rearrange("p h (k n) -> p h k n", k=rows)

        def columns(w, c0, n, at=0, width=None):
            width = width or n

            def half(h):
                return (lambda sl: in_halves(sl, 4, width)[:, h, :, at:at + n],
                        w[h * HALF:(h + 1) * HALF, c0:c0 + n].rearrange("(k p) n -> p k n", p=P))

            return [half(0)], [half(1)]

        def together(*loads):
            return [sum((load[h] for load in loads), []) for h in range(2)]

        down_groups = [(0, 4), (4, 4), (8, 4), (12, 4), (16, 4), (20, 2)]

        w_in, w_out = io["w_in"][0], io["w_out"][0]
        P1 = {"iq": [(2688, 512)], "kk": [(2560, 128), (3200, 72)], "aq": [(2048, 512)], "rk": [(512, 512)],
              "rq": [(0, 512)], "rv": [(1024, 512)], "rg": [(1536, 512)]}
        P1_ORDER = ["iq", "kk", "aq", "rk", "rq", "rv", "rg"]
        ROPED = ["iq", "kk", "aq", "rk", "rq"]

        plan_bank("vec")

        def plan_norm(i):
            for kt in range(KT):
                plan_bank(("xT", i, kt))

        def plan_tok_gemm(name, pieces_of, n_units):
            for u in range(n_units):
                for t in range(NT):
                    plan_bank((name, u, t))
                unit((name, u), pieces_of(u), ("bank", (name, u, NT - 1)))

        ADA_W = [io["ada_w_2"][m] for m in range(4)] + [io["kv_ada_w_2"]]
        ADA = [(0, j) for j in range(6)] + [(1, j) for j in range(6)] + [(2, j) for j in range(6)] \
            + [(4, j) for j in range(4)] + [(3, j) for j in range(6)]
        ADA_N = {mj: n for n, mj in enumerate(ADA)}
        ada_after = {(0, u): [ADA[u]] for u in range(10)}
        ada_after.update({(1, u): [ADA[12 + u]] for u in range(11)})
        ada_down = {0: ADA[10:12], 1: ADA[23:25]}
        ADA_LATE = ADA[25:]

        def ada_unit(m, j):
            unit(("ada", m, j), columns(ADA_W[m], j * HALF, HALF), ("sem", "acc_done", ADA_N[(m, j)] + 1),
                 ("sem", "acc_half", ADA_N[(m, j)] + 1))

        splits = [0]
        split_at = {}
        piece_end = []
        counted_pieces = [0]

        def plan_piece(key, last_bank=None):
            split_at[key] = splits[0]
            splits[0] += 1
            counted_pieces[0] += last_bank is None
            piece_end.append(last_bank or counted_pieces[0])

        def piece_read(eng, n):
            if isinstance(piece_end[n], int):
                eng.wait_ge(s["piece_done"], piece_end[n])
            else:
                filled(eng, piece_end[n])

        def plan_split_unit(key, pieces, last_bank):
            for q in range(4):
                plan_piece((key, q), last_bank if q == 3 else None)
            unit(key, pieces, ("sem", "lo_done", splits[0]), ("sem", "lo_done", splits[0] - 2))

        def plan_ffn(i, w_up, w_down):
            for u in range(FFN_UNITS):
                for j in range(4):
                    plan_bank(("up", i, u, j))
                for q in range(4):
                    plan_piece(("up", i, u, q), ("up", i, u, 3) if q == 3 else None)
                unit(("up", i, u), together(columns(w_up, u * 256, 256, 0, 512), columns(w_up, DFF + u * 256, 256, 256, 512)),
                     ("sem", "lo_done", splits[0]), ("sem", "lo_done", splits[0] - 2))
                for m, j in ada_after.get((i, u), []):
                    ada_unit(m, j)
                for m, j in ada_after.get((i, u - 1), []):
                    plan_bank(("ada", m, j))
            for m, j in ada_after.get((i, FFN_UNITS - 1), []):
                plan_bank(("ada", m, j))
            for j in range(8):
                plan_bank(("down", i, j))
            for g, (k0, n) in enumerate(down_groups):
                for k in range(k0, k0 + n):
                    plan_piece(("down", i, k), ("down", i, 7) if k == FT - 1 else None)
                n //= 2
                halves = [[(lambda sl, n=n, h=h: in_halves(sl, n, D)[:, h],
                            w_down[(k0 + h * n) * P:(k0 + h * n + n) * P, :].rearrange("(k p) n -> p k n", p=P))] for h in range(2)]
                unit(("down", i, g), halves, ("sem", "lo_done", splits[0]), ("sem", "lo_done", splits[0] - n))
                for mj in ada_down.get(i, [])[g:g + 1]:
                    ada_unit(*mj)
            for mj in ada_down.get(i, []):
                plan_bank(("ada",) + mj)

        def plan_out(name, w, n_in=KT):
            for kt in range(n_in):
                plan_bank((name, "T", kt))
            for u in range(2):
                for t in range(NT):
                    plan_bank((name, u, t))
                plan_split_unit((name, u), columns(w, u * 512, 512), (name, u, NT - 1))

        def plan_attention(name, n_units, okeys):
            for i in range(n_units + 3):
                if i < n_units:
                    plan_bank((name, "S", i), i % 2)
                if 2 <= i < n_units + 2:
                    plan_bank((name, "T", i - 2), 2 + i % 2)
                if i >= 3 and (i - 3) % 8 < 2:
                    g, odd = (i - 3) // 8, (i - 3) % 8
                    plan_bank((name, "O", g, odd), 4 + 2 * (g % 2) + odd, counted=False)

        plan_norm(0)
        P1_PIECES = [(k, q) for k in range(len(P1_ORDER)) for q in range(4)]
        for k, name in enumerate(P1_ORDER):
            loads, at = [], 0
            total = sum(n for _, n in P1[name])
            for c0, n in P1[name]:
                loads.append(columns(w_in, c0, n, at, total))
                at += n
            for t in range(NT):
                plan_bank((name, t), 4 * (k % 2) + t)
            if k and P1_ORDER[k - 1] in ROPED:
                for t in range(NT):
                    plan_bank((P1_ORDER[k - 1], "T", t), 4 * ((k - 1) % 2) + t)
            plan_split_unit(name, together(*loads), (name, NT - 1))

        def p1_piece(w, k, q):
            n = sum(c for _, c in P1[P1_ORDER[k]])
            at = (q // 2) * (SLOT // 2) + (q % 2) * 2 * n
            return w[:, at:at + 2 * n]

        for t in range(1, NT):
            for h in range(RH):
                plan_bank(("index", t, h))
        unit("decay", [[(lambda sl, h=h: sl[:, h * 2048:(h + 1) * 2048], io["c_decay"][:, h * 2048:(h + 1) * 2048])] for h in range(2)],
             ("sem", "decayed", RH))
        for h in range(RH + 1):
            if h < RH:
                for m in range(NT):
                    plan_bank(("ret_s", h, m), m)
            if h == 1:
                for t in range(NT):
                    plan_bank(("ret_o", t), 4 + t)
        DSA_UNITS = [(t, h) for t in range(NT) for h in range(RH)]
        plan_attention("dsa", len(DSA_UNITS), None)
        plan_out("mix1", w_out)
        plan_norm(1)
        plan_ffn(0, io["w_up"][0], io["w_down"][0])
        plan_norm(2)
        hw = io["hgrn_w_in_2"][0]
        H_UNITS = [("hq", 0), ("hq", 1), ("hg", 0), ("hg", 1), ("hf", 0), ("hf", 1), ("hi", 0), ("hi", 1)]
        H_PIECES = [(key, k) for key in H_UNITS for k in range(KT)]
        H_COLUMN = {"hq": 0, "hg": 3072, "hf": 1024, "hi": 2048}
        for key in H_UNITS:
            name, u = key
            for j in range(4):
                plan_bank((name, u, j))
            for k in range(KT):
                plan_piece((key, k), (name, u, 3) if k == KT - 1 else None)
            unit(key, columns(hw, H_COLUMN[name] + u * 512, 512), ("sem", "lo_done", splits[0]), ("sem", "lo_done", splits[0] - 4))
        H_LAG = KT + 2
        for h in range(HH + 1):
            if h < HH:
                for lv in range(LEVELS + 1):
                    plan_bank(("diag", h, lv), lv % 4)
                for b in range(2):
                    plan_bank(("far", h, b), 4 + b)
            if h >= 1:
                plan_bank(("ho", h - 1), 6 + h % 2)
        plan_out("mix2", io["hgrn_w_out_2"][0])
        plan_norm(3)
        plan_ffn(1, io["ffn_w_in_2"][0], io["ffn_w_out_2"][0])
        plan_norm(4)
        wkv, wq = io["nsa_w_kv_2"], io["nsa_w_q_2"][0]
        for j in range(4):
            plan_bank(("kvc", j))
        unit("kvc", columns(wkv, 0, 512), ("bank", ("kvc", 3)))
        plan_tok_gemm("kvs", lambda u: columns(wkv, 512 + u * 512, 512), 2)
        plan_tok_gemm("nq", lambda u: columns(wq, u * 512, 512 if u < 2 else 48), 3)
        w1 = io["cmp_w1_2"]
        for kv in range(2):
            for j in range(2):
                plan_bank(("cmp1", kv, j))
            unit(("cmp1", kv), [[(lambda sl, h=h: sl[:, h * 2048:(h + 1) * 2048].rearrange("p (r n) -> p r n", r=8),
                                  w1[kv, h * 1024:(h + 1) * 1024, :].rearrange("(r p) n -> p r n", p=P))] for h in range(2)],
                 ("bank", ("cmp1", kv, 1)))
        plan_bank("cmp2")
        plan_bank("cmpT")
        for t in range(NT):
            for j in range(5):
                plan_bank(("nT", t, j))
        GROUPS = [(t, kp) for t in range(NT) for kp in range(2)]
        for i in range(len(GROUPS) + 2):
            if i < len(GROUPS):
                plan_bank(("cS", i), i % 4)
            if 1 <= i <= len(GROUPS):
                plan_bank(("cT", i - 1), 4 + i % 2)
            if i >= 2:
                plan_bank(("cO", i - 2), 6 + i % 2)
        NSA_GROUPS = [(t, kp, br) for t in range(NT) for kp in range(2) for br in range(2)]
        plan_attention("nsa", 8 * len(NSA_GROUPS), None)
        for m, j in ADA_LATE:
            plan_bank(("ada", m, j))
            ada_unit(m, j)
        plan_out("mix3", io["nsa_w_out_2"][0])
        plan_norm(5)
        plan_ffn(2, io["ffn_w_in_2"][1], io["ffn_w_out_2"][1])

        (a_xn, a_rq, a_rk, a_aq, a_iq, a_kk, a_rv, a_rg, a_av, a_tmp, a_sT, a_isc, a_sel, a_rel) = carve(
            [4096, 2048, 2048, 2048, 2048, 2048, 2048, 2048, 320, 3072, 2560, 1152, 1152, 1024])
        tiles4 = lambda a: a.rearrange("p (k n) -> p k n", k=4)
        xn = tiles4(a_xn)
        T1 = {"rq": tiles4(a_rq), "rk": tiles4(a_rk), "aq": tiles4(a_aq), "iq": tiles4(a_iq),
              "kk": a_kk.rearrange("p (q k n) -> p q k n", q=2, k=2)}
        rk_pair = [T1["rk"], tiles4(a_xn[:, 0:2048])]
        rv_tok, rg_tok = tiles4(a_rv), tiles4(a_rg)
        av_tok = a_av.rearrange("p (k n) -> p k n", k=5)
        iw = fac[:, 64:96].rearrange("p (t h) -> p t h", t=NT)
        rope_a, rope_b, rope_o = [a_tmp[:, i * 1024:(i + 1) * 1024].rearrange("p (j n) -> p j n", j=2) for i in range(3)]
        sT = a_sT.rearrange("p (j n) -> p j n", j=2)
        isc, sel_bias = [[a[:, o:o + n] for o, n in ((0, 256), (256, 384), (640, 512))] for a in (a_isc, a_sel)]
        rel = a_rel.rearrange("p (j n) -> p j n", j=2)
        mixed = tiles4(a_xn)
        att_l, att_p, att_pt = rope_a, rope_b, rope_o
        y1 = arena[:, 4096:8192].rearrange("p (k n) -> p k n", k=4)

        f_xn, f_hid, f_tmp = carve([4096, FT * S, 8 * S])
        hid = f_hid.rearrange("p (k n) -> p k n", k=FT)
        ftmp = f_tmp.rearrange("p (j n) -> p j n", j=8)
        hid_hi = x_hi[:, 0:4, :]
        hid_lo = x_hi[:, 4:8, :]
        yf = tiles4(f_xn)

        (h_v, h_sg, h_q, h_k, h_g, h_d0, h_at) = carve([4096, 4096, 4096, 4096, 4096, 3584, 4096])
        v_tok, sg_tok = tiles4(h_v), tiles4(h_sg)
        xn_h = tiles4(h_v)
        HQ, HK, HG = [a.rearrange("p (h n) -> p h n", h=HH) for a in (h_q, h_k, h_g)]
        lvl = [h_d0.rearrange("p (l n) -> p l n", l=LEVELS),
               h_t[:, 0:LEVELS, :]]
        attn = h_at.rearrange("p (j s n) -> p j s n", j=2, s=NT)
        f_work = [arena[:, 0:2048], arena[:, 2048:4096]]
        k1 = small2[:, 0:512].rearrange("p (s n) -> p s n", s=4)
        q1 = small2[:, 512:1024].rearrange("p (s n) -> p s n", s=4)
        tot = small2[:, 1024:1032]
        y2 = tiles4(h_q)

        (n_xn, n_raw, n_qn, n_qr, n_k, n_v, n_hkv, n_vc) = carve([4096, 6144, 4096, 4096, 2048, 2048, 4096, 1024])
        raw = n_raw.rearrange("p (t h d) -> p t h d", t=NT, h=24)
        qn_t = n_qn.rearrange("p (k n) -> p k n", k=8)
        qr_t = n_qr.rearrange("p (k n) -> p k n", k=8)
        k_t = tiles4(n_k)
        k_pair = [k_t, tiles4(n_raw[:, 4096:6144])]
        v_nsa = n_v.rearrange("p (t b n) -> p t b n", t=NT, b=2)
        hkv_t = n_hkv.rearrange("p (k n) -> p k n", k=8)
        win = n_qn[:, 0:3968].rearrange("p (kv r h i) -> p kv r h i", kv=2, r=16, h=4)
        h1 = small2[:, 0:496].rearrange("p (kv n h i) -> p kv n h i", kv=2, n=2, h=4)
        kc_raw = small2[0:NCMP, 496:752]
        kc_tok = small2[0:NCMP, 752:1008].rearrange("p (h d) -> p h d", h=4)
        kc_t = small2[:, 0:256].rearrange("p (c q i) -> p c q i", c=2, q=2)
        vc_diag = n_vc.rearrange("p (h g d) -> p h g d", h=4, g=4)
        w2_sb = n_hkv[:, 3776:4032].rearrange("p (kv n d) -> p kv n d", kv=2, n=2)
        nsa_tok = tiles4(n_xn)
        n_a, n_b, n_o = [n_hkv[:, i * 1024:(i + 1) * 1024].rearrange("p (j n) -> p j n", j=2) for i in range(3)]
        cl = n_raw[:, 0:496].rearrange("p (j h c) -> p j h c", j=2, h=8)
        cp = n_raw[:, 512:1024].rearrange("p (j h c) -> p j h c", j=2, h=8)
        cpt = n_raw[:, 1024:1536].rearrange("p (j q n) -> p j q n", j=2, q=2)
        n_tmp = n_raw[:, 3072:4096].rearrange("p (j n) -> p j n", j=2)
        gates = n_hkv[:, 3072:3264].rearrange("p (t g) -> p t g", t=NT)
        gates_e = n_hkv[:, 3264:3456].rearrange("p (t g) -> p t g", t=NT)
        y3 = tiles4(n_qn)

        XN = {0: xn, 1: tiles4(f_xn), 2: xn_h, 3: tiles4(f_xn), 4: tiles4(n_xn), 5: tiles4(f_xn)}

        vec_at, at = {}, 0
        for n, r in VEC_ROWS:
            vec_at[n] = at
            at += r
        CONV = 64
        POS = CONV + 176
        BIAS = POS + 64

        def vcol(name, i=0):
            return vec[:, vec_at[name] + 8 * i:vec_at[name] + 8 * i + 8]

        NORM_OUT = {
            0: [(h_t, vcol("mix_norm_pre"), None)], 1: [(h_t, vcol("ffn_norm_pre"), None)],
            2: [(h_t, mod[:, 0, 0], mod[:, 0, 1])], 3: [(h_t, mod[:, 1, 0], mod[:, 1, 1])],
            4: [(h_t, mod[:, 2, 0], mod[:, 2, 1]), (hkv_t, mod[:, 4, 0], mod[:, 4, 1])],
            5: [(h_t, mod[:, 3, 0], mod[:, 3, 1])]}
        MOD_GAIN = {0: vcol("norm_mix_2", 0), 1: vcol("norm_ffn_2", 0), 2: vcol("norm_mix_2", 1),
                    3: vcol("norm_ffn_2", 1), 4: vcol("kv_norm_2")}
        MOD_ORDER = [0, 1, 2, 4, 3]
        MOD_READY = {m: i + 1 for i, m in enumerate(MOD_ORDER)}
        FFN_NORM = {1: 0, 3: 1, 5: 2}
        MIXER_NORM = {0: 0, 2: 1}
        NORM_MOD = {2: 0, 3: 1, 4: 4, 5: 3}

        vec_rows = arena[0:64, 8192:8320]
        conv_rows = [arena[0:88, 8320:8448], arena[0:88, 8448:8576]]
        bias_rows = arena[0:112, 8832:8960]
        mask_rows = arena[:, 9216:9216 + (LEVELS + 1) * P].rearrange("p (l n) -> p l n", l=LEVELS + 1)
        pos_rows = arena[0:32, 8576:8832]

        def dsa_unit(i):
            t, h = DSA_UNITS[i]
            n = (t + 1) * P
            return dict(q=T1["aq"][:, h // 2, t * P:(t + 1) * P], k=T1["kk"][:, h % 2, 0, 0:n], n=n,
                        bias=strip[:, 3 * P:] if t == 0 else sel_bias[t - 1],
                        v=lambda b: a_av[:, b * HD:b * HD + P], slot=h)

        def nsa_unit(i):
            t, kp, br = NSA_GROUPS[i // 8]
            g, ko = (i % 8) // 2, i % 2
            n = (t + 1) * P
            return dict(q=qr_t[:, kp * 4 + g, t * P:(t + 1) * P], k=k_pair[ko][:, 2 * br + kp, 0:n], n=n,
                        bias=strip[:, 3 * P - t * P:],
                        v=lambda b: v_nsa[:, b, br, kp * P:(kp + 1) * P], slot=ko * 4 + g)

        ATT = {"dsa": (dsa_unit, len(DSA_UNITS), (att_l, att_p, att_pt), 0),
               "nsa": (nsa_unit, 8 * len(NSA_GROUPS), (n_a, n_b, n_o), len(DSA_UNITS))}
        neg_max = stat[:, 160:164]
        den = fac[:, 0:16].rearrange("p (j h) -> p j h", j=2)
        rden = fac[:, 16:32].rearrange("p (j h) -> p j h", j=2)

        def hid_ready(eng, i, k):
            if i == 0:
                eng.wait_ge(s["hid_done"], k + 1)
            else:
                evacuated(eng, ("up", i, k // 2, 2 + k % 2))

        def tok_keys(name):
            return [(u, t, (name, u, t)) for u in range(2) for t in range(NT)]

        def down_keys(i):
            return [(u, t, ("down", i, 2 * t + u)) for u in range(2) for t in range(NT)]

        EARLY = {i: [(("up", f, 0, q), ("up", f, 0), q * PIECE, PIECE) for q in range(2)] for i, f in FFN_NORM.items()}
        EARLY[2] = [((H_UNITS[0], k), H_UNITS[0], k * S, S) for k in range(3)]

        OUT_STEPS = [("x", 0), ("x", 1), ("w", 0), ("x", 2), ("x", 3), ("w", 1), ("x", 4), ("x", 5), ("x", 6), ("x", 7)] \
            + [("w", i) for i in range(2, 8)]

        block = ctx.enter_context(nc.Block())

        @block.sync
        def _(sp):
            sp.wait_ge(s["x_in"], 16)
            for n, (pieces, _) in enumerate(units):
                for h in range(2):
                    if n >= RING:
                        kind = units[n - RING][1][h]
                        if kind[0] == "bank":
                            filled(sp, kind[1])
                        else:
                            sp.wait_ge(s[kind[1]], kind[2])
                    for dst, src in pieces[h]:
                        sp.dma_start(dst(ring[:, n % RING]), src).then_inc(landed[2 * (n % RING) + h], 16)

        @block.gpsimd
        def _(pool):
            g = nc.gpsimd
            g.memset(ones[:, :], 1.0).then_inc(s["ones_done"], 1)
            g.memset(av_tok[:, NT], 0.0).then_inc(s["zero_done"], 1)
            g.memset(a_kk, 0.0).then_inc(s["zero_done"], 1)

            def load_row(src, i, n):
                pool.dma_start(row[:, i, :], src.partition_broadcast(P)).then_inc(s["row_in"], 16)

            load_row(io["mix_norm_post"][0], 0, 0)
            load_row(io["ffn_norm_post"][0], 1, 0)

            def load_gate(m):
                pool.wait_ge(s["x_ready_v"], 2 * (m + 1))
                pool.dma_start(row[:, m % 2, :], io["ada_b_2"][m, 2 * D:3 * D].partition_broadcast(P)).then_inc(s[f"gate_row_in{m % 2}"], 16)

            def add_to_x(stage, y, keys=None):
                for t in (0, 1):
                    if keys is None:
                        pool.wait_ge(s["y_scaled"], NT * stage + t + 1)
                    else:
                        for _, tt, key in keys:
                            if tt == t:
                                evacuated(pool, key)
                    g.tensor_tensor(x_tok[:, t], x_tok[:, t], y[:, t], ALU.add).then_inc(s["x_ready"], 1)

            filled(pool, ("rg", NT - 1))
            g.memset(a_xn[:, 0:2048], 0.0).then_inc(s["zero_done"], 1)
            pool.wait_ge(s["rk_shifted"], 1)
            pool.wait_ge(s["zero_done"], 3)
            g.memset(rk_pair[0][64:128], 0.0).then_inc(s["zero_done"], 1)
            pool.wait_ge(s["zero_done"], 4)
            dec = arrived(pool, "decay")
            for h in range(RH):
                for m in range(NT):
                    n = S - m * P
                    evacuated(pool, ("ret_s", h, m))
                    o = [0, 512, 896, 1152][m]
                    ins = g.tensor_tensor(sT[:, h % 2, o:o + n], sT[:, h % 2, o:o + n], dec[:, h * S:h * S + n], ALU.mult)
                    if m == NT - 1:
                        ins.then_inc(s["decayed"], 1)
            for t in range(NT):
                evacuated(pool, ("ret_o", t))
                g.tensor_tensor(mixed[:, t, 0:512], mixed[:, t, 0:512], rg_tok[:, t], ALU.mult).then_inc(s["mixed_ready"], 1)
            add_to_x(0, y1)
            load_gate(0)
            add_to_x(1, yf)
            load_gate(1)
            pool.wait_ge(s["out_norm_in"], 16)
            for u in range(2):
                for t in range(NT):
                    evacuated(pool, ("hg", u, t))
                    w = sg_tok[:, t, u * 512:(u + 1) * 512].rearrange("p (h d) -> p h d", h=4)
                    g.tensor_tensor(w, w, out_norm[:, :].unsqueeze(1).broadcast_to([P, 4, P]), ALU.mult).then_inc(s["sg_done"], 1)
            filled(pool, ("hi", 1, NT - 1))
            g.memset(attn[:, :, :, :], 0.0).then_inc(s["attn_zero"], 1)
            for h in range(HH):
                pool.wait_ge(s["g_done"], h + 1)
                for lv in range(LEVELS):
                    if h >= 2:
                        filled(pool, ("diag", h - 2, lv + 1))
                    c = 1 << lv
                    src = HG[:, h].rearrange("p (b q c) -> p b q c", q=2, c=c)
                    dst = lvl[h % 2][:, lv].rearrange("p (b q c) -> p b q c", q=2, c=c)
                    mid = src[:, :, 0, c - 1:c].broadcast_to([P, S // (2 * c), c])
                    g.tensor_tensor(dst[:, :, 0], mid, src[:, :, 0], ALU.subtract).then_inc(s["d_sub"], 1)
                    g.tensor_tensor(dst[:, :, 1], src[:, :, 1], mid, ALU.subtract).then_inc(s["d_sub"], 1)
            for t in (0, 1):
                pool.wait_ge(s["ho_scaled"], t + 1)
                g.tensor_tensor(v_tok[:, t], v_tok[:, t], sg_tok[:, t], ALU.mult).then_inc(s["ho_ready"], 1)
            add_to_x(2, y2, tok_keys("mix2"))
            load_gate(2)
            add_to_x(3, yf, down_keys(1))
            load_gate(3)
            g.memset(vc_diag[:, :, :, :], 0.0).then_inc(s["cmp_zero"], 1)
            for t in range(NT):
                for j in range(3):
                    i = 3 * t + j
                    pool.wait_ge(s["raw_norm"], i + 1)
                    if j < 2:
                        w = n_a[:, i % 2].rearrange("p (h d) -> p h d", h=8)
                        g.tensor_tensor(w, w, qk_norm[:, 0:1, :].broadcast_to([P, 8, HD]), ALU.mult).then_inc(s["gained"], 1)
                    else:
                        w = n_a[:, i % 2].rearrange("p (k h d) -> p k h d", k=2, h=4)
                        g.tensor_tensor(w, w, qk_norm[:, 1:3, :].unsqueeze(2).broadcast_to([P, 2, 4, HD]), ALU.mult).then_inc(s["gained"], 1)
            g.memset(cp[:, :, :, NCMP:32], 0.0).then_inc(s["keys_zero"], 1)
            g.memset(n_raw[:, 4096:6144], 0.0).then_inc(s["keys_zero"], 1)
            pool.wait_ge(s["k_shifted"], 1)
            pool.wait_ge(s["keys_zero"], 2)
            g.memset(k_pair[0][64:128], 0.0).then_inc(s["keys_zero"], 1)
            pool.wait_ge(s["keys_zero"], 3)
            for i in range(len(NSA_GROUPS)):
                t, kp, br = NSA_GROUPS[i]
                evacuated(pool, ("nsa", "O", i, 0))
                evacuated(pool, ("nsa", "O", i, 1))
                if i >= 1:
                    pool.wait_ge(s["nsa_added"], i)
                w = nsa_tok[:, t, kp * 512:(kp + 1) * 512]
                g.tensor_tensor(w, w, n_tmp[:, i % 2], ALU.add).then_inc(s["nsa_added"], 1)
            add_to_x(4, y3, tok_keys("mix3"))
            add_to_x(5, yf, down_keys(2))
            pool.wait_ge(s["x_ready"], 6 * 2)

        @block.scalar
        def _(act):
            a = nc.scalar
            step, after = own_order(act, s["act_step"])
            highs = set()
            act.dma_start(small[:, :], io["c_small"]).then_inc(s["consts_in"], 16)
            act.dma_start(x_tok[:, :, :], io["x"][0].rearrange("(t p) n -> p t n", p=P)).then_inc(s["x_in"], 16)
            act.dma_start(mask_rows, io["c_masks"]).then_inc(s["consts_in"], 16)
            n_rows = 0
            for name, r in VEC_ROWS:
                src = io[name]
                src = src.rearrange("a (k p) -> (a k) p", p=P) if len(src.shape) == 2 else src.rearrange("(k p) -> k p", p=P)
                act.dma_start(vec_rows[vec_at[name]:vec_at[name] + r, :], src).then_inc(s["rows_in"], 16)
                n_rows += 16
            for j in range(3):
                act.dma_start(conv_rows[j // 2][44 * (j % 2):44 * (j % 2) + 44, :],
                              io["conv_w"][0, j].rearrange("(k p) -> k p", p=P)).then_inc(s["rows_in"], 16)
            act.dma_start(conv_rows[1][44:88, :], io["conv_b"][0].rearrange("(k p) -> k p", p=P)).then_inc(s["rows_in"], 16)
            for kv in range(2):
                for q in range(2):
                    act.dma_start(pos_rows[:, kv * 128 + q * 64:kv * 128 + q * 64 + 64], io["cmp_pos_2"][kv]).then_inc(s["rows_in"], 16)
            act.dma_start(bias_rows[0:96, :], io["ada_b_2"].rearrange("m (k p) -> (m k) p", p=P)).then_inc(s["rows_in"], 16)
            act.dma_start(bias_rows[96:112, :], io["kv_ada_b_2"].rearrange("(k p) -> k p", p=P)).then_inc(s["rows_in"], 16)
            assert n_rows + 16 * 10 == ROWS_IN
            act.dma_start(out_norm[:, :], io["hgrn_out_norm_2"][0].partition_broadcast(P)).then_inc(s["out_norm_in"], 16)
            act.dma_start(qk_norm[:, 0, :], io["nsa_q_norm_2"][0].partition_broadcast(P)).then_inc(s["cmp_pos_in"], 16)
            act.dma_start(qk_norm[:, 1, :], io["nsa_k_norm_2"][1].partition_broadcast(P)).then_inc(s["cmp_pos_in"], 16)
            act.dma_start(qk_norm[:, 2, :], io["nsa_k_norm_2"][2].partition_broadcast(P)).then_inc(s["cmp_pos_in"], 16)
            act.dma_start(cmp_norm[:, :], io["nsa_k_norm_2"][0].partition_broadcast(P)).then_inc(s["cmp_pos_in"], 16)

            def x_tile_ready(stage, t):
                act.wait_ge(s["x_ready" if t < 2 else "x_ready_v"], 2 * stage + t % 2 + 1)

            def norm(i):
                if i == 0:
                    act.wait_ge(s["x_in"], 16)
                for t in range(NT):
                    if i:
                        x_tile_ready(i - 1, t)
                    step(a.activation(XN[i][:, t], x_tok[:, t], ACT.Square, accum_out=stat[:, t:t + 1]))
                after()
                a.activation(stat[:, 4:8], stat[:, 0:4], ACT.Sqrt, scale=1.0 / D, bias=eps[:, :]).then_inc(s["norm_rms"], 1)
                for key, slot, at, n in EARLY.get(i, []):
                    high(key, arrived(act, slot, (0,))[:, at:at + n], w2_hi if i == 2 else w_hi)
                norm_out(i)

            def norm_out(i):
                if i in MIXER_NORM:
                    if i:
                        act.wait_ge(s["mod_ready"], MOD_READY[NORM_MOD[i]])
                    _, gain, shift = NORM_OUT[i][0]
                    for kt in range(KT):
                        if kt >= 2:
                            act.wait_ge(s["x0_split"], KT * MIXER_NORM[i] + kt - 1)
                        p = filled(act, ("xT", i, kt))
                        a.activation(ada_acc[:, kt % 2], p, ACT.Identity, scale=gain[:, kt:kt + 1],
                                     bias=0.0 if shift is None else shift[:, kt:kt + 1]).then_inc(free(("xT", i, kt)), 1)
                    return
                if i in FFN_NORM:
                    if i >= 2:
                        act.wait_ge(s["mod_ready"], MOD_READY[NORM_MOD[i]])
                    _, gain, shift = NORM_OUT[i][0]
                    for kt in range(KT):
                        if kt >= 4:
                            act.wait_ge(s["x_split"], (KT + FT) * FFN_NORM[i] + kt - 3)
                        p = filled(act, ("xT", i, kt))
                        a.activation(ftmp[:, kt % 4], p, ACT.Identity, scale=gain[:, kt:kt + 1],
                                     bias=0.0 if shift is None else shift[:, kt:kt + 1]).then_inc(free(("xT", i, kt)), 1)
                    return
                if i >= 2:
                    act.wait_ge(s["mod_ready"], MOD_READY[NORM_MOD[i]])
                for kt in range(0, KT, 2):
                    p = filled(act, ("xT", i, kt))
                    outs = NORM_OUT[i]
                    for j, (dst, gain, shift) in enumerate(outs):
                        ins = a.activation(dst[:, kt], p, ACT.Identity, scale=gain[:, kt:kt + 1],
                                           bias=0.0 if shift is None else shift[:, kt:kt + 1])
                        if j == len(outs) - 1:
                            ins.then_inc(free(("xT", i, kt)), 1)

            def post_rms(i, y, keys):
                for t in range(NT):
                    for _, tt, key in keys:
                        if tt == t:
                            evacuated(act, key)
                    step(a.activation(junk[:, 0:1024], y[:, t], ACT.Square, accum_out=stat[:, 16 + t:17 + t]))
                    after()
                a.activation(stat[:, 20:24], stat[:, 16:20], ACT.Sqrt, scale=1.0 / D, bias=eps[:, :]).then_inc(s["y_rms"], 1)

            def high(key, src, to=w_hi):
                if key in highs:
                    return
                highs.add(key)
                n, depth = split_at[key], to.shape[1]
                if n >= depth:
                    piece_read(act, n - depth)
                a.activation(to[:, n % depth, 0:src.shape[-1]], src, ACT.Copy).then_inc(s["hi_done"], 1)

            def out_parts(n, name):
                for kind, i in OUT_STEPS:
                    if kind == "x":
                        p = filled(act, (name, "T", i))
                        a.activation(x_hi[:, i], p, ACT.Copy).then_inc(s["out_hi"], 1)
                    else:
                        w = arrived(act, (name, i // 4), ((i % 4) // 2,))
                        high(((name, i // 4), i % 4), w[:, (i % 4) * PIECE:(i % 4 + 1) * PIECE])

            def up_out(i, u):
                up_first(i, u)
                up_silu(i, u)

            def up_first(i, u):
                for q in range(4):
                    buf = ftmp[:, 4 * (u % 2) + q]
                    if i == 0:
                        n = 22 * (q // 2) + 2 * u + q % 2
                        if u >= 2:
                            act.wait_ge(s["hid_done"], 2 * (u - 1))
                        if u < 2 and q == 0:
                            act.wait_ge(s["x_split"], KT)
                        p = filled(act, ("up", i, u, q))
                        a.activation(buf, p, ACT.Identity, scale=vec[:, CONV + 88 + n:CONV + 89 + n],
                                     bias=vec[:, CONV + 132 + n:CONV + 133 + n]).then_inc(s["conv_pre"], 1)
                    elif q < 2:
                        if u >= 2:
                            evacuated(act, ("up", i, u - 2, 2 + q))
                        p = filled(act, ("up", i, u, q))
                        a.activation(buf, p, ACT.Silu).then_inc(free(("up", i, u, q)), 1)

            def up_silu(i, u):
                if i == 0:
                    for q in range(2):
                        evacuated(act, ("up", i, u, q))
                        a.activation(ftmp[:, 4 * (u % 2) + q], ftmp[:, 4 * (u % 2) + q], ACT.Silu).then_inc(s["hid_gate"], 1)

            def ffn(i):
                for u in range(FFN_UNITS):
                    w = arrived(act, ("up", i, u), (0,))
                    for q in range(4):
                        if q == 2:
                            arrived(act, ("up", i, u), (1,))
                        high(("up", i, u, q), w[:, q * PIECE:(q + 1) * PIECE])
                        if u and q == 0:
                            up_first(i, u - 1)
                        if u and q == 2:
                            up_silu(i, u - 1)
                up_out(i, FFN_UNITS - 1)
                for g, (k0, n) in enumerate(down_groups):
                    w = arrived(act, ("down", i, g), (0,))
                    for k in range(k0, k0 + n):
                        if k == k0 + n // 2:
                            arrived(act, ("down", i, g), (1,))
                        high(("down", i, k), in_halves(w, n // 2, PIECE)[:, (k - k0) // (n // 2), (k - k0) % (n // 2)])
                        hid_ready(act, i, k)
                        if k == 0:
                            filled(act, ("up", i, FFN_UNITS - 1, 3))
                        if k >= 4:
                            piece_read(act, split_at[("down", i, k - 4)])
                        a.activation(hid_hi[:, k % 4], hid[:, k], ACT.Copy).then_inc(s["hid_hi"], 1)

            def attention(name, after_t):
                unit_of, n_units, (L, PB, PT), base = ATT[name]
                for i in range(n_units + 2):
                    if i < n_units:
                        u = unit_of(i)
                        evacuated(act, (name, "S", i))
                        if i >= 2:
                            filled(act, (name, "T", i - 2))
                        if i % 8 == 0 and i >= 16:
                            evacuated(act, (name, "O", i // 8 - 2, 0))
                            evacuated(act, (name, "O", i // 8 - 2, 1))
                        a.activation(PB[:, i % 2, 0:u["n"]], L[:, i % 2, 0:u["n"]], ACT.Exp, scale=-1.0,
                                     bias=neg_max[:, i % 4:i % 4 + 1],
                                     accum_out=den[:, (i // 8) % 2, u["slot"]:u["slot"] + 1]).then_inc(s["p_ready"], 1)
                    if i >= 2 and i % 2 == 0:
                        pt_out(act, a, name, i - 2)

            def pt_out(eng, e, name, i):
                unit_of, _, (_, _, PT), base = ATT[name]
                n = unit_of(i)["n"]
                if i >= 2:
                    eng.wait_ge(s["pv_done"], base + i - 1)
                p = filled(eng, (name, "T", i))
                a.activation(PT[:, i % 2, 0:n], p[:, 0:n], ACT.Copy).then_inc(free((name, "T", i)), 1)

            evacuated(act, "vec")
            act.wait_ge(s["e_done"], 1)
            a.activation(c_act[:, :], vcol("c_2"), ACT.Silu).then_inc(s["c_act_done"], 1)
            norm(0)
            def p1_out(k, t):
                name = P1_ORDER[k]
                if name == "rv" or name == "rg":
                    p = filled(act, (name, t))
                    dst, f = (rv_tok, ACT.Copy) if name == "rv" else (rg_tok, ACT.Silu)
                    a.activation(dst[:, t], p, f).then_inc(free((name, t)), 1)
                    return
                p = filled(act, (name, "T", t))
                if name == "kk":
                    act.wait_ge(s["zero_done"], 2)
                    for q in range(2):
                        d = slice(64 * q, 64 * q + 64)
                        ins = a.activation(T1["kk"][d, q, :, t * P:(t + 1) * P],
                                           p[d, 0:2 * P].rearrange("p (k n) -> p k n", k=2), ACT.Copy)
                    ins.then_inc(free((name, "T", t)), 1)
                    return
                a.activation(T1[name][:, :, t * P:(t + 1) * P], p.rearrange("p (k n) -> p k n", k=4), ACT.Copy)\
                    .then_inc(free((name, "T", t)), 1)

            for g, (k, q) in enumerate(P1_PIECES):
                w = arrived(act, P1_ORDER[k], (q // 2,))
                high((P1_ORDER[k], q), p1_piece(w, k, q), w0_hi)
                if g >= 5:
                    p1_out(P1_PIECES[g - 5][0], P1_PIECES[g - 5][1])
            for k, t in P1_PIECES[-5:]:
                p1_out(k, t)
            act.wait_ge(s["zero_done"], 3)
            for t in range(NT):
                evacuated(act, ("rk", "T", t))
            a.activation(rk_pair[1][64:128], rk_pair[0][64:128], ACT.Copy).then_inc(s["rk_shifted"], 1)
            i = 0
            for t in range(1, NT):
                n = (t + 1) * P
                for h in range(RH):
                    p = filled(act, ("index", t, h))
                    if i >= 2:
                        act.wait_ge(s["rel_used"], i - 1)
                    a.activation(rel[:, i % 2, 0:n], p[:, 0:n], ACT.Relu).then_inc(free(("index", t, h)), 1)
                    i += 1
            for h in range(RH):
                for m in range(NT):
                    n = S - m * P
                    o = [0, 512, 896, 1152][m]
                    if h >= 2 and m == 0:
                        act.wait_ge(s["ret_pv"], h - 1)
                    p = filled(act, ("ret_s", h, m))
                    a.activation(sT[:, h % 2, o:o + n], p[:, 0:n], ACT.Copy).then_inc(free(("ret_s", h, m)), 1)
            for t in range(NT):
                p = filled(act, ("ret_o", t))
                if t >= 1:
                    act.wait_ge(s["ret_rms"], t)
                a.activation(junk[:, 0:512], p, ACT.Square).then_inc(s["ret_square"], 1)
            act.wait_ge(s["ret_rms"], NT)
            a.activation(stat[:, 64:96], stat[:, 32:64], ACT.Sqrt, scale=1.0 / HD, bias=eps[:, :]).then_inc(s["ret_square"], 1)
            attention("dsa", None)
            out_parts(0, "mix1")
            post_rms(0, y1, tok_keys("mix1"))
            norm(1)
            ffn(0)
            post_rms(1, yf, down_keys(0))
            norm(2)
            def h_result(key, k):
                name, u = key
                if name != "hf":
                    if k < 4:
                        p = filled(act, (name, u, k))
                        dst = {"hq": HQ[:, 4 * u + k], "hg": sg_tok[:, k, u * 512:(u + 1) * 512],
                               "hi": v_tok[:, k, u * 512:(u + 1) * 512]}[name]
                        a.activation(dst, p, ACT.Copy if name == "hi" else ACT.Silu).then_inc(free((name, u, k)), 1)
                    return
                fa, fe = f_work
                if k < 2:
                    if u:
                        act.wait_ge(s["logf_done"], 4)
                    for j in (2 * k, 2 * k + 1):
                        p = filled(act, ("hf", u, j))
                        step(a.activation(fa[:, j * S:(j + 1) * S], p, ACT.Abs))
                elif k == 2:
                    after()
                    step(a.activation(fe, fa, ACT.Exp, scale=-1.0))
                elif k == 3:
                    after()
                    a.activation(fa, fe, ACT.Ln, bias=1.0).then_inc(s["f_abs"], 1)
                elif k == 7:
                    for j in range(4):
                        evacuated(act, ("hf", u, j))
                    a.activation(HK[:, 4 * u:4 * u + 4], HK[:, 4 * u:4 * u + 4], ACT.Exp).then_inc(s["k_done"], 1)

            for g, (key, k) in enumerate(H_PIECES):
                w = arrived(act, key, (k // 4,))
                high((key, k), w[:, k * S:(k + 1) * S], w2_hi)
                if g >= H_LAG:
                    h_result(*H_PIECES[g - H_LAG])
            for piece in H_PIECES[-H_LAG:]:
                h_result(*piece)

            def ho_squares(h):
                evacuated(act, ("ho", h))
                after()
                for t in range(NT):
                    step(a.activation(junk[:, t * P:(t + 1) * P], v_tok[:, t, h * P:(h + 1) * P], ACT.Square,
                                      accum_out=stat[:, 96 + 8 * t + h:97 + 8 * t + h]))

            for h in range(HH + 1):
                if h >= 2:
                    ho_squares(h - 2)
                if h < HH:
                    G = HG[:, h].rearrange("p (t n) -> p t n", t=NT)
                    for l0, l1 in ((0, 4), (4, LEVELS)):
                        act.wait_ge(s["d_sub"], 2 * (LEVELS * h + l1))
                        w = lvl[h % 2][:, l0:l1]
                        a.activation(w, w, ACT.Exp).then_inc(s["d_exp"], 1)
                    if h >= 1:
                        filled(act, ("far", h - 1, 1))
                        act.wait_ge(s["q1_done"], 4 * h)
                    a.activation(q1[:, 0:2], G[:, 1:3], ACT.Exp).then_inc(s["eq_done"], 1)
                    a.activation(q1[:, 3], G[:, 3], ACT.Exp).then_inc(s["eq_done"], 1)
                    act.wait_ge(s["tabs_done"], h + 1)
                    a.activation(q1[:, 2], G[:, 3], ACT.Exp, bias=G[:, 2, P - 1:P]).then_inc(s["eq_done"], 1)
                    for t in range(3):
                        a.activation(k1[:, t], G[:, t], ACT.Exp, scale=-1.0, bias=G[:, t, P - 1:P]).then_inc(s["eq_done"], 1)
                    a.activation(k1[:, 3], G[:, 0], ACT.Exp, scale=-1.0, bias=tot[:, 0:1]).then_inc(s["eq_done"], 1)
                if h >= 1:
                    if h >= 3:
                        filled(act, ("ho", h - 3))
                    p0 = filled(act, ("far", h - 1, 0))
                    a.activation(attn[:, (h - 1) % 2, 0, P:S], p0[:, 0:3 * P], ACT.Copy).then_inc(free(("far", h - 1, 0)), 1)
                    p1 = filled(act, ("far", h - 1, 1))
                    a.activation(attn[:, (h - 1) % 2, 1, 2 * P:S], p1[:, 0:2 * P], ACT.Copy)
                    a.activation(attn[:, (h - 1) % 2, 2, 3 * P:S], p1[:, 2 * P:3 * P], ACT.Copy).then_inc(free(("far", h - 1, 1)), 1)
            ho_squares(HH - 1)
            after()
            a.activation(stat[:, 128:160], stat[:, 96:128], ACT.Sqrt, scale=1.0 / P, bias=eps[:, :]).then_inc(s["ho_rms"], 1)
            out_parts(1, "mix2")
            norm(3)
            ffn(1)
            norm(4)
            for u in range(2):
                for t in range(NT):
                    p = filled(act, ("kvs", u, t))
                    a.activation(v_nsa[:, t, u], p[:, 256:512], ACT.Copy).then_inc(s["kvraw"], 1)
                    a.activation(raw[:, t, 16 + 4 * u:20 + 4 * u], p[:, 0:256].rearrange("p (h d) -> p h d", h=4), ACT.Copy)\
                        .then_inc(free(("kvs", u, t)), 1)
            for u in range(2):
                for t in range(NT):
                    p = filled(act, ("nq", u, t))
                    a.activation(raw[:, t, 8 * u:8 * u + 8], p.rearrange("p (h d) -> p h d", h=8), ACT.Copy)\
                        .then_inc(free(("nq", u, t)), 1)
            for t in range(NT):
                p = filled(act, ("nq", 2, t))
                a.activation(gates_e[:, t], p[:, 0:48], ACT.Exp, scale=-1.0).then_inc(free(("nq", 2, t)), 1)
            for kv in range(2):
                act.dma_start(w2_sb[:, kv], io["cmp_w2_2"][kv].rearrange("(n p) d -> p n d", p=P)).then_inc(s["w2_in"], 16)
            act.wait_ge(s["raw_done"], 3 * NT)
            a.activation(stat[:, 128:224], stat[:, 32:128], ACT.Sqrt, scale=1.0 / HD, bias=eps[:, :]).then_inc(s["raw_rms"], 1)
            for kv in range(2):
                for n in range(2):
                    p = filled(act, ("cmp1", kv, n))
                    a.activation(h1[:, kv, n], p[:, 0:4 * NCMP].rearrange("p (h i) -> p h i", h=4), ACT.Silu)\
                        .then_inc(free(("cmp1", kv, n)), 1)
            act.wait_ge(s["cmp_sq"], 1)
            a.activation(stat[0:NCMP, 248:252], stat[0:NCMP, 244:248], ACT.Sqrt, scale=1.0 / HD, bias=eps[0:NCMP, :]).then_inc(s["cmp_rms"], 1)
            for t in range(NT):
                for j in (0, 2, 1, 3, 4):
                    p = filled(act, ("nT", t, j))
                    dst = [qn_t[:, 0:4], qn_t[:, 4:8], qr_t[:, 0:4], qr_t[:, 4:8], k_t][j]
                    a.activation(dst[:, :, t * P:(t + 1) * P], p.rearrange("p (k n) -> p k n", k=4), ACT.Copy)\
                        .then_inc(free(("nT", t, j)), 1)
            for t in range(NT):
                evacuated(act, ("nT", t, 4))
            act.wait_ge(s["keys_zero"], 2)
            a.activation(k_pair[1][64:128], k_pair[0][64:128], ACT.Copy).then_inc(s["k_shifted"], 1)
            for i in range(len(GROUPS) + 1):
                if i < len(GROUPS):
                    act.wait_ge(s["cmp_l"], i + 1)
                    if i >= 2:
                        filled(act, ("cT", i - 2))
                    a.activation(cp[:, i % 2, :, 0:NCMP], cl[:, i % 2], ACT.Exp, scale=SCALE).then_inc(s["cmp_p"], 1)
                if i >= 1:
                    if i >= 3:
                        filled(act, ("cO", i - 3))
                    p = filled(act, ("cT", i - 1))
                    a.activation(cpt[:, (i - 1) % 2], p[:, 0:256].rearrange("p (q n) -> p q n", q=2), ACT.Copy)\
                        .then_inc(free(("cT", i - 1)), 1)
            attention("nsa", None)
            out_parts(2, "mix3")
            norm(5)
            ffn(2)
            for t in range(NT):
                x_tile_ready(5, t)
                act.dma_start(out[0, t * P:(t + 1) * P, :], x_tok[:, t]).then_inc(s["out_done"], 16)
            act.wait_ge(s["out_done"], 16 * NT)

        @block.vector
        def _(dve):
            v = nc.vector
            step, after = own_order(dve, s["dve_step"])
            lows = set()

            def bcast(ap, shape):
                return ap.broadcast_to(shape)

            def norm(i):
                dve.wait_ge(s["norm_rms"], i + 1)
                step(v.reciprocal(stat[:, 8:12], stat[:, 4:8]))
                after()
                for t in range(NT):
                    v.tensor_scalar(XN[i][:, t], x_tok[:, t], stat[:, 8 + t:9 + t], None, ALU.mult).then_inc(s["xn_ready"], 1)
                for key, slot, at, n in EARLY.get(i, []):
                    low(key, arrived(dve, slot, (0,))[:, at:at + n], *((w2_lo, w2_hi) if i == 2 else (w_lo, w_hi)))
                if i in MIXER_NORM:
                    if i == 0:
                        filled(dve, ("xT", 0, KT - 1))
                    for kt in range(KT):
                        evacuated(dve, ("xT", i, kt))
                        v.tensor_copy(x_hi[:, kt], ada_acc[:, kt % 2]).then_inc(s["x0_hi"], 1)
                        dve.wait_ge(s["x0_hi"], KT * MIXER_NORM[i] + kt + 1)
                        v.tensor_tensor((x2_lo if i else x0_lo)[:, kt], ada_acc[:, kt % 2], x_hi[:, kt].bitcast(F32), ALU.subtract)\
                            .then_inc(s["x0_split"], 1)
                    return
                if i in FFN_NORM:
                    for kt in range(KT):
                        evacuated(dve, ("xT", i, kt))
                        v.tensor_copy(x_hi[:, kt], ftmp[:, kt % 4]).then_inc(s["whole_done"], 1)
                        dve.wait_ge(s["whole_done"], KT * FFN_NORM[i] + kt + 1)
                        v.tensor_tensor(x_lo[:, kt], ftmp[:, kt % 4], x_hi[:, kt].bitcast(F32), ALU.subtract)\
                            .then_inc(s["x_split"], 1)
                    return
                for kt in range(1, KT, 2):
                    p = filled(dve, ("xT", i, kt))
                    outs = NORM_OUT[i]
                    if i >= 2:
                        dve.wait_ge(s["mod_ready"], MOD_READY[NORM_MOD[i]])
                    for j, (dst, gain, shift) in enumerate(outs):
                        if shift is None:
                            ins = v.tensor_scalar(dst[:, kt], p, gain[:, kt:kt + 1], None, ALU.mult)
                        else:
                            ins = v.tensor_scalar(dst[:, kt], p, gain[:, kt:kt + 1], shift[:, kt:kt + 1], ALU.mult, ALU.add)
                        if j == len(outs) - 1:
                            ins.then_inc(free(("xT", i, kt)), 1)

            def post_norm(stage, i, y, keys):
                for half, t, key in keys:
                    p = filled(dve, key)
                    v.tensor_copy(y[:, t, half * HALF:(half + 1) * HALF], p).then_inc(free(key), 1)
                dve.wait_ge(s["y_rms"], i + 1)
                step(v.reciprocal(stat[:, 24:28], stat[:, 20:24]))
                after()
                dve.wait_ge(s["row_in"], 32)
                for t in range(NT):
                    v.scalar_tensor_tensor(y[:, t], y[:, t], stat[:, 24 + t:25 + t], row[:, i], ALU.mult, ALU.mult)\
                        .then_inc(s["y_scaled"], 1)
                for t in (2, 3):
                    dve.wait_ge(s["y_scaled"], NT * stage + t + 1)
                    v.tensor_tensor(x_tok[:, t], x_tok[:, t], y[:, t], ALU.add).then_inc(s["x_ready_v"], 1)

            def post_gate(stage, m, y, keys):
                for half, t, key in keys:
                    p = filled(dve, key)
                    evacuated(dve, ("ada", m, 4 + half))
                    v.tensor_tensor(y[:, t, half * HALF:(half + 1) * HALF], p, row[:, m % 2, half * HALF:(half + 1) * HALF],
                                    ALU.mult).then_inc(free(key), 1)
                for t in (2, 3):
                    for _, tt, key in keys:
                        if tt == t:
                            evacuated(dve, key)
                    v.tensor_tensor(x_tok[:, t], x_tok[:, t], y[:, t], ALU.add).then_inc(s["x_ready_v"], 1)

            def out_parts(n, name):
                for kind, i in OUT_STEPS:
                    if kind == "x":
                        dve.wait_ge(s["out_hi"], KT * n + i + 1)
                        p = filled(dve, (name, "T", i))
                        v.tensor_tensor(x_lo[:, i], p, x_hi[:, i].bitcast(F32), ALU.subtract).then_inc(free((name, "T", i)), 1)
                    else:
                        w = arrived(dve, (name, i // 4), ((i % 4) // 2,))
                        low(((name, i // 4), i % 4), w[:, (i % 4) * PIECE:(i % 4 + 1) * PIECE])

            def ada_sum(m, j):
                for k in range(KT):
                    ada_term(m, j, k)

            def ada_term(m, j, k):
                n = ADA_N[(m, j)]
                w = arrived(dve, ("ada", m, j), (k // 4,)).rearrange("p (k n) -> p k n", k=KT)
                acc = ada_acc[:, n % 2]
                if k == 0:
                    if n >= 2:
                        filled(dve, ("ada",) + ADA[n - 2])
                    step(v.tensor_scalar(acc, w[:, 0], c_act[:, 0:1], None, ALU.mult))
                    return
                if k == 4:
                    dve.wait_ge(s["acc_half"], n + 1)
                else:
                    after()
                ins = v.scalar_tensor_tensor(acc, w[:, k], c_act[:, k:k + 1], acc, ALU.mult, ALU.add)
                if k == 3:
                    ins.then_inc(s["acc_half"], 1)
                elif k < KT - 1:
                    step(ins)
                else:
                    ins.then_inc(s["acc_done"], 1)

            def ada_out(m, j):
                p = filled(dve, ("ada", m, j))
                if j >= 4:
                    dve.wait_ge(s[f"gate_row_in{m % 2}"], 16 * (m // 2 + 1))
                    r = row[:, m % 2, (j - 4) * HALF:(j - 3) * HALF]
                    v.tensor_tensor(r, p, r, ALU.add).then_inc(free(("ada", m, j)), 1)
                    return
                after()
                prod = junk2.rearrange("p (k n) -> p k n", k=4)
                step(v.tensor_tensor(prod, p.rearrange("p (k n) -> p k n", k=4), bcast(ident.unsqueeze(1), [P, 4, P]), ALU.mult))
                after()
                raw_col = stat[:, 224 + 4 * (j % 2):228 + 4 * (j % 2)]
                v.tensor_reduce(raw_col, prod, AX, ALU.add).then_inc(free(("ada", m, j)), 1)
                evacuated(dve, ("ada", m, j))
                dst = mod[:, m, 1, 4 * j:4 * j + 4] if j < 2 else raw_col
                step(v.tensor_tensor(dst, raw_col, vec[:, BIAS + 24 * m + 4 * j:BIAS + 24 * m + 4 * j + 4], ALU.add))
                after()
                if j >= 2:
                    ins = v.scalar_tensor_tensor(mod[:, m, 0, 4 * (j - 2):4 * (j - 1)], raw_col, 1.0,
                                                 MOD_GAIN[m][:, 4 * (j - 2):4 * (j - 1)], ALU.add, ALU.mult)
                    if j == 3:
                        ins.then_inc(s["mod_ready"], 1)
                    else:
                        step(ins)

            def low(key, src, to=w_lo, hi=w_hi):
                if key in lows:
                    return
                lows.add(key)
                n = split_at[key]
                dve.wait_ge(s["hi_done"], n + 1)
                width, depth = src.shape[-1], to.shape[1]
                v.tensor_tensor(to[:, n % depth, 0:width], src, hi[:, n % depth, 0:width].bitcast(F32), ALU.subtract).then_inc(s["lo_done"], 1)

            def up_out(i, u):
                up_taps(i, u, (0, 1, 2, 3))
                up_gated(i, u)

            def up_taps(i, u, tiles):
                for q in tiles:
                    if i:
                        continue
                    n = 22 * (q // 2) + 2 * u + q % 2
                    buf = ftmp[:, 4 * (u % 2) + q]
                    dve.wait_ge(s["conv_pre"], 4 * u + q + 1)
                    p = filled(dve, ("up", i, u, q))
                    step(v.scalar_tensor_tensor(buf[:, 1:S], p[:, 0:S - 1], vec[:, CONV + 44 + n:CONV + 45 + n],
                                                buf[:, 1:S], ALU.mult, ALU.add))
                    after()
                    v.scalar_tensor_tensor(buf[:, 2:S], p[:, 0:S - 2], vec[:, CONV + n:CONV + 1 + n],
                                           buf[:, 2:S], ALU.mult, ALU.add).then_inc(free(("up", i, u, q)), 1)

            def up_gated(i, u):
                for q in range(2):
                    gate, value = ftmp[:, 4 * (u % 2) + q], ftmp[:, 4 * (u % 2) + 2 + q]
                    if i == 0:
                        dve.wait_ge(s["hid_gate"], 2 * u + q + 1)
                        evacuated(dve, ("up", i, u, 2 + q))
                        v.tensor_tensor(hid[:, 2 * u + q], gate, value, ALU.mult).then_inc(s["hid_done"], 1)
                    else:
                        evacuated(dve, ("up", i, u, q))
                        p = filled(dve, ("up", i, u, 2 + q))
                        v.tensor_tensor(hid[:, 2 * u + q], gate, p, ALU.mult).then_inc(free(("up", i, u, 2 + q)), 1)

            def ffn(i):
                for u in range(FFN_UNITS):
                    w = arrived(dve, ("up", i, u), (0,))
                    for q in range(4):
                        if q == 2:
                            arrived(dve, ("up", i, u), (1,))
                        low(("up", i, u, q), w[:, q * PIECE:(q + 1) * PIECE])
                        if u and q < 2:
                            up_taps(i, u - 1, (2 * q, 2 * q + 1))
                        if u and q == 2:
                            up_gated(i, u - 1)
                    for mj in ada_after.get((i, u - 2), []):
                        ada_out(*mj)
                    for mj in ada_after.get((i, u), []):
                        ada_sum(*mj)
                up_out(i, FFN_UNITS - 1)
                for u in (FFN_UNITS - 2, FFN_UNITS - 1):
                    for mj in ada_after.get((i, u), []):
                        ada_out(*mj)
                for g, (k0, n) in enumerate(down_groups):
                    w = arrived(dve, ("down", i, g), (0,))
                    for k in range(k0, k0 + n):
                        if k == k0 + n // 2:
                            arrived(dve, ("down", i, g), (1,))
                        low(("down", i, k), in_halves(w, n // 2, PIECE)[:, (k - k0) // (n // 2), (k - k0) % (n // 2)])
                        dve.wait_ge(s["hid_hi"], FT * i + k + 1)
                        v.tensor_tensor(hid_lo[:, k % 4], hid[:, k], hid_hi[:, k % 4].bitcast(F32), ALU.subtract)\
                            .then_inc(s["x_split"], 1)
                    for mj in ada_down.get(i, [])[g:g + 1]:
                        ada_sum(*mj)

            def rope(src, t, a, b, heads, read=None):
                cos, sin, nsin = [rope_t[:, i, t] for i in range(3)]
                sv = src.rearrange("p (h q d) -> p h q d", h=heads, q=2)
                av = a.rearrange("p (h q d) -> p h q d", h=heads, q=2)
                bv = b.rearrange("p (h q d) -> p h q d", h=heads, q=2)
                step(v.tensor_tensor(av, sv, bcast(cos.unsqueeze(1).unsqueeze(1), [P, heads, 2, HD // 2]), ALU.mult))
                step(v.tensor_tensor(bv[:, :, 0], sv[:, :, 1], bcast(nsin.unsqueeze(1), [P, heads, HD // 2]), ALU.mult))
                ins = v.tensor_tensor(bv[:, :, 1], sv[:, :, 0], bcast(sin.unsqueeze(1), [P, heads, HD // 2]), ALU.mult)
                if read is None:
                    step(ins)
                else:
                    ins.then_inc(free(read), 1)
                    evacuated(dve, read)
                after()

            def raw_squares(t, h0):
                w = raw[:, t, h0:h0 + 8, :]
                sq = junk[:, 0:HALF].rearrange("p (h d) -> p h d", h=8)
                step(v.tensor_tensor(sq, w, w, ALU.mult))
                after()
                v.tensor_reduce(stat[:, 32 + 24 * t + h0:40 + 24 * t + h0], sq, AX, ALU.add).then_inc(s["raw_done"], 1)
                raw_sums[0] += 1
                dve.wait_ge(s["raw_done"], raw_sums[0])

            raw_sums = [0]

            def attention(name, bias_ready, finish):
                unit_of, n_units, (L, PB, PT), base = ATT[name]
                for i in range(n_units + 4):
                    if i < n_units:
                        u = unit_of(i)
                        bias_ready(i)
                        p = filled(dve, (name, "S", i))
                        if i >= 2:
                            dve.wait_ge(s["p_ready"], base + i - 1)
                        v.tensor_tensor_reduce(L[:, i % 2, 0:u["n"]], p[:, 0:u["n"]], u["bias"], -SCALE, 3e38,
                                               ALU.add, ALU.min, neg_max[:, i % 4:i % 4 + 1]).then_inc(free((name, "S", i)), 1)
                    if 2 <= i < n_units + 2 and i % 2 == 1:
                        j = i - 2
                        if j >= 2:
                            dve.wait_ge(s["pv_done"], base + j - 1)
                        n = unit_of(j)["n"]
                        pt = filled(dve, (name, "T", j))
                        v.tensor_copy(PT[:, j % 2, 0:n], pt[:, 0:n]).then_inc(free((name, "T", j)), 1)
                    if i >= 4 and (i - 4) % 8 == 7:
                        finish((i - 4) // 8, base)

            v.memset(eps[:, :], EPS).then_inc(s["e_done"], 1)
            p = filled(dve, "vec")
            v.tensor_copy(vec[:, :], p[:, 0:416]).then_inc(free("vec"), 1)
            norm(0)
            dve.wait_ge(s["consts_in"], 32)
            step(v.tensor_copy(masks[:, :, :], mask_rows))
            dve.wait_ge(s["c_act_done"], 1)
            def roped(k, t):
                name, n = P1_ORDER[k], NT * k + t
                p = filled(dve, (name, t))
                if n >= 2:
                    filled(dve, (ROPED[(n - 2) // NT], "T", (n - 2) % NT))
                a, b, o = rope_a[:, n % 2], rope_b[:, n % 2], rope_o[:, n % 2]
                if name == "kk":
                    step(v.tensor_copy(av_tok[:, t], p[:, 64:128]))
                    step(v.tensor_scalar(iw[:, t], p[:, 192:200], (RH * HD) ** -0.5, None, ALU.mult))
                    for j, c in enumerate((0, 128)):
                        rope(p[:, c:c + 64], t, a[:, 64 * j:64 * j + 64], b[:, 64 * j:64 * j + 64], 1, (name, t) if j else None)
                    av = a[:, 0:128].rearrange("p (j d) -> p j d", j=2).unsqueeze(2)
                    bv = b[:, 0:128].rearrange("p (j d) -> p j d", j=2).unsqueeze(2)
                    v.tensor_tensor(o[:, 0:256].rearrange("p (j q d) -> p j q d", j=2, q=2), bcast(av, [P, 2, 2, HD]),
                                    bcast(bv, [P, 2, 2, HD]), ALU.add).then_inc(s["rope_done"], 1)
                else:
                    rope(p, t, a, b, 8, (name, t))
                    v.tensor_tensor(o, a, b, ALU.add).then_inc(s["rope_done"], 1)

            for k, q in P1_PIECES:
                w = arrived(dve, P1_ORDER[k], (q // 2,))
                low((P1_ORDER[k], q), p1_piece(w, k, q), w0_lo, w0_hi)
                if k and P1_ORDER[k - 1] in ROPED:
                    roped(k - 1, q)
            i = 0
            for t in range(1, NT):
                n = (t + 1) * P
                w = isc[t - 1]
                for h in range(RH):
                    evacuated(dve, ("index", t, h))
                    if h:
                        dve.wait_ge(s["rel_used"], i)
                        v.scalar_tensor_tensor(w, rel[:, i % 2, 0:n], iw[:, t, h:h + 1], w, ALU.mult, ALU.add).then_inc(s["rel_used"], 1)
                    else:
                        v.tensor_scalar(w, rel[:, i % 2, 0:n], iw[:, t, h:h + 1], None, ALU.mult).then_inc(s["rel_used"], 1)
                    i += 1
                dve.wait_ge(s["rel_used"], i)
                step(v.tensor_tensor(w[:, t * P:n], w[:, t * P:n], strip[:, 3 * P:], ALU.add))
                after()
            for r in range(TOPK // 8):
                for t in range(1, NT):
                    after(2)
                    step(v.max(best[:, t - 1], isc[t - 1]))
                for t in range(1, NT):
                    after(2)
                    step(v.match_replace(isc[t - 1], best[:, t - 1], isc[t - 1], REPLACED))
            after()
            for t in range(1, NT):
                w = isc[t - 1]
                v.tensor_scalar(sel_bias[t - 1], w, REPLACED / 2, NEG, ALU.is_ge, ALU.mult).then_inc(s["picked"], 1)
            for t in range(NT):
                dve.wait_ge(s["ret_square"], t + 1)
                v.tensor_reduce(stat[:, 32 + 8 * t:40 + 8 * t], junk[:, 0:512].rearrange("p (h d) -> p h d", h=RH), AX, ALU.add)\
                    .then_inc(s["ret_rms"], 1)
            dve.wait_ge(s["ret_square"], NT + 1)
            step(v.reciprocal(stat[:, 96:128], stat[:, 64:96]))
            after()
            for t in range(NT):
                p = filled(dve, ("ret_o", t))
                v.tensor_tensor(mixed[:, t, 0:512].rearrange("p (h d) -> p h d", h=RH), p.rearrange("p (h d) -> p h d", h=RH),
                                bcast(stat[:, 96 + 8 * t:104 + 8 * t].unsqueeze(2), [P, RH, HD]), ALU.mult)\
                    .then_inc(free(("ret_o", t)), 1)

            def dsa_bias(i):
                if i % RH == 0 and i // RH >= 1:
                    dve.wait_ge(s["picked"], i // RH)

            def dsa_finish(g, base):
                dve.wait_ge(s["p_ready"], base + 8 * (g + 1))
                dve.wait_ge(s["pv_done"], base + 8 * (g + 1))
                step(v.reciprocal(rden[:, g % 2], den[:, g % 2]))
                after()
                for odd in range(2):
                    key = ("dsa", "O", g, odd)
                    p = ps[:, bank_use[key][0]]
                    v.tensor_tensor(mixed[:, g, 512:1024].rearrange("p (h q d) -> p h q d", h=4, q=2)[:, :, odd],
                                    p.rearrange("p (h d) -> p h d", h=4)[:, :, 0:HD],
                                    bcast(rden[:, g % 2].rearrange("p (h q) -> p h q", q=2)[:, :, odd].unsqueeze(2), [P, 4, HD]),
                                    ALU.mult).then_inc(free(key), 1)

            attention("dsa", dsa_bias, dsa_finish)
            out_parts(0, "mix1")
            post_norm(0, 0, y1, tok_keys("mix1"))
            norm(1)
            ffn(0)
            post_norm(1, 1, yf, down_keys(0))
            for mj in ada_down[0]:
                ada_out(*mj)
            norm(2)
            def h_log(u, j):
                dve.wait_ge(s["f_abs"], u + 1)
                p = filled(dve, ("hf", u, j))
                h = 4 * u + j
                v.scalar_tensor_tensor(HG[:, h], p, 0.0, f_work[0][:, j * S:(j + 1) * S], ALU.min, ALU.subtract).then_inc(s["logf_done"], 1)
                dve.wait_ge(s["logf_done"], h + 1)
                v.tensor_tensor(HK[:, h], HG[:, h], p, ALU.subtract).then_inc(free(("hf", u, j)), 1)

            for g, (key, k) in enumerate(H_PIECES):
                w = arrived(dve, key, (k // 4,))
                low((key, k), w[:, k * S:(k + 1) * S], w2_lo, w2_hi)
                if g >= H_LAG and H_PIECES[g - H_LAG][0][0] == "hf" and H_PIECES[g - H_LAG][1] >= 4:
                    (_, u), j = H_PIECES[g - H_LAG]
                    h_log(u, j - 4)
                    h = 4 * u + j - 4
                    evacuated(dve, ("hf", u, j - 4))
                    v.tensor_tensor_scan(HG[:, h], keep, HG[:, h], 0.0, ALU.mult, ALU.add).then_inc(s["g_done"], 1)

            def attn_diag(h, lv):
                p = filled(dve, ("diag", h, lv))
                if h >= 2 and lv == 0:
                    filled(dve, ("ho", h - 2))
                A = attn[:, h % 2].rearrange("p s n -> p (s n)")
                dst = bass.AP(A.tensor, A.offset, [A.ap[0], [S + P, NT], [1, P]])
                m = bcast(masks[:, lv, :].unsqueeze(1), [P, NT, P])
                evacuated_prev(h, lv)
                v.copy_predicated(dst, m, p.rearrange("p (s n) -> p s n", s=NT)).then_inc(free(("diag", h, lv)), 1)

            def evacuated_prev(h, lv):
                if lv:
                    evacuated(dve, ("diag", h, lv - 1))

            for h in range(HH + 1):
                if h < HH:
                    dve.wait_ge(s["g_done"], h + 1)
                    G = HG[:, h].rearrange("p (t n) -> p t n", t=NT)
                    if h:
                        dve.wait_ge(s["eq_done"], 7 * h)
                    v.tensor_tensor(tot[:, 0:1], G[:, 0, P - 1:P], G[:, 1, P - 1:P], ALU.add).then_inc(s["tabs_done"], 1)
                    dve.wait_ge(s["k_done"], 2)
                    dve.wait_ge(s["attn_zero"], 1)
                    L = lvl[h % 2]
                    for lv in range(LEVELS):
                        dve.wait_ge(s["d_exp"], 2 * h + 1 + (lv >= 4))
                        c = 1 << lv
                        for q, src in ((0, HK), (1, HQ)):
                            d = L[:, lv].rearrange("p (b q c) -> p b q c", q=2, c=c)[:, :, q]
                            w = src[:, h].rearrange("p (b q c) -> p b q c", q=2, c=c)[:, :, q]
                            v.tensor_tensor(d, d, w, ALU.mult).then_inc(s["qk_done"], 1)
                        if lv:
                            attn_diag(h, lv - 1)
                    dve.wait_ge(s["eq_done"], 7 * (h + 1))
                    K = HK[:, h].rearrange("p (t n) -> p t n", t=NT)
                    Q = HQ[:, h].rearrange("p (t n) -> p t n", t=NT)
                    v.tensor_tensor(q1[:, 0:2], q1[:, 0:2], Q[:, 1:3], ALU.mult).then_inc(s["q1_done"], 1)
                    v.tensor_tensor(q1[:, 2:4], q1[:, 2:4], bcast(Q[:, 3:4], [P, 2, P]), ALU.mult).then_inc(s["q1_done"], 1)
                    v.tensor_tensor(k1[:, 0:3], k1[:, 0:3], K[:, 0:3], ALU.mult).then_inc(s["q1_done"], 1)
                    v.tensor_tensor(k1[:, 3], k1[:, 3], K[:, 0], ALU.mult).then_inc(s["q1_done"], 1)
                    for lv in (LEVELS - 1, LEVELS):
                        attn_diag(h, lv)
                if h >= 1:
                    p = filled(dve, ("ho", h - 1))
                    v.tensor_copy(v_tok[:, :, (h - 1) * P:h * P], p.rearrange("p (t n) -> p t n", t=NT)).then_inc(free(("ho", h - 1)), 1)
            dve.wait_ge(s["ho_rms"], 1)
            step(v.reciprocal(stat[:, 160:192], stat[:, 128:160]))
            after()
            dve.wait_ge(s["sg_done"], 8)
            for t in range(NT):
                w = v_tok[:, t].rearrange("p (h d) -> p h d", h=HH)
                v.tensor_tensor(w, w, bcast(stat[:, 160 + 8 * t:168 + 8 * t].unsqueeze(2), [P, HH, P]), ALU.mult).then_inc(s["ho_scaled"], 1)
            for t in (2, 3):
                dve.wait_ge(s["ho_scaled"], t + 1)
                v.tensor_tensor(v_tok[:, t], v_tok[:, t], sg_tok[:, t], ALU.mult).then_inc(s["ho_ready"], 1)
            out_parts(1, "mix2")
            post_gate(2, 0, y2, tok_keys("mix2"))
            norm(3)
            ffn(1)
            post_gate(3, 1, yf, down_keys(1))
            for mj in ada_down[1]:
                ada_out(*mj)
            norm(4)
            for j in range(4):
                p = filled(dve, ("kvc", j))
                for q in range(2):
                    for par in range(2):
                        d = slice(64 * par, 64 * par + 64)
                        w = p[64 * q:64 * q + 64, :]
                        src = bass.AP(w.tensor, w.offset + par, [w.ap[0], [2, 16], [16, NCMP]])
                        pos = vec[d, POS + 32 * (j // 2):POS + 32 * (j // 2) + 32].rearrange("p (r e) -> p r e", e=2)[:, :, par:par + 1]
                        ins = v.tensor_tensor(win[d, j // 2, :, 2 * (j % 2) + q, :], src, bcast(pos, [64, 16, NCMP]), ALU.add)
                        if (q, par) == (1, 1):
                            ins.then_inc(free(("kvc", j)), 1)
                        else:
                            ins.then_inc(s["u_done"], 1)
            for u in range(2):
                for t in range(NT):
                    evacuated(dve, ("kvs", u, t))
                    if u == 1:
                        raw_squares(t, 16)
            for u in range(2):
                for t in range(NT):
                    evacuated(dve, ("nq", u, t))
                    raw_squares(t, 8 * u)
            for t in range(NT):
                evacuated(dve, ("nq", 2, t))
            step(v.tensor_scalar(gates_e[:, :, :], gates_e[:, :, :], 1.0, None, ALU.add))
            after()
            step(v.reciprocal(gates[:, :, :], gates_e[:, :, :]))
            dve.wait_ge(s["raw_rms"], 1)
            step(v.reciprocal(stat[:, 32:128], stat[:, 128:224]))
            after()
            p = filled(dve, "cmp2")
            step(v.tensor_copy(kc_raw, p[0:NCMP, 0:256]))
            v.memset(kc_t[:, :, :, :], 0.0).then_inc(s["cmp_zero"], 1)
            dve.wait_ge(s["cmp_zero"], 2)
            for gg in range(GROUP):
                ins = v.tensor_copy(vc_diag[32 * gg:32 * gg + NCMP, :, gg], p[0:NCMP, 256:512].rearrange("p (h d) -> p h d", h=4))
                if gg < GROUP - 1:
                    step(ins)
            ins.then_inc(free("cmp2"), 1)
            after()
            step(v.tensor_tensor(kc_tok, kc_raw.rearrange("p (h d) -> p h d", h=4), kc_raw.rearrange("p (h d) -> p h d", h=4), ALU.mult))
            after()
            v.tensor_reduce(stat[0:NCMP, 244:248], kc_tok, AX, ALU.add).then_inc(s["cmp_sq"], 1)
            dve.wait_ge(s["cmp_rms"], 1)
            step(v.reciprocal(stat[0:NCMP, 252:256], stat[0:NCMP, 248:252]))
            after()
            step(v.tensor_tensor(kc_tok, kc_raw.rearrange("p (h d) -> p h d", h=4),
                                       bcast(stat[0:NCMP, 252:256].unsqueeze(2), [NCMP, 4, HD]), ALU.mult))
            after()
            dve.wait_ge(s["cmp_pos_in"], 64)
            v.tensor_tensor(kc_tok, kc_tok, bcast(cmp_norm[0:NCMP, :].unsqueeze(1), [NCMP, 4, HD]), ALU.mult).then_inc(s["cmp_tok"], 1)
            p = filled(dve, "cmpT")
            w = p[:, 0:64].rearrange("p (c i) -> p c i", c=2)[:, :, 0:NCMP]
            step(v.tensor_copy(kc_t[0:64, :, 0, 0:NCMP], w[0:64]))
            after()
            v.tensor_copy(kc_t[64:128, :, 1, 0:NCMP], w[64:128]).then_inc(free("cmpT"), 1)
            def chunk_norm(i):
                t, j = i // 3, i % 3
                if i >= 2:
                    filled(dve, ("nT", (i - 2) // 3, 2 + (i - 2) % 3))
                a = n_a[:, i % 2]
                if j < 2:
                    for ko in range(2):
                        src = raw[:, t, 8 * j + 4 * ko:8 * j + 4 * ko + 4, :]
                        dst = a.rearrange("p (g q d) -> p g q d", g=4, q=2)[:, :, ko]
                        r = stat[:, 32 + 24 * t + 8 * j + 4 * ko:36 + 24 * t + 8 * j + 4 * ko]
                        ins = v.tensor_tensor(dst, src, bcast(r.unsqueeze(2), [P, 4, HD]), ALU.mult)
                        if ko == 0:
                            step(ins)
                            after()
                    ins.then_inc(s["raw_norm"], 1)
                else:
                    r = stat[:, 48 + 24 * t:56 + 24 * t]
                    v.tensor_tensor(a.rearrange("p (h d) -> p h d", h=8), raw[:, t, 16:24, :], bcast(r.unsqueeze(2), [P, 8, HD]),
                                    ALU.mult).then_inc(s["raw_norm"], 1)

            chunk_norm(0)
            for i in range(3 * NT):
                dve.wait_ge(s["gained"], i + 1)
                if i >= 2:
                    filled(dve, ("nT", (i - 2) // 3, 2 + (i - 2) % 3))
                rope(n_a[:, i % 2], i // 3, n_b[:, i % 2], n_o[:, i % 2], 8)
                if i + 1 < 3 * NT:
                    chunk_norm(i + 1)
                v.tensor_tensor(n_o[:, i % 2], n_b[:, i % 2], n_o[:, i % 2], ALU.add).then_inc(s["rope2_done"], 1)
            for i in range(len(GROUPS) + 2):
                if i < len(GROUPS):
                    t, kp = GROUPS[i]
                    L = cl[:, i % 2]
                    if i >= 2:
                        dve.wait_ge(s["cmp_p"], i - 1)
                    p = filled(dve, ("cS", i))
                    v.tensor_tensor(L.rearrange("p (q g) c -> p g q c", q=2), p.rearrange("p (g q c) -> p g q c", g=4, q=2)[:, :, :, 0:NCMP],
                                    bcast(cmp_bias[:, t].unsqueeze(1).unsqueeze(1), [P, 4, 2, NCMP]), ALU.add).then_inc(free(("cS", i)), 1)
                    evacuated(dve, ("cS", i))
                    step(v.tensor_reduce(fac[:, 32:40], L, AX, ALU.max))
                    after()
                    v.tensor_tensor(L, L, bcast(fac[:, 32:40].unsqueeze(2), [P, 8, NCMP]), ALU.subtract).then_inc(s["cmp_l"], 1)
                if 1 <= i <= len(GROUPS):
                    t, kp = GROUPS[i - 1]
                    f = fac[:, 48 + 8 * ((i - 1) % 2):56 + 8 * ((i - 1) % 2)]
                    dve.wait_ge(s["cmp_p"], i)
                    step(v.tensor_reduce(fac[:, 40:48], cp[:, (i - 1) % 2, :, 0:NCMP], AX, ALU.add))
                    after()
                    step(v.reciprocal(fac[:, 40:48], fac[:, 40:48]))
                    after()
                    step(v.scalar_tensor_tensor(f, fac[:, 40:48], row_valid[:, t:t + 1], gates[:, t, 8 * kp:8 * kp + 8],
                                                      ALU.mult, ALU.mult))
                if i >= 2:
                    t, kp = GROUPS[i - 2]
                    f = fac[:, 48 + 8 * (i % 2):56 + 8 * (i % 2)]
                    p = filled(dve, ("cO", i - 2))
                    after()
                    v.tensor_tensor(nsa_tok[:, t, kp * 512:(kp + 1) * 512].rearrange("p (h d) -> p h d", h=8),
                                    p.rearrange("p (h d) -> p h d", h=8), bcast(f.unsqueeze(2), [P, 8, HD]), ALU.mult)\
                        .then_inc(free(("cO", i - 2)), 1)
            evacuated(dve, ("cO", len(GROUPS) - 1))
            evacuated(dve, ("cO", len(GROUPS) - 2))

            def nsa_finish(g, base):
                t, kp, br = NSA_GROUPS[g]
                dve.wait_ge(s["p_ready"], base + 8 * (g + 1))
                dve.wait_ge(s["pv_done"], base + 8 * (g + 1))
                step(v.reciprocal(rden[:, g % 2], den[:, g % 2]))
                after()
                step(v.tensor_tensor(rden[:, g % 2], rden[:, g % 2], gates[:, t, 16 + 16 * br + 8 * kp:24 + 16 * br + 8 * kp], ALU.mult))
                after()
                if g >= 2:
                    dve.wait_ge(s["nsa_added"], g - 1)
                for odd in range(2):
                    key = ("nsa", "O", g, odd)
                    p = ps[:, bank_use[key][0]]
                    v.tensor_tensor(n_tmp[:, g % 2, 256 * odd:256 * odd + 256].rearrange("p (h d) -> p h d", h=4),
                                    p.rearrange("p (h d) -> p h d", h=4)[:, :, odd * HD:(odd + 1) * HD],
                                    bcast(rden[:, g % 2, 4 * odd:4 * odd + 4].unsqueeze(2), [P, 4, HD]),
                                    ALU.mult).then_inc(free(key), 1)

            def late_terms(i):
                n, k = divmod(i - 96, KT)
                if 0 <= n < 2:
                    ada_term(*ADA_LATE[n], k)

            attention("nsa", late_terms, nsa_finish)
            ada_out(*ADA_LATE[0])
            ada_sum(*ADA_LATE[2])
            ada_out(*ADA_LATE[1])
            ada_out(*ADA_LATE[2])
            out_parts(2, "mix3")
            post_gate(4, 2, y3, tok_keys("mix3"))
            norm(5)
            ffn(2)
            post_gate(5, 3, yf, down_keys(2))

        @block.tensor
        def _(pe):
            mm = nc.tensor.matmul
            tr = nc.tensor.transpose

            pe.wait_ge(s["consts_in"], 32)
            pe.wait_ge(s["rows_in"], ROWS_IN)
            b = open_bank("vec")
            tr(b[:, 0:64], vec_rows, ident[0:64, 0:64])
            tr(b[:, 64:152], conv_rows[0], ident[0:88, 0:88])
            tr(b[:, 152:240], conv_rows[1], ident[0:88, 0:88])
            tr(b[:, 240:272], pos_rows[:, 0:128], ident[0:32, 0:32])
            tr(b[:, 272:304], pos_rows[:, 128:256], ident[0:32, 0:32])
            tr(b[:, 304:416], bias_rows, ident[0:112, 0:112]).then_inc(full("vec"), 1)

            def turn(src, key):
                b = open_bank(key)
                for t in range(NT):
                    ins = tr(b[:, t * P:(t + 1) * P], src(t), ident)
                ins.then_inc(full(key), 1)

            def norm(i):
                pe.wait_ge(s["xn_ready"], NT * (i + 1))
                for kt in range(KT):
                    turn(lambda t: XN[i][:, t, kt * P:(kt + 1) * P], ("xT", i, kt))
                if i in MIXER_NORM or i in FFN_NORM:
                    return
                for kt in range(KT):
                    evacuated(pe, ("xT", i, kt))

            def tok_bank(w, h, t, key, n):
                b = open_bank(key)
                for k in range(KT):
                    ins = mm(b[:, 0:n], h[:, k, t * P:(t + 1) * P], w[:, k // 4, k % 4, :], start=(k == 0), stop=(k == KT - 1))
                ins.then_inc(full(key), 1)

            def tok_gemm(name, h, n_units, width=lambda u: 512):
                for u in range(n_units):
                    n = width(u)
                    w = in_halves(arrived(pe, (name, u)), 4, n)
                    for t in range(NT):
                        tok_bank(w, h, t, (name, u, t), n)

            def feat_gemm(ukey, h, keys):
                w = arrived(pe, ukey)[:, 0:KT * 512].rearrange("p (k n) -> p k n", k=KT)
                for j, key in enumerate(keys):
                    b = open_bank(key)
                    for k in range(KT):
                        ins = mm(b, w[:, k, j * P:(j + 1) * P], h[:, k, :], start=(k == 0), stop=(k == KT - 1))
                    ins.then_inc(full(key), 1)

            def split_piece(key, q, bank_keys, bs, n, xl=x_lo, wh=w_hi, wl=w_lo):
                i = split_at[(key, q)]
                pe.wait_ge(s["lo_done"], i + 1)
                hi, lo = [w[:, i % 2, 0:2 * n].rearrange("p (k n) -> p k n", k=2) for w in (wh, wl)]
                for t in range(NT):
                    c = slice(t * P, (t + 1) * P)
                    if q == 0:
                        bs[t] = open_bank(bank_keys[t])
                    for k in range(2):
                        b = bs[t][:, 0:n]
                        mm(b, x_hi[:, 2 * q + k, c], hi[:, k], start=((q, k) == (0, 0)), stop=False)
                        mm(b, x_hi[:, 2 * q + k, c], lo[:, k], start=False, stop=False)
                        ins = mm(b, xl[:, 2 * q + k, c], hi[:, k], start=False, stop=((q, k) == (3, 1)))
                    if q == 3:
                        ins.then_inc(full(bank_keys[t]), 1)
                if q < 3:
                    ins.then_inc(s["piece_done"], 1)

            def ada_row(m, j):
                pe.wait_ge(s["acc_done"], ADA_N[(m, j)] + 1)
                pe.wait_ge(s["ones_done"], 1)
                b = open_bank(("ada", m, j))
                mm(b, ones[:, :], ada_acc[:, ADA_N[(m, j)] % 2], start=True, stop=True).then_inc(full(("ada", m, j)), 1)

            def ffn(i):
                for u in range(FFN_UNITS):
                    keys = [("up", i, u, j) for j in range(4)]
                    bs = [None] * 4
                    for q in range(4):
                        n = split_at[("up", i, u, q)]
                        pe.wait_ge(s["lo_done"], n + 1)
                        if u == 0:
                            pe.wait_ge(s["x_split"], (KT + FT) * i + 2 * q + 2)
                        wh, wl = [w[:, n % 2].rearrange("p (k n) -> p k n", k=2) for w in (w_hi, w_lo)]
                        for j in range(4):
                            if q == 0:
                                bs[j] = open_bank(keys[j])
                            c = slice(j * P, (j + 1) * P)
                            for k in range(2):
                                first, last = (q, k) == (0, 0), (q, k) == (3, 1)
                                mm(bs[j], wh[:, k, c], x_hi[:, 2 * q + k], start=first, stop=False)
                                mm(bs[j], wh[:, k, c], x_lo[:, 2 * q + k], start=False, stop=False)
                                ins = mm(bs[j], wl[:, k, c], x_hi[:, 2 * q + k], start=False, stop=last)
                            if q == 3 and j < 3:
                                ins.then_inc(full(keys[j]), 1)
                        if q < 3:
                            ins.then_inc(s["piece_done"], 1)
                    ins.then_inc(full(keys[3]), 1)
                    for mj in ada_after.get((i, u - 1), []):
                        ada_row(*mj)
                for mj in ada_after.get((i, FFN_UNITS - 1), []):
                    ada_row(*mj)
                bs = [open_bank(("down", i, j)) for j in range(8)]
                for k in range(FT):
                    n = split_at[("down", i, k)]
                    pe.wait_ge(s["lo_done"], n + 1)
                    pe.wait_ge(s["x_split"], (KT + FT) * i + KT + k + 1)
                    for t in range(NT):
                        c = slice(t * P, (t + 1) * P)
                        for half in range(2):
                            f = slice(half * HALF, (half + 1) * HALF)
                            b = bs[2 * t + half]
                            mm(b, hid_hi[:, k % 4, c], w_hi[:, n % 2, f], start=(k == 0), stop=False)
                            mm(b, hid_hi[:, k % 4, c], w_lo[:, n % 2, f], start=False, stop=False)
                            ins = mm(b, hid_lo[:, k % 4, c], w_hi[:, n % 2, f], start=False, stop=(k == FT - 1))
                            if k == FT - 1:
                                ins.then_inc(full(("down", i, 2 * t + half)), 1)
                    if k < FT - 1:
                        ins.then_inc(s["piece_done"], 1)
                for mj in ada_down.get(i, []):
                    ada_row(*mj)

            def attention(name, ready):
                unit_of, n_units, (L, PB, PT), base = ATT[name]
                for i in range(n_units + 3):
                    if i < n_units:
                        u = unit_of(i)
                        b = open_bank((name, "S", i))
                        mm(b[:, 0:u["n"]], u["q"], u["k"], start=True, stop=True).then_inc(full((name, "S", i)), 1)
                    if 2 <= i < n_units + 2:
                        u = unit_of(i - 2)
                        pe.wait_ge(s["p_ready"], base + i - 1)
                        b = open_bank((name, "T", i - 2))
                        for c in range(u["n"] // P):
                            ins = tr(b[:, c * P:(c + 1) * P], PB[:, i % 2, c * P:(c + 1) * P], ident)
                        ins.then_inc(full((name, "T", i - 2)), 1)
                    if i >= 3:
                        j = i - 3
                        u = unit_of(j)
                        okey = (name, "O", j // 8, j % 2)
                        b = open_bank(okey) if j % 8 < 2 else ps[:, bank_use[okey][0]]
                        evacuated(pe, (name, "T", j))
                        slot = (j % 8) // 2
                        nb = u["n"] // P
                        for c in range(nb):
                            ins = mm(b[:, slot * P:(slot + 1) * P], PT[:, j % 2, c * P:(c + 1) * P], u["v"](c),
                                     start=(c == 0), stop=(c == nb - 1))
                        ins.then_inc(s["pv_done"], 1)

            def out_gemm(name, src, wait):
                wait()
                for kt in range(KT):
                    turn(lambda t: src[:, t, kt * P:(kt + 1) * P], (name, "T", kt))
                for u in range(2):
                    bs = [None] * NT
                    for q in range(4):
                        if u == 0:
                            for kt in (2 * q, 2 * q + 1):
                                evacuated(pe, (name, "T", kt))
                        split_piece((name, u), q, [(name, u, t) for t in range(NT)], bs, 512)

            norm(0)
            for k, q in P1_PIECES:
                name = P1_ORDER[k]
                if k == 0:
                    pe.wait_ge(s["x0_split"], 2 * q + 2)
                if q == 0:
                    bs = [None] * NT
                split_piece(name, q, [(name, t) for t in range(NT)], bs, sum(c for _, c in P1[name]), x0_lo, w0_hi, w0_lo)
                if k and P1_ORDER[k - 1] in ROPED:
                    before = P1_ORDER[k - 1]
                    i = NT * (k - 1) + q
                    pe.wait_ge(s["rope_done"], i + 1)
                    b = open_bank((before, "T", q))
                    nb = 2 if before == "kk" else 4
                    for c in range(nb):
                        ins = tr(b[:, c * P:(c + 1) * P], rope_o[:, i % 2, c * P:(c + 1) * P], ident)
                    ins.then_inc(full((before, "T", q)), 1)
            for t in range(1, NT):
                for h in range(RH):
                    if h == 0 and t == 1:
                        pe.wait_ge(s["zero_done"], 2)
                        for nm in ("iq", "kk"):
                            for tt in range(NT):
                                evacuated(pe, (nm, "T", tt))
                    b = open_bank(("index", t, h))
                    mm(b[:, 0:(t + 1) * P], T1["iq"][:, h // 2, t * P:(t + 1) * P], T1["kk"][:, h % 2, 1, 0:(t + 1) * P],
                       start=True, stop=True).then_inc(full(("index", t, h)), 1)
            pe.wait_ge(s["zero_done"], 4)
            for nm in ("rk", "rq", "aq"):
                for tt in range(NT):
                    evacuated(pe, (nm, "T", tt))
            for tt in range(NT):
                evacuated(pe, ("rv", tt))
            for h in range(RH + 1):
                if h < RH:
                    for m in range(NT):
                        b = open_bank(("ret_s", h, m))
                        mm(b[:, 0:S - m * P], rk_pair[h % 2][:, h // 2, m * P:(m + 1) * P], T1["rq"][:, h // 2, m * P:S],
                           start=True, stop=True).then_inc(full(("ret_s", h, m)), 1)
                if h >= 1:
                    g = h - 1
                    if h == 1:
                        obs = [open_bank(("ret_o", t)) for t in range(NT)]
                    pe.wait_ge(s["decayed"], h)
                    for t in range(NT):
                        for m in range(t + 1):
                            o = [0, 512, 896, 1152][m] + (t - m) * P
                            ins = mm(obs[t][:, g * HD:(g + 1) * HD], sT[:, g % 2, o:o + P], rv_tok[:, m, g * HD:(g + 1) * HD],
                                     start=(m == 0), stop=(m == t))
                        if h == RH:
                            ins.then_inc(full(("ret_o", t)), 1)
                    if h < RH:
                        ins.then_inc(s["ret_pv"], 1)
            attention("dsa", None)

            def wait_mix1():
                pe.wait_ge(s["mixed_ready"], NT)
                for g in range(NT):
                    evacuated(pe, ("dsa", "O", g, 0))
                    evacuated(pe, ("dsa", "O", g, 1))

            out_gemm("mix1", mixed, wait_mix1)
            norm(1)
            ffn(0)
            norm(2)
            for key, k in H_PIECES:
                name, u = key
                n = split_at[(key, k)]
                pe.wait_ge(s["lo_done"], n + 1)
                pe.wait_ge(s["x0_split"], KT + k + 1)
                hi, lo = w2_hi[:, n % 3], w2_lo[:, n % 3]
                if k == 0:
                    bs = [None] * 4
                for j in range(4):
                    if k == 0:
                        bs[j] = open_bank((name, u, j))
                    c = slice(j * P, (j + 1) * P)
                    for w, x, first, last in ((hi, x_hi, True, False), (lo, x_hi, False, False), (hi, x2_lo, False, True)):
                        start, stop = first and k == 0, last and k == KT - 1
                        if name in ("hq", "hf"):
                            ins = mm(bs[j], w[:, c], x[:, k], start=start, stop=stop)
                        else:
                            ins = mm(bs[j], x[:, k, c], w, start=start, stop=stop)
                    if k == KT - 1:
                        ins.then_inc(full((name, u, j)), 1)
                if k < KT - 1:
                    ins.then_inc(s["piece_done"], 1)
            for u in range(2):
                for t in range(NT):
                    evacuated(pe, ("hi", u, t))
            for h in range(HH + 1):
                if h < HH:
                    L = lvl[h % 2]
                    for lv in range(LEVELS + 1):
                        b = open_bank(("diag", h, lv))
                        if lv:
                            pe.wait_ge(s["qk_done"], 2 * (LEVELS * h + lv))
                        else:
                            pe.wait_ge(s["k_done"], 2)
                        for t in range(NT):
                            c = slice(t * P, (t + 1) * P)
                            k, q = (HK[:, h, c], HQ[:, h, c]) if lv == 0 else (L[:, lv - 1, c], L[:, lv - 1, c])
                            ins = mm(b[:, c], k, q, start=True, stop=True)
                        ins.then_inc(full(("diag", h, lv)), 1)
                    pe.wait_ge(s["q1_done"], 4 * (h + 1))
                    b = open_bank(("far", h, 0))
                    mm(b[:, 0:P], k1[:, 0], q1[:, 0], start=True, stop=True)
                    mm(b[:, P:3 * P], k1[:, 3], q1[:, 1:3].rearrange("p s n -> p (s n)"), start=True, stop=True).then_inc(full(("far", h, 0)), 1)
                    b = open_bank(("far", h, 1))
                    mm(b[:, 0:2 * P], k1[:, 1], q1[:, 1:3].rearrange("p s n -> p (s n)"), start=True, stop=True)
                    mm(b[:, 2 * P:3 * P], k1[:, 2], q1[:, 3], start=True, stop=True).then_inc(full(("far", h, 1)), 1)
                if h >= 1:
                    g = h - 1
                    b = open_bank(("ho", g))
                    evacuated(pe, ("diag", g, LEVELS))
                    evacuated(pe, ("far", g, 0))
                    evacuated(pe, ("far", g, 1))
                    for t in range(NT):
                        for m in range(t + 1):
                            ins = mm(b[:, t * P:(t + 1) * P], attn[:, g % 2, m, t * P:(t + 1) * P], v_tok[:, m, g * P:(g + 1) * P],
                                     start=(m == 0), stop=(m == t))
                    ins.then_inc(full(("ho", g)), 1)
            out_gemm("mix2", v_tok, lambda: pe.wait_ge(s["ho_ready"], NT))
            norm(3)
            ffn(1)
            norm(4)
            feat_gemm("kvc", hkv_t, [("kvc", j) for j in range(4)])
            tok_gemm("kvs", hkv_t, 2)
            tok_gemm("nq", h_t, 3, lambda u: 512 if u < 2 else 48)
            pe.wait_ge(s["u_done"], 12)
            for j in range(4):
                evacuated(pe, ("kvc", j))
            for kv in range(2):
                w = arrived(pe, ("cmp1", kv)).rearrange("p (r n) -> p r n", r=16)
                for n in range(2):
                    b = open_bank(("cmp1", kv, n))
                    for r in range(16):
                        ins = mm(b[:, 0:4 * NCMP], w[:, r, n * P:(n + 1) * P], win[:, kv, r].rearrange("p h i -> p (h i)"),
                                 start=(r == 0), stop=(r == 15))
                    ins.then_inc(full(("cmp1", kv, n)), 1)
            for kv in range(2):
                for j in range(2):
                    evacuated(pe, ("cmp1", kv, j))
            pe.wait_ge(s["w2_in"], 32)
            b = open_bank("cmp2")
            for kv in range(2):
                for kh in range(NSA_KV):
                    for n in range(2):
                        ins = mm(b[0:NCMP, kv * 256 + kh * HD:kv * 256 + (kh + 1) * HD], h1[:, kv, n, kh], w2_sb[:, kv, n, :],
                                 start=(n == 0), stop=(n == 1))
            ins.then_inc(full("cmp2"), 1)
            pe.wait_ge(s["cmp_tok"], 1)
            b = open_bank("cmpT")
            for c in range(2):
                ins = tr(b[:, 32 * c:32 * c + NCMP], kc_tok[:, 2 * c:2 * c + 2, :].rearrange("p h d -> p (h d)"), ident[0:NCMP, 0:NCMP])
            ins.then_inc(full("cmpT"), 1)
            for t in range(NT):
                for j in range(3):
                    i = 3 * t + j
                    if j < 2:
                        pe.wait_ge(s["gained"], i + 1)
                        b = open_bank(("nT", t, j))
                        for c in range(4):
                            ins = tr(b[:, c * P:(c + 1) * P], n_a[:, i % 2, c * P:(c + 1) * P], ident)
                        ins.then_inc(full(("nT", t, j)), 1)
                    pe.wait_ge(s["rope2_done"], i + 1)
                    key = ("nT", t, 2 + j)
                    b = open_bank(key)
                    for c in range(4):
                        ins = tr(b[:, c * P:(c + 1) * P], n_o[:, i % 2, c * P:(c + 1) * P], ident)
                    ins.then_inc(full(key), 1)
            for t in range(NT):
                for j in range(5):
                    evacuated(pe, ("nT", t, j))
            evacuated(pe, "cmpT")
            for i in range(len(GROUPS) + 2):
                if i < len(GROUPS):
                    t, kp = GROUPS[i]
                    b = open_bank(("cS", i))
                    for g in range(4):
                        ins = mm(b[:, g * P:(g + 1) * P], qn_t[:, kp * 4 + g, t * P:(t + 1) * P],
                                 kc_t[:, kp].rearrange("p q i -> p (q i)"), start=True, stop=True)
                    ins.then_inc(full(("cS", i)), 1)
                if 1 <= i <= len(GROUPS):
                    pe.wait_ge(s["cmp_p"], i)
                    pe.wait_ge(s["keys_zero"], 1)
                    b = open_bank(("cT", i - 1))
                    for q in range(2):
                        ins = tr(b[:, q * P:(q + 1) * P], cp[:, (i - 1) % 2, 4 * q:4 * q + 4, :].rearrange("p g c -> p (g c)"), ident)
                    ins.then_inc(full(("cT", i - 1)), 1)
                if i >= 2:
                    t, kp = GROUPS[i - 2]
                    evacuated(pe, ("cT", i - 2))
                    b = open_bank(("cO", i - 2))
                    for q in range(2):
                        ins = mm(b[:, q * 256:(q + 1) * 256], cpt[:, i % 2, q, :], vc_diag[:, 2 * kp + q].rearrange("p g d -> p (g d)"),
                                 start=True, stop=True)
                    ins.then_inc(full(("cO", i - 2)), 1)
            pe.wait_ge(s["keys_zero"], 3)
            attention("nsa", None)
            for mj in ADA_LATE:
                ada_row(*mj)
            out_gemm("mix3", nsa_tok, lambda: pe.wait_ge(s["nsa_added"], len(NSA_GROUPS)))
            norm(5)
            ffn(2)


_INS = """x mix_norm_pre mix_norm_post w_in w_out ffn_norm_pre ffn_norm_post w_up conv_w conv_b w_down c_2 ada_w_2 ada_b_2
norm_mix_2 norm_ffn_2 hgrn_w_in_2 hgrn_out_norm_2 hgrn_w_out_2 kv_ada_w_2 kv_ada_b_2 kv_norm_2 nsa_w_kv_2
nsa_k_norm_2 cmp_pos_2 cmp_w1_2 cmp_w2_2 nsa_w_q_2 nsa_q_norm_2 nsa_w_out_2 ffn_w_in_2 ffn_w_out_2""".split()


def kernel(**inputs):
    import concourse.bacc as _bacc
    from concourse.bass_utils import run_bass_kernel_spmd as _run

    nc = _bacc.Bacc("TRN2", target_bir_lowering=False, num_devices=1)
    arrays, io = {}, {}
    given = {n: np.ascontiguousarray(inputs[n]) for n in _INS}
    given.update(shape_constants())
    for name, a in given.items():
        arrays[f"in_{name}"] = a
        io[name] = nc.dram_tensor(f"in_{name}", a.shape, mybir.dt.from_np(a.dtype), kind="ExternalInput").ap()
    out = nc.dram_tensor("out_0", (1, S, D), F32, kind="ExternalOutput").ap()
    build(nc, io, out)
    r = _run(nc, [arrays], core_ids=[0])
    return r.results[0]["out_0"]
```
